# Optimizing a Trainium2 kernel written in Bass

```python
import jax, jax.numpy as jnp
from jax import lax
import numpy as np

D_MODEL = 1024
BATCH = 1
SEQ = 256
DEPTH = 2

N_EVEN = (DEPTH + 1) // 2
N_ODD = DEPTH // 2
EPS = 1e-6
LRU_WIDTH = D_MODEL // 2
LRU_BLOCKS = 8
LRU_BLOCK = LRU_WIDTH // LRU_BLOCKS
CONV_W = 4
LRU_C = 8.0
FOX_HEADS = 8
FOX_HEAD_DIM = (D_MODEL // 2) // FOX_HEADS
FOX_WIDTH = FOX_HEADS * FOX_HEAD_DIM
Q_BLOCK = 128
EVEN_SPLITS = [LRU_WIDTH, 2 * LRU_WIDTH, 2 * LRU_WIDTH + FOX_WIDTH, 2 * LRU_WIDTH + 2 * FOX_WIDTH, 2 * LRU_WIDTH + 3 * FOX_WIDTH]
EVEN_IN = 2 * LRU_WIDTH + 3 * FOX_WIDTH + FOX_HEADS
GLA_HEADS = 4
GLA_DK = (D_MODEL // 2) // GLA_HEADS
GLA_DV = D_MODEL // GLA_HEADS
GLA_RANK = 16
GLA_TAU = 16.0
GLA_CHUNK = 64
GLA_KW = GLA_HEADS * GLA_DK
GLA_VW = GLA_HEADS * GLA_DV
ODD_SPLITS = [GLA_KW, 2 * GLA_KW, 2 * GLA_KW + GLA_VW, 2 * GLA_KW + 2 * GLA_VW]
ODD_IN = 2 * GLA_KW + 2 * GLA_VW + GLA_RANK
D_FF = 2816
N_EXPERTS = 8
TOP_K = 2
D_FF_EXPERT = 3584


def rms_norm(x, g):
    xf = x.astype(jnp.float32)
    y = xf * lax.rsqrt(jnp.mean(xf * xf, axis=-1, keepdims=True) + EPS)
    return (y * g.astype(jnp.float32)).astype(x.dtype)

def causal_depthwise_conv(x, w, b):
    s = x.shape[1]
    xp = jnp.pad(x, ((0, 0), (CONV_W - 1, 0), (0, 0)))
    out = b
    for j in range(CONV_W):
        out = out + xp[:, j:j + s] * w[j]
    return out

def block_diag_linear(x, w, b):
    xb = x.reshape(x.shape[0], x.shape[1], LRU_BLOCKS, LRU_BLOCK)
    return jnp.einsum('bsni,nij->bsnj', xb, w).reshape(x.shape) + b

def rglru(x, ga_w, ga_b, gx_w, gx_b, lam):
    xf = x.astype(jnp.float32)
    r = jax.nn.sigmoid(block_diag_linear(xf, ga_w.astype(jnp.float32), ga_b.astype(jnp.float32)))
    i = jax.nn.sigmoid(block_diag_linear(xf, gx_w.astype(jnp.float32), gx_b.astype(jnp.float32)))
    log_a = -LRU_C * r * jax.nn.softplus(-lam.astype(jnp.float32))
    a = jnp.exp(log_a)
    u = jnp.sqrt(-jnp.expm1(2.0 * log_a)) * (i * xf)

    def combine(c1, c2):
        a1, b1 = c1
        a2, b2 = c2
        return a1 * a2, a2 * b1 + b2

    _, h = lax.associative_scan(combine, (a, u), axis=1)
    return h

def fox_attention(q, k, v, log_f):
    bsz, s, h, dh = q.shape
    nb = s // Q_BLOCK
    c = jnp.cumsum(log_f, axis=1).transpose(0, 2, 1)
    qh = q.transpose(0, 2, 1, 3) * (dh ** -0.5)
    kh = k.transpose(0, 2, 1, 3)
    vh = v.transpose(0, 2, 1, 3)
    qb = qh.reshape(bsz, h, nb, Q_BLOCK, dh).transpose(2, 0, 1, 3, 4)
    cb = c.reshape(bsz, h, nb, Q_BLOCK).transpose(2, 0, 1, 3)
    pos_b = jnp.arange(s).reshape(nb, Q_BLOCK)
    k_pos = jnp.arange(s)

    def one_block(args):
        q_blk, c_blk, p_blk = args
        logits = jnp.einsum('bhqd,bhkd->bhqk', q_blk, kh).astype(jnp.float32)
        logits = logits + c_blk[..., None] - c[:, :, None, :]
        mask = p_blk[:, None] >= k_pos[None, :]
        logits = jnp.where(mask, logits, -jnp.inf)
        p = jax.nn.softmax(logits, axis=-1)
        return jnp.einsum('bhqk,bhkd->bhqd', p.astype(vh.dtype), vh)

    ob = lax.map(one_block, (qb, cb, pos_b))
    return ob.transpose(1, 0, 3, 2, 4).reshape(bsz, s, h * dh)

def gla_chunked(q, k, v, log_a):
    bsz, s, h, dk = q.shape
    dv = v.shape[-1]
    n = s // GLA_CHUNK

    def chunks(t):
        return t.reshape(bsz, n, GLA_CHUNK, h, t.shape[-1]).transpose(1, 0, 3, 2, 4)

    qc, kc, vc, gc = chunks(q), chunks(k), chunks(v), chunks(log_a)
    b = jnp.cumsum(gc, axis=3)
    b_last = b[:, :, :, -1:, :]
    q_dec = qc * jnp.exp(b)
    k_intra = kc * jnp.exp(-b)
    k_state = kc * jnp.exp(b_last - b)
    chunk_decay = jnp.exp(b_last[:, :, :, 0, :])
    causal = jnp.tril(jnp.ones((GLA_CHUNK, GLA_CHUNK), dtype=bool))
    scores = jnp.where(causal, jnp.einsum('nbhid,nbhjd->nbhij', q_dec, k_intra), 0.0)
    o_intra = jnp.einsum('nbhij,nbhje->nbhie', scores, vc)

    def step(state, xs):
        q_n, k_n, v_n, d_n = xs
        o_n = jnp.einsum('bhid,bhde->bhie', q_n, state)
        state = d_n[..., None] * state + jnp.einsum('bhjd,bhje->bhde', k_n, v_n)
        return state, o_n

    state0 = jnp.zeros((bsz, h, dk, dv), jnp.float32)
    _, o_inter = lax.scan(step, state0, (q_dec, k_state, vc, chunk_decay))
    o = o_intra + o_inter
    return o.transpose(1, 0, 3, 2, 4).reshape(bsz, s, h, dv)

def even_mixer(hn, w_in, conv_w, conv_b, ga_w, ga_b, gx_w, gx_b, lam, f_b, w_out):
    bsz, s, _ = hn.shape
    proj = hn @ w_in
    xr, yr, q, k, v, f_logit = jnp.split(proj, EVEN_SPLITS, axis=-1)
    xc = causal_depthwise_conv(xr, conv_w, conv_b)
    h_lru = rglru(xc, ga_w, ga_b, gx_w, gx_b, lam)
    y_a = (h_lru * jax.nn.gelu(yr.astype(jnp.float32))).astype(hn.dtype)
    log_f = jax.nn.log_sigmoid((f_logit + f_b).astype(jnp.float32))
    shp = (bsz, s, FOX_HEADS, FOX_HEAD_DIM)
    y_b = fox_attention(q.reshape(shp), k.reshape(shp), v.reshape(shp), log_f).astype(hn.dtype)
    return jnp.concatenate([y_a, y_b], axis=-1) @ w_out

def odd_mixer(hn, w_in, gate_w2, gate_b, head_norm, w_out):
    bsz, s, _ = hn.shape
    proj = hn @ w_in
    q, k, v, g, lr = jnp.split(proj, ODD_SPLITS, axis=-1)
    log_a = jax.nn.log_sigmoid((lr @ gate_w2 + gate_b).astype(jnp.float32)) / GLA_TAU
    kshp = (bsz, s, GLA_HEADS, GLA_DK)
    o = gla_chunked((q.astype(jnp.float32) * (GLA_DK ** -0.5)).reshape(kshp),
                    k.astype(jnp.float32).reshape(kshp),
                    v.astype(jnp.float32).reshape(bsz, s, GLA_HEADS, GLA_DV),
                    log_a.reshape(kshp))
    o = o * lax.rsqrt(jnp.mean(o * o, axis=-1, keepdims=True) + EPS)
    o = o * head_norm.astype(jnp.float32).reshape(GLA_HEADS, GLA_DV)
    o = o.reshape(bsz, s, GLA_VW) * jax.nn.silu(g.astype(jnp.float32))
    return o.astype(hn.dtype) @ w_out

def swiglu(hn, w1, w3, w2):
    return (jax.nn.silu(hn @ w1) * (hn @ w3)) @ w2

def moe_swiglu(hn, router, w1, w3, w2):
    bsz, s, d = hn.shape
    t = hn.reshape(-1, d)
    logits = (t @ router).astype(jnp.float32)
    top_vals, top_idx = lax.top_k(logits, TOP_K)
    top_w = jax.nn.softmax(top_vals, axis=-1)
    gates = jnp.sum(top_w[..., None] * jax.nn.one_hot(top_idx, N_EXPERTS, dtype=jnp.float32), axis=1)
    out = jnp.zeros_like(t)
    for e in range(N_EXPERTS):
        h_e = jax.nn.silu(t @ w1[e]) * (t @ w3[e])
        out = out + gates[:, e:e + 1].astype(t.dtype) * (h_e @ w2[e])
    return out.reshape(bsz, s, d)

def first_inputs(seed: int = 0) -> dict:
    key = jax.random.key(seed)
    ks = iter(jax.random.split(key, 32))
    f32 = jnp.float32
    out_scale = (2.0 * DEPTH) ** -0.5

    def dense(shape, fan_in, scale=1.0):
        return jax.random.normal(next(ks), shape, f32) * (scale * fan_in ** -0.5)

    def gain(shape):
        return 1.0 + 0.02 * jax.random.normal(next(ks), shape, f32)

    def small(shape):
        return 0.02 * jax.random.normal(next(ks), shape, f32)

    x = jax.random.normal(next(ks), (BATCH, SEQ, D_MODEL), f32)
    norm_mix = gain((DEPTH, D_MODEL))
    norm_ffn = gain((DEPTH, D_MODEL))
    norm_final = gain((D_MODEL,))
    ev_w_in = dense((N_EVEN, D_MODEL, EVEN_IN), D_MODEL)
    ev_conv_w = dense((N_EVEN, CONV_W, LRU_WIDTH), CONV_W)
    ev_conv_b = small((N_EVEN, LRU_WIDTH))
    ev_ga_w = dense((N_EVEN, LRU_BLOCKS, LRU_BLOCK, LRU_BLOCK), LRU_BLOCK)
    ev_ga_b = small((N_EVEN, LRU_WIDTH))
    ev_gx_w = dense((N_EVEN, LRU_BLOCKS, LRU_BLOCK, LRU_BLOCK), LRU_BLOCK)
    ev_gx_b = small((N_EVEN, LRU_WIDTH))
    u = jax.random.uniform(next(ks), (N_EVEN, LRU_WIDTH), f32, minval=0.9, maxval=0.999)
    p = u ** (1.0 / LRU_C)
    ev_lambda = jnp.log(p) - jnp.log1p(-p)
    ev_f_b = 2.0 + 0.1 * jax.random.normal(next(ks), (N_EVEN, FOX_HEADS), f32)
    ev_w_out = dense((N_EVEN, D_MODEL, D_MODEL), D_MODEL, out_scale)
    ev_ffn_w1 = dense((N_EVEN, D_MODEL, D_FF), D_MODEL)
    ev_ffn_w3 = dense((N_EVEN, D_MODEL, D_FF), D_MODEL)
    ev_ffn_w2 = dense((N_EVEN, D_FF, D_MODEL), D_FF, out_scale)
    od_w_in = dense((N_ODD, D_MODEL, ODD_IN), D_MODEL)
    od_gate_w2 = dense((N_ODD, GLA_RANK, GLA_KW), GLA_RANK)
    od_gate_b = small((N_ODD, GLA_KW))
    od_head_norm = gain((N_ODD, GLA_VW))
    od_w_out = dense((N_ODD, GLA_VW, D_MODEL), GLA_VW, out_scale)
    od_router = dense((N_ODD, D_MODEL, N_EXPERTS), D_MODEL)
    od_exp_w1 = dense((N_ODD, N_EXPERTS, D_MODEL, D_FF_EXPERT), D_MODEL)
    od_exp_w3 = dense((N_ODD, N_EXPERTS, D_MODEL, D_FF_EXPERT), D_MODEL)
    od_exp_w2 = dense((N_ODD, N_EXPERTS, D_FF_EXPERT, D_MODEL), D_FF_EXPERT, out_scale)
    return {"x": x, "norm_mix": norm_mix, "norm_ffn": norm_ffn, "norm_final": norm_final,
            "ev_w_in": ev_w_in, "ev_conv_w": ev_conv_w, "ev_conv_b": ev_conv_b,
            "ev_ga_w": ev_ga_w, "ev_ga_b": ev_ga_b, "ev_gx_w": ev_gx_w, "ev_gx_b": ev_gx_b,
            "ev_lambda": ev_lambda, "ev_f_b": ev_f_b, "ev_w_out": ev_w_out,
            "ev_ffn_w1": ev_ffn_w1, "ev_ffn_w3": ev_ffn_w3, "ev_ffn_w2": ev_ffn_w2,
            "od_w_in": od_w_in, "od_gate_w2": od_gate_w2, "od_gate_b": od_gate_b,
            "od_head_norm": od_head_norm, "od_w_out": od_w_out, "od_router": od_router,
            "od_exp_w1": od_exp_w1, "od_exp_w3": od_exp_w3, "od_exp_w2": od_exp_w2}

def first_block(x, norm_mix, norm_ffn, norm_final,
              ev_w_in, ev_conv_w, ev_conv_b, ev_ga_w, ev_ga_b, ev_gx_w, ev_gx_b,
              ev_lambda, ev_f_b, ev_w_out, ev_ffn_w1, ev_ffn_w3, ev_ffn_w2,
              od_w_in, od_gate_w2, od_gate_b, od_head_norm, od_w_out, od_router,
              od_exp_w1, od_exp_w3, od_exp_w2):
    h = x
    for layer in range(DEPTH):
        j = layer // 2
        hn = rms_norm(h, norm_mix[layer])
        if layer % 2 == 0:
            h = h + even_mixer(hn, ev_w_in[j], ev_conv_w[j], ev_conv_b[j], ev_ga_w[j], ev_ga_b[j],
                               ev_gx_w[j], ev_gx_b[j], ev_lambda[j], ev_f_b[j], ev_w_out[j])
            h = h + swiglu(rms_norm(h, norm_ffn[layer]), ev_ffn_w1[j], ev_ffn_w3[j], ev_ffn_w2[j])
        else:
            h = h + odd_mixer(hn, od_w_in[j], od_gate_w2[j], od_gate_b[j], od_head_norm[j], od_w_out[j])
            h = h + moe_swiglu(rms_norm(h, norm_ffn[layer]), od_router[j], od_exp_w1[j],
                               od_exp_w3[j], od_exp_w2[j])
    return rms_norm(h, norm_final)


N_MIXERS = 4
GROUP_W = D_MODEL // N_MIXERS
HEAD_DIM = 64
N_HEADS = GROUP_W // HEAD_DIM
FFN_RESID = 0.5
SC_WIDTH = 3
CHUNK = 128
CM_WIDTH = 31
RANK_W = 32
RANK_A = 32
RANK_G = 64
A_COLS = 3 * GROUP_W
B_COLS = 2 * GROUP_W
C_COLS = 3 * GROUP_W + RANK_W + RANK_A + RANK_G
D_COLS = 2 * GROUP_W
IN_COLS = A_COLS + B_COLS + C_COLS + D_COLS
RMS_EPS = 1e-6
LN_EPS = 1e-5
GN_EPS = 1e-5 * HEAD_DIM


def rms_norm_2(x, g):
    xf = x.astype(jnp.float32)
    y = xf * lax.rsqrt(jnp.mean(xf * xf, axis=-1, keepdims=True) + RMS_EPS)
    return (y * g.astype(jnp.float32)).astype(x.dtype)

def layer_norm(x, g, b, eps=LN_EPS):
    xf = x.astype(jnp.float32)
    mu = jnp.mean(xf, axis=-1, keepdims=True)
    var = jnp.mean(jnp.square(xf - mu), axis=-1, keepdims=True)
    y = (xf - mu) * lax.rsqrt(var + eps) * g.astype(jnp.float32) + b.astype(jnp.float32)
    return y.astype(x.dtype)

def swiglu_2(h, w_gate, w_up, w_down):
    return (jax.nn.silu(h @ w_gate) * (h @ w_up)) @ w_down

def token_shift(t):
    return jnp.pad(t, ((0, 0), (1, 0), (0, 0)))[:, :-1, :]

def causal_depthwise_conv_2(x, w):
    K, C = w.shape
    return lax.conv_general_dilated(
        x, w[:, None, :].astype(x.dtype), window_strides=(1,), padding=[(K - 1, 0)],
        dimension_numbers=("NWC", "WIO", "NWC"), feature_group_count=C)

def spatial_gating(u, v, w_s, b_s, ln_w, ln_b):
    Bsz, S, G = v.shape
    v = layer_norm(v, ln_w, ln_b)
    v = v.reshape(Bsz, S // CHUNK, CHUNK, N_HEADS, G // N_HEADS)
    w = w_s * jnp.tril(jnp.ones((CHUNK, CHUNK), w_s.dtype))
    s = jnp.einsum("hts,bnshd->bnthd", w, v) + b_s.T[None, None, :, :, None]
    return u * s.reshape(Bsz, S, G)

def rwkv7_recurrence(r, w, k, v, a, b):
    Bsz, S, H, N = r.shape
    seq = tuple(jnp.swapaxes(t.astype(jnp.float32), 0, 1) for t in (r, w, k, v, a, b))

    def step(state, inp):
        r_t, w_t, k_t, v_t, a_t, b_t = inp
        sa = jnp.einsum("bhij,bhj->bhi", state, a_t)
        state = (state * w_t[:, :, None, :] + sa[..., None] * b_t[:, :, None, :]
                 + v_t[..., None] * k_t[:, :, None, :])
        y = jnp.einsum("bhij,bhj->bhi", state, r_t)
        return state, y

    s0 = jnp.zeros((Bsz, H, N, N), jnp.float32)
    _, ys = lax.scan(step, s0, seq)
    return jnp.swapaxes(ys, 0, 1)

def rwkv7_time_mix(pc, mu, w0, w_up, a0, a_up, g_up, k_k, k_a, r_k, ln_w, ln_b):
    Bsz, S, _ = pc.shape
    pc = pc + (token_shift(pc) - pc) * mu
    G = GROUP_W
    r, k, v, wd, ad, gd = jnp.split(
        pc, [G, 2 * G, 3 * G, 3 * G + RANK_W, 3 * G + RANK_W + RANK_A], axis=-1)
    w_log = -jax.nn.softplus(-(w0 + jnp.tanh(wd) @ w_up)) - 0.5
    decay = jnp.exp(-jnp.exp(w_log.astype(jnp.float32)))
    a = jax.nn.sigmoid(a0 + ad @ a_up)
    g = jax.nn.sigmoid(gd) @ g_up
    heads = lambda t: t.reshape(Bsz, S, N_HEADS, HEAD_DIM)
    kk = heads(k * k_k).astype(jnp.float32)
    kk = kk / jnp.maximum(jnp.sqrt(jnp.sum(kk * kk, axis=-1, keepdims=True)), 1e-12)
    k = k * (1.0 + (a - 1.0) * k_a)
    rh, kh, vh, ah = heads(r), heads(k), heads(v), heads(a)
    o = rwkv7_recurrence(rh, heads(decay), kh, vh, -kk, kk * ah).astype(pc.dtype)
    o = layer_norm(o, ln_w.reshape(N_HEADS, HEAD_DIM), ln_b.reshape(N_HEADS, HEAD_DIM), eps=GN_EPS)
    o = o + jnp.sum(rh * kh * r_k, axis=-1, keepdims=True) * vh
    return o.reshape(Bsz, S, G) * g

def hybrid_mix(h, w_in, sc_conv_w, sg_ln_w, sg_ln_b, sg_w, sg_b,
               rk_mu, rk_w0, rk_w_up, rk_a0, rk_a_up, rk_g_up, rk_k_k, rk_k_a, rk_r_k,
               rk_ln_w, rk_ln_b, cm_conv_w, cm_conv_b, cm_ln_w, cm_ln_b, w_out):
    p = h @ w_in
    pa, pb, pc, pd = jnp.split(p, [A_COLS, A_COLS + B_COLS, A_COLS + B_COLS + C_COLS], axis=-1)
    gate_b, gate_c, xa = jnp.split(pa, 3, axis=-1)
    y_a = gate_b * causal_depthwise_conv_2(gate_c * xa, sc_conv_w)
    u, v = jnp.split(pb, 2, axis=-1)
    y_b = spatial_gating(u, v, sg_w, sg_b, sg_ln_w, sg_ln_b)
    y_c = rwkv7_time_mix(pc, rk_mu, rk_w0, rk_w_up, rk_a0, rk_a_up, rk_g_up,
                         rk_k_k, rk_k_a, rk_r_k, rk_ln_w, rk_ln_b)
    z1, z2 = jnp.split(pd, 2, axis=-1)
    zd = causal_depthwise_conv_2(z1 * jax.nn.sigmoid(z2), cm_conv_w) + cm_conv_b
    y_d = jax.nn.silu(layer_norm(zd, cm_ln_w, cm_ln_b))
    return jnp.concatenate([y_a, y_b, y_c, y_d], axis=-1) @ w_out

def second_inputs(seed: int = 0) -> dict:
    key = jax.random.key(seed)
    ks = iter(jax.random.split(key, 48))
    nrm = lambda shape, scale: jax.random.normal(next(ks), shape, jnp.float32) * scale
    gain = lambda shape: 1.0 + 0.02 * jax.random.normal(next(ks), shape, jnp.float32)
    L, D, F, G = DEPTH, D_MODEL, D_FF, GROUP_W
    return {
        "x": nrm((BATCH, SEQ, D), 1.0),
        "ffn1_pre_g": gain((L, D)),
        "ffn1_w_gate": nrm((L, D, F), D ** -0.5),
        "ffn1_w_up": nrm((L, D, F), D ** -0.5),
        "ffn1_w_down": nrm((L, F, D), F ** -0.5),
        "ffn1_post_g": gain((L, D)),
        "mix_pre_g": gain((L, D)),
        "w_in": nrm((L, D, IN_COLS), D ** -0.5),
        "sc_conv_w": nrm((L, SC_WIDTH, G), SC_WIDTH ** -0.5),
        "sg_ln_w": gain((L, G)),
        "sg_ln_b": nrm((L, G), 0.02),
        "sg_w": nrm((L, N_HEADS, CHUNK, CHUNK), 0.5 * CHUNK ** -0.5),
        "sg_b": gain((L, N_HEADS, CHUNK)) + nrm((L, N_HEADS, CHUNK), 0.1),
        "rk_mu": jax.random.uniform(next(ks), (L, C_COLS), jnp.float32, 0.0, 1.0),
        "rk_w0": jax.random.uniform(next(ks), (L, G), jnp.float32, -6.0, 1.0),
        "rk_w_up": nrm((L, RANK_W, G), 0.1 * RANK_W ** -0.5),
        "rk_a0": nrm((L, G), 0.1),
        "rk_a_up": nrm((L, RANK_A, G), 0.1 * RANK_A ** -0.5),
        "rk_g_up": nrm((L, RANK_G, G), RANK_G ** -0.5),
        "rk_k_k": 0.85 + nrm((L, G), 0.02),
        "rk_k_a": gain((L, G)),
        "rk_r_k": nrm((L, N_HEADS, HEAD_DIM), 0.1),
        "rk_ln_w": gain((L, G)),
        "rk_ln_b": nrm((L, G), 0.02),
        "cm_conv_w": nrm((L, CM_WIDTH, G), CM_WIDTH ** -0.5),
        "cm_conv_b": nrm((L, G), 0.02),
        "cm_ln_w": gain((L, G)),
        "cm_ln_b": nrm((L, G), 0.02),
        "w_out": nrm((L, D, D), D ** -0.5),
        "mix_post_g": gain((L, D)),
        "ffn2_pre_g": gain((L, D)),
        "ffn2_w_gate": nrm((L, D, F), D ** -0.5),
        "ffn2_w_up": nrm((L, D, F), D ** -0.5),
        "ffn2_w_down": nrm((L, F, D), F ** -0.5),
        "ffn2_post_g": gain((L, D)),
    }

def second_block(x, ffn1_pre_g, ffn1_w_gate, ffn1_w_up, ffn1_w_down, ffn1_post_g,
              mix_pre_g, w_in, sc_conv_w, sg_ln_w, sg_ln_b, sg_w, sg_b,
              rk_mu, rk_w0, rk_w_up, rk_a0, rk_a_up, rk_g_up, rk_k_k, rk_k_a, rk_r_k,
              rk_ln_w, rk_ln_b, cm_conv_w, cm_conv_b, cm_ln_w, cm_ln_b, w_out, mix_post_g,
              ffn2_pre_g, ffn2_w_gate, ffn2_w_up, ffn2_w_down, ffn2_post_g):
    for l in range(DEPTH):
        h = rms_norm_2(x, ffn1_pre_g[l])
        x = x + FFN_RESID * rms_norm_2(
            swiglu_2(h, ffn1_w_gate[l], ffn1_w_up[l], ffn1_w_down[l]), ffn1_post_g[l])
        h = rms_norm_2(x, mix_pre_g[l])
        m = hybrid_mix(h, w_in[l], sc_conv_w[l], sg_ln_w[l], sg_ln_b[l], sg_w[l], sg_b[l],
                       rk_mu[l], rk_w0[l], rk_w_up[l], rk_a0[l], rk_a_up[l], rk_g_up[l],
                       rk_k_k[l], rk_k_a[l], rk_r_k[l], rk_ln_w[l], rk_ln_b[l],
                       cm_conv_w[l], cm_conv_b[l], cm_ln_w[l], cm_ln_b[l], w_out[l])
        x = x + rms_norm_2(m, mix_post_g[l])
        h = rms_norm_2(x, ffn2_pre_g[l])
        x = x + FFN_RESID * rms_norm_2(
            swiglu_2(h, ffn2_w_gate[l], ffn2_w_up[l], ffn2_w_down[l]), ffn2_post_g[l])
    return x


_first_inputs = second_inputs


def second_inputs(seed=0):
    import zlib

    import numpy as np

    out = dict(_first_inputs(seed))
    spreads = {}
    factors = {'ffn1_post_g': 3.416,
     'sg_ln_w': 41.239,
     'sg_ln_b': 42.814,
     'rk_w_up': 8.0,
     'rk_a0': 3.909,
     'rk_a_up': 3.968,
     'rk_k_k': 37.458,
     'rk_k_a': 8.0,
     'rk_ln_w': 26.007,
     'rk_ln_b': 25.556,
     'cm_conv_b': 3.499,
     'cm_ln_w': 20.823,
     'cm_ln_b': 19.123,
     'mix_post_g': 2.747,
     'ffn2_pre_g': 4.258,
     'ffn2_post_g': 17.911,
     'sg_b': 2.739}
    for name, (base, spread) in spreads.items():
        noise = np.random.default_rng([zlib.crc32(name.encode()), seed]).standard_normal(out[name].shape)
        drawn = base * np.exp(spread * noise) if base else spread * noise
        out[name] = __import__('jax').numpy.asarray(drawn.astype(out[name].dtype))
    for name, factor in factors.items():
        out[name] = (out[name] * factor).astype(out[name].dtype)
    return out


_narrow_inputs = second_inputs


def second_inputs(seed=0):

    out = dict(_narrow_inputs(seed))
    wider = {'sg_ln_w': 3.85,
     'sg_ln_b': 3.89,
     'sg_b': 3.77,
     'rk_k_k': 5.81,
     'rk_ln_w': 3.75,
     'rk_ln_b': 3.92,
     'cm_ln_w': 3.86,
     'cm_ln_b': 3.89}
    for name, times in wider.items():
        mean = out[name].mean()
        out[name] = (mean + times * (out[name] - mean)).astype(out[name].dtype)
    return out


def setup_inputs(seed=0):
    out = dict(first_inputs(seed))
    for name, value in second_inputs(seed + 1).items():
        if name != "x":
            out[name + "_2"] = value
    return out


def reference(
    x, norm_mix, norm_ffn, norm_final, ev_w_in, ev_conv_w, ev_conv_b, ev_ga_w, ev_ga_b, ev_gx_w,
    ev_gx_b, ev_lambda, ev_f_b, ev_w_out, ev_ffn_w1, ev_ffn_w3, ev_ffn_w2, od_w_in, od_gate_w2,
    od_gate_b, od_head_norm, od_w_out, od_router, od_exp_w1, od_exp_w3, od_exp_w2, ffn1_pre_g_2,
    ffn1_w_gate_2, ffn1_w_up_2, ffn1_w_down_2, ffn1_post_g_2, mix_pre_g_2, w_in_2, sc_conv_w_2,
    sg_ln_w_2, sg_ln_b_2, sg_w_2, sg_b_2, rk_mu_2, rk_w0_2, rk_w_up_2, rk_a0_2, rk_a_up_2,
    rk_g_up_2, rk_k_k_2, rk_k_a_2, rk_r_k_2, rk_ln_w_2, rk_ln_b_2, cm_conv_w_2, cm_conv_b_2,
    cm_ln_w_2, cm_ln_b_2, w_out_2, mix_post_g_2, ffn2_pre_g_2, ffn2_w_gate_2, ffn2_w_up_2,
    ffn2_w_down_2, ffn2_post_g_2,
):
    x = first_block(
        x, norm_mix, norm_ffn, norm_final, ev_w_in, ev_conv_w, ev_conv_b, ev_ga_w, ev_ga_b,
        ev_gx_w, ev_gx_b, ev_lambda, ev_f_b, ev_w_out, ev_ffn_w1, ev_ffn_w3, ev_ffn_w2, od_w_in,
        od_gate_w2, od_gate_b, od_head_norm, od_w_out, od_router, od_exp_w1, od_exp_w3,
        od_exp_w2,
    )
    return second_block(
        x, ffn1_pre_g_2, ffn1_w_gate_2, ffn1_w_up_2, ffn1_w_down_2, ffn1_post_g_2, mix_pre_g_2,
        w_in_2, sc_conv_w_2, sg_ln_w_2, sg_ln_b_2, sg_w_2, sg_b_2, rk_mu_2, rk_w0_2, rk_w_up_2,
        rk_a0_2, rk_a_up_2, rk_g_up_2, rk_k_k_2, rk_k_a_2, rk_r_k_2, rk_ln_w_2, rk_ln_b_2,
        cm_conv_w_2, cm_conv_b_2, cm_ln_w_2, cm_ln_b_2, w_out_2, mix_post_g_2, ffn2_pre_g_2,
        ffn2_w_gate_2, ffn2_w_up_2, ffn2_w_down_2, ffn2_post_g_2,
    )


_drawn_inputs = setup_inputs


def setup_inputs(seed=0):
    import zlib

    import numpy as np

    out = dict(_drawn_inputs(seed))
    spreads = {}
    factors = {'ev_ga_b': 8.0,
     'ev_gx_b': 8.0,
     'ev_f_b': 84.68,
     'od_gate_b': 8.159,
     'rk_k_a_2': 32.498,
     'od_head_norm': 2.757}
    for name, (base, spread) in spreads.items():
        noise = np.random.default_rng([zlib.crc32(name.encode()), seed]).standard_normal(out[name].shape)
        drawn = base * np.exp(spread * noise) if base else spread * noise
        out[name] = __import__('jax').numpy.asarray(drawn.astype(out[name].dtype))
    for name, factor in factors.items():
        out[name] = (out[name] * factor).astype(out[name].dtype)
    return out
```

```python
from contextlib import ExitStack

import concourse.bass as bass
from concourse import mybir

F32 = mybir.dt.float32
F32R = mybir.dt.float32r
ALU = mybir.AluOpType
ACT = mybir.ActivationFunctionType
AX = mybir.AxisListType

P = 128
S = 256
TT = S // P
D = 1024
KT = D // P
F_DENSE = 2816 // P
F_EXPERT = 3584 // P
NE = 8
RING = 6
LEAD = 3
EPS = 1e-6
LN_EPS = 1e-5
GN_EPS = 1e-5 * 64
DECAY_C = 0.6065306597126334
NEG = -1e30
ARENA_W = 19816

EV_COLS = [P] * 20 + [8]
OD_COLS = [P] * 24 + [16]
HY_COLS = [P] * 21


def build(nc, A, out):
    ctx = ExitStack()
    with ctx:
        ctx.enter_context(nc.allow_non_contiguous_dma(reason="small parameter rows"))

        def sb(name, shape, dt=F32):
            return ctx.enter_context(nc.sbuf_tensor(name, shape, dt))

        def sem(name):
            return ctx.enter_context(nc.semaphore(name))

        plan = []
        at = {"c": 0, "q": 0, "t": 0}

        def phase(kind, **kw):
            ph = dict(kind=kind, c0=at["c"], q0=at["q"], t0=at["t"], **kw)
            if kind == "proj":
                at["c"] += len(kw["cols"])
                at["q"] += len(kw["cols"])
            elif kind == "out":
                at["c"] += KT
            else:
                at["c"] += 3 * kw["tiles"]
                at["q"] += kw["tiles"]
                at["t"] += kw["tiles"]
            plan.append(ph)
            return ph

        EV_PROJ = phase("proj", w=A["ev_w_in"][0], cols=EV_COLS)
        EV_OUT = phase("out", w=A["ev_w_out"][0])
        EV_FFN = phase("ffn", tiles=F_DENSE, experts=1, w1=A["ev_ffn_w1"], w3=A["ev_ffn_w3"], w2=A["ev_ffn_w2"])
        OD_PROJ = phase("proj", w=A["od_w_in"][0], cols=OD_COLS)
        OD_OUT = phase("out", w=A["od_w_out"][0])
        MOE = phase("ffn", tiles=NE * F_EXPERT, experts=NE, w1=A["od_exp_w1"][0], w3=A["od_exp_w3"][0],
                    w2=A["od_exp_w2"][0])
        HY = []
        for l in range(2):
            f1 = phase("ffn", tiles=F_DENSE, experts=1, w1=A["ffn1_w_gate_2"][l:l + 1],
                       w3=A["ffn1_w_up_2"][l:l + 1], w2=A["ffn1_w_down_2"][l:l + 1])
            pr = phase("proj", w=A["w_in_2"][l], cols=HY_COLS)
            ou = phase("out", w=A["w_out_2"][l])
            f2 = phase("ffn", tiles=F_DENSE, experts=1, w1=A["ffn2_w_gate_2"][l:l + 1],
                       w3=A["ffn2_w_up_2"][l:l + 1], w2=A["ffn2_w_down_2"][l:l + 1])
            HY.append((f1, pr, ou, f2))
        N_CHUNKS = at["c"]
        width = {}
        for ph in plan:
            if ph["kind"] == "proj":
                for i, n in enumerate(ph["cols"]):
                    width[ph["c0"] + i] = KT * n

        RAW = sb("raw_ring", [P, RING, 1024])
        WHI = sb("whi_ring", [P, RING, 1024], F32R)
        WLO = sb("wlo_ring", [P, RING, 1024], F32R)
        XHI = sb("xhi", [P, KT, S], F32R)
        XLO = sb("xlo", [P, KT, S], F32R)
        H = sb("h", [P, TT, D])
        HID = sb("hid", [P, 2, S])
        HIDHI = sb("hidhi", [P, 2, S], F32R)
        HIDLO = sb("hidlo", [P, 2, S], F32R)
        SIL = sb("sil", [P, 2, S])
        IDENT = sb("ident", [P, P])
        ONES = sb("ones", [P, P])
        UPPER = sb("upper", [P, P])
        UPPER64 = sb("upper64", [P, P])
        STRICT64 = sb("strict64", [P, P])
        LEVEL = sb("level", [P, 6, P])
        BLOCK64 = sb("block64", [P, P])
        CAUSAL = sb("causal", [P, S])
        SEL = sb("sel", [8, 8, P])
        RESET = sb("reset", [P, 4 * S])
        IOTA8 = sb("iota8", [P, NE])
        ROWS = sb("rows", [P, 3, P])
        COLS = sb("cols", [P, 3, P])
        GBC = sb("gbc", [P, 2, D])
        STAT = sb("stat", [P, 84])
        ARENA = sb("arena", [P, ARENA_W])
        HN = ARENA[:, ARENA_W - 2 * D:].rearrange("p (t d) -> p t d", t=TT)

        class Carve:
            def __init__(self):
                self.at = 0

            def __call__(self, *dims, dt=F32, parts=P):
                n = 1
                for d_ in dims:
                    n *= d_
                ap = ARENA[0:parts, self.at:self.at + n]
                self.at += n
                assert self.at <= ARENA_W - 2 * D, self.at
                if len(dims) == 2:
                    ap = ap.rearrange("p (a b) -> p a b", a=dims[0])
                elif len(dims) == 3:
                    ap = ap.rearrange("p (a b c) -> p a b c", a=dims[0], b=dims[1])
                return ap

        BANK = [ctx.enter_context(nc.psum_tensor(f"bank{i}", [P, 512], F32)) for i in range(8)]
        YB = [[BANK[4 + 2 * t + h] for h in range(2)] for t in range(TT)]

        names = """hi_ready lo_ready chunk_used bank_free silu_ready hid_made hid_gated hidhi_made
        hid_ready h_ready ssq_ready hn_ready tp_ready xhi_ready x_ready consts_ready cols_tp cols_ready
        loads_done gbc_used dve_order act_order pool_order x_loaded router_ready gates_ready rows_zero
        conv_ready gates_mm sig_ready aexp_ready gelu_ready root_in root_ready spx_ready spe_ready lrk_act small_ready cum_ready cumev_ready
        score_ready logit_ready prob_ready probn_ready probt_ready probt_copied pv_ready
        lr_tp lrt_ready gate_mm nab_ready gexp_ready gexp1_ready gln_ready bcum_ready bexp_ready kdec_ready kstp_ready
        ksr_ready sct_mm sct_ready upd_ready state_ready o_ready o_ssq og_ready silug_ready
        up_in_ready lrk_ready up_mm upsig_ready pexp_in pexp_ready kk_in nrm_mm abkr_ready rows_tp rows_ready
        pair_mm pair_ready lvl_in t1_mm t1_ready xx_mm xx_ready rhs_mm rhs_ready sa_mm sa_ready sn_mm sn_ready
        yc_mm mean_in mean_mm var_in var_mm bonus_in bonus_mm wt_tp wt_ready vn_ready sp_mm z_sig zln_in zln_mm
        zc_in zv_mm zn_ready zs_ready mixer_done fin_ready out_done""".split()
        s = {n: sem(n) for n in names}
        raw_full = [sem(f"raw_full{i}") for i in range(RING)]
        gbc_full = [sem(f"gbc_full{i}") for i in range(2)]

        row_at = {}
        row_loads = []
        fill = [0, 0, 0]

        def rows_of(name, src, tile):
            n = src.shape[0]
            row_at[name] = (tile, fill[tile])
            row_loads.append((ROWS[fill[tile]:fill[tile] + n, tile, :], src))
            fill[tile] += n
            assert fill[tile] <= P

        def vec(ap):
            return ap.rearrange("(k p) -> k p", p=P)

        for l in range(2):
            rows_of(f"norm_mix{l}", vec(A["norm_mix"][l]), 0)
            rows_of(f"norm_ffn{l}", vec(A["norm_ffn"][l]), 0)
            rows_of(f"ffn1_pre{l}", vec(A["ffn1_pre_g_2"][l]), 0)
            rows_of(f"mix_pre{l}", vec(A["mix_pre_g_2"][l]), 0)
            rows_of(f"ffn2_pre{l}", vec(A["ffn2_pre_g_2"][l]), 0)
        rows_of("head_norm", vec(A["od_head_norm"][0]), 0)
        rows_of("lam", vec(A["ev_lambda"][0]), 0)
        rows_of("conv_w", A["ev_conv_w"][0].rearrange("t (k p) -> (t k) p", p=P), 0)
        rows_of("conv_b", vec(A["ev_conv_b"][0]), 0)
        rows_of("ga_b", vec(A["ev_ga_b"][0]), 0)
        rows_of("gx_b", vec(A["ev_gx_b"][0]), 0)
        for l in range(2):
            for n, src in (("sc_conv_w", None), ("rk_mu", None), ("rk_w0", None), ("rk_a0", None), ("rk_k_k", None),
                           ("rk_k_a", None), ("rk_r_k", None), ("rk_ln_w", None), ("rk_ln_b", None),
                           ("cm_conv_w", None), ("cm_conv_b", None), ("cm_ln_w", None), ("cm_ln_b", None)):
                a = A[n + "_2"][l]
                if n in ("sc_conv_w", "cm_conv_w"):
                    a = a.rearrange("t (k p) -> (t k) p", p=P)
                elif n == "rk_r_k":
                    a = a.rearrange("(k x) d -> k (x d)", x=2)
                else:
                    a = vec(a)
                rows_of(f"{n}{l}", a, 1 + l)
        rows_of("gate_b", vec(A["od_gate_b"][0]), 1)

        def col(name, i=0):
            tile, r = row_at[name]
            return COLS[:, tile, r + i:r + i + 1]

        def colr(name, n):
            tile, r = row_at[name]
            return COLS[:, tile, r:r + n]

        c = Carve()
        GA, GX = c(4, P), c(4, P)
        FB = c(8)
        EV_KEEP = c.at
        XR = c(4, S + 4)
        YR, Q, K = c(4, S), c(4, S), c(4, S)
        V = c(2, 512)
        XC, RG, IG, AE, TH = c(4, S), c(4, S), c(4, S), c(4, S), c(4, S)
        FL = c(2, 8)
        SPX, SPE, SPN, SPR, SPS, SPP, SP = (c(20) for _ in range(7))
        NCT = c(S, parts=8)
        CC = c(2, 8)
        LG, PR = c(2, S), c(2, S)
        PT = c(2, 2, P)
        AMX, ASUM, AREC = c(16), c(16), c(16)
        c = Carve()
        GW2 = c(512, parts=16)
        RT = c(KT, NE)
        OQ, OK, OV, OG = c(4, S), c(4, S), c(2, D), c(2, D)
        OLR = c(2, 16)
        LRT = c(S, parts=16)
        GXX, GE, BC_, EB, ENB = c(4, S), c(4, S), c(4, S), c(4, S), c(4, S)
        KSR = c(2, 512)
        SCT = c(2, 512)
        ST = c(4, 256)
        GATES = c(TT, NE)
        LOGITS, GMAX, EQ1, EQ2 = c(TT, NE), c(TT, NE), c(TT, NE), c(TT, NE)
        GIDX = c(TT, NE).bitcast(mybir.dt.uint32)
        GIF = c(TT, NE)
        GSM = c(TT, 8)
        SDEC = c(4, 4)
        GATE_BC = c(NE, S)
        c = Carve()
        UPW = c(256)
        SGW = c(4, P)
        SGB = c(P, parts=4)
        SGG, SGBB = c(256), c(256)
        HY_EARLY = c.at
        GB, GC, XA = c(2, S), c(2, S), c(2, S + 4)
        UU, VR = c(2, S), c(2, S)
        PC = c(7, S + 4)
        Z1, Z2 = c(2, S), c(2, S + 32)
        HY_EARLY_END = c.at
        CM = c(7, S)
        LRK = c(S)
        HY_DEC = c.at
        SGW_, CB, PPV, PIN, KK = c(2, S), c(2, S), c(2, S), c(2, S), c(2, S)
        AV, GG, PP = c(2, S), c(2, S), c(2, S)
        AH, BH, KH, RH, KN = c(2, S), c(2, S), c(2, S), c(2, S), c(2, S)
        RB, RK, RV = c(2, 256), c(2, 256), c(2, 256)
        RHS = SGG.rearrange("p (h i) -> p h i", h=4)
        SA = SGBB.rearrange("p (h i) -> p h i", h=4)
        ST2 = c(8, 64)
        PPM = c(12, 1).rearrange("p (n h) a -> p n h a", n=3)
        WT = KN.rearrange("p a b -> p (a b)").rearrange("p (h t) -> p h t", h=4)
        c.at = HY_EARLY
        PAIR = [c(2, 512) for _ in range(3)]
        LT, XX = c(2, 512), c(2, 512)
        assert c.at <= HY_EARLY_END
        c.at = HY_DEC
        XT, LM, T1 = c(2, 512), c(2, 512), c(512)

        block = ctx.enter_context(nc.Block())

        def order(eng, name):
            n = [0]

            def link(ins):
                n[0] += 1
                ins.then_inc(s[name], 1)
                eng.wait_ge(s[name], n[0])
            return link

        def wait(eng, name, n):
            if not isinstance(n, int) or n > 0:
                eng.wait_ge(s[name], n)

        @block.sync
        def _(sp):
            def load(c_, slot, src):
                if not isinstance(c_, int) or c_ >= RING:
                    sp.wait_ge(s["lo_ready"], c_ - RING + 1)
                sp.dma_start(RAW[:, slot, :].rearrange("p (k n) -> p k n", k=src.shape[1]) if src.shape[1] * src.shape[2] == 1024
                             else RAW[:, slot, 0:src.shape[1] * src.shape[2]].rearrange("p (k n) -> p k n", k=src.shape[1]),
                             src).then_inc(raw_full[slot], 16)

            def columns(w, at_, n):
                return w[:, bass.ds(at_, n)].rearrange("(k p) n -> p k n", p=P)

            def rows(w, at_):
                return w[bass.ds(at_, P), :].rearrange("p (k n) -> p k n", k=1)

            for ph in plan:
                c0 = ph["c0"]
                if ph["kind"] == "proj":
                    x = 0
                    for i, n in enumerate(ph["cols"]):
                        load(c0 + i, (c0 + i) % RING, columns(ph["w"], x, n))
                        x += n
                elif ph["kind"] == "out":
                    for i in range(KT):
                        load(c0 + i, (c0 + i) % RING, rows(ph["w"], i * P))
                else:
                    F = ph["tiles"] // ph["experts"]
                    w1, w3 = ph["w1"].rearrange("e k n -> e k n"), ph["w3"]
                    w2 = ph["w2"].rearrange("e f n -> (e f) n")

                    def w13(e, j, c_, slot):
                        for w in (w1, w3):
                            if isinstance(e, int):
                                src = columns(w[e], j * P, P)
                            else:
                                src = columns(w[bass.ds(e, 1)].rearrange("e k n -> (e k) n"), j * P, P)
                            load(c_, slot % RING, src)
                            c_, slot = c_ + 1, slot + 1
                    w13(0, 0, c0, c0)
                    w13(0, 1, c0 + 2, c0 + 2)
                    load(c0 + 4, (c0 + 4) % RING, rows(w2, 0))

                    def pair(e, j, n, c_, slot):
                        w13(e, j, c_, slot)
                        load(c_ + 2, (slot + 2) % RING, rows(w2, (n - 1) * P))
                        w13(e, j + 1, c_ + 3, slot + 3)
                        load(c_ + 5, (slot + 5) % RING, rows(w2, n * P))
                    with sp.Fori(1, F // 2) as i:
                        pair(0, 2 * i, 2 * i, c0 + 6 * i - 1, c0 + 5)
                    if ph["experts"] > 1:
                        with sp.Fori(1, ph["experts"]) as e:
                            with sp.Fori(0, F // 2) as i:
                                pair(e, 2 * i, F * e + 2 * i, c0 + 3 * F * e + 6 * i - 1, c0 + 5)
                    T = ph["tiles"]
                    load(c0 + 3 * T - 1, (c0 + 3 * T - 1) % RING, rows(w2, (T - 1) * P))
            sp.wait_ge(s["h_ready"], 2 * 11)
            sp.dma_start(out[0].rearrange("(t p) d -> p t d", p=P), H[:, :, :]).then_inc(s["out_done"], 16)
            sp.wait_ge(s["out_done"], 16)

        gbc_list = [A["norm_final"]]
        for l in range(2):
            gbc_list += [A["ffn1_post_g_2"][l], A["mix_post_g_2"][l], A["ffn2_post_g_2"][l]]
        N_LOADS = len(row_loads) + 16 + 1

        @block.gpsimd
        def _(pool):
            link = order(pool, "pool_order")
            pool.dma_start(H[:, :, :], A["x"][0].rearrange("(t p) d -> p t d", p=P)).then_inc(s["x_loaded"], 16)
            link(nc.gpsimd.memset(ROWS[:, :, :], 0.0))
            for dst, src in row_loads:
                pool.dma_start(dst, src).then_inc(s["loads_done"], 16)
            link(nc.gpsimd.memset(GA[:, :, :], 0.0))
            link(nc.gpsimd.memset(GX[:, :, :], 0.0))
            for dst, src in ((GA, A["ev_ga_w"]), (GX, A["ev_gx_w"])):
                for n in range(8):
                    o = 64 * (n % 2)
                    pool.dma_start(dst[o:o + 64, n // 2, o:o + 64], src[0, n]).then_inc(s["loads_done"], 16)
            pool.dma_start(FB[:, :], A["ev_f_b"].broadcast_to([P, 8])).then_inc(s["loads_done"], 16)

            def select(t, op, fill_, pattern, base, cm):
                link(nc.gpsimd.affine_select(out=t, in_=t, compare_op=op, fill=fill_, base=base, pattern=pattern,
                                             channel_multiplier=cm))
            link(nc.gpsimd.memset(IDENT[:, :], 0.0))
            link(nc.gpsimd.memset(ONES[:, :], 1.0))
            link(nc.gpsimd.memset(UPPER[:, :], 1.0))
            link(nc.gpsimd.memset(BLOCK64[:, :], 0.0))
            link(nc.gpsimd.memset(BLOCK64[0:64, 0:64], 1.0))
            link(nc.gpsimd.memset(BLOCK64[64:128, 64:128], 1.0))
            link(nc.gpsimd.memset(CAUSAL[:, :], 0.0))
            link(nc.gpsimd.memset(SEL[:, :, :], 1.0))
            link(nc.gpsimd.memset(RESET[:, :], 1.0))
            link(nc.gpsimd.memset(RESET[:, 0:4 * S:64], 0.0))
            link(nc.gpsimd.memset(LEVEL[:, :, :], 1.0))
            select(IDENT[:, :], ALU.not_equal, 1.0, [[-1, P]], 0, 1)
            select(UPPER[:, :], ALU.is_ge, 0.0, [[1, P]], 0, -1)
            link(nc.gpsimd.tensor_tensor(UPPER64[:, :], UPPER[:, :], BLOCK64[:, :], ALU.mult))
            link(nc.gpsimd.tensor_tensor(STRICT64[:, :], UPPER64[:, :], IDENT[:, :], ALU.subtract))
            select(CAUSAL[:, P:2 * P], ALU.is_ge, NEG, [[-1, P]], 0, 1)
            select(SEL[:, :, :], ALU.is_equal, 0.0, [[1, 8], [0, P]], 0, -1)
            for j in range(NE):
                link(nc.gpsimd.memset(IOTA8[:, j:j + 1], float(j)))
            for lv in range(6):
                half = 1 << lv
                nb = P // (2 * half)
                view = LEVEL[:, lv, :].rearrange("p (b o x) -> p b o x", b=nb, o=2)
                link(nc.gpsimd.memset(view[:, :, 0, :], 0.0))
                part = view[:, :, 1, :]
                select(part, ALU.is_ge, 0.0, [[-2 * half, nb], [0, half]], 0, 1)
                select(part, ALU.is_ge, 0.0, [[2 * half, nb], [0, half]], half - 1, -1)
            nc.gpsimd.tensor_copy(IOTA8[:, 0:1], IOTA8[:, 0:1]).then_inc(s["consts_ready"], 1)
            for i, g in enumerate(gbc_list):
                if i >= 2:
                    pool.wait_ge(s["gbc_used"], i - 1)
                pool.dma_start(GBC[:, i % 2, :], g.rearrange("(a n) -> a n", a=1).broadcast_to([P, D]))\
                    .then_inc(gbc_full[i % 2], 16)
                if i == 0:
                    pool.wait_ge(s["mixer_done"], 1)
                    pool.dma_start(GW2[:, :], A["od_gate_w2"][0]).then_inc(s["router_ready"], 16)
                    pool.dma_start(RT[:, :, :], A["od_router"][0].rearrange("(k p) e -> p k e", p=P))\
                        .then_inc(s["router_ready"], 16)
                if i in (1, 4):
                    l = i // 3
                    pool.wait_ge(s["mixer_done"], 2 + l)
                    for dst, src in ((UPW[0:32, :], A["rk_w_up_2"][l]), (UPW[32:64, :], A["rk_a_up_2"][l]),
                                     (UPW[64:128, :], A["rk_g_up_2"][l]),
                                     (SGW[:, :, :], A["sg_w_2"][l].rearrange("h t s -> t h s")),
                                     (SGB[:, :], A["sg_b_2"][l]),
                                     (SGG[:, :], A["sg_ln_w_2"][l:l + 1, :].broadcast_to([P, 256])),
                                     (SGBB[:, :], A["sg_ln_b_2"][l:l + 1, :].broadcast_to([P, 256]))):
                        pool.dma_start(dst, src).then_inc(s["up_in_ready"], 16)

        def ev_dest(i):
            t, o = i // 4, i % 4
            if t == 0:
                return XR[:, o, 4:S + 4], False
            if t < 4:
                return (None, YR, Q, K)[t][:, o, :], False
            return (V[:, :, o * P:(o + 1) * P] if t == 4 else FL[:, :, :]), True

        def od_dest(i):
            if i < 8:
                return (OQ, OK)[i // 4][:, i % 4, :], False
            if i < 24:
                o = (i - 8) % 8
                return (OV, OG)[(i - 8) // 8][:, :, o * P:(o + 1) * P], True
            return OLR[:, :, :], True

        def hy_dest(i):
            if i < 6:
                return (GB, GC, XA)[i // 2][:, i % 2, 0:S] if i < 4 else XA[:, i % 2, 4:S + 4], False
            if i < 8:
                return UU[:, i % 2, :], False
            if i < 10:
                return VR[:, :, (i - 8) * P:(i - 7) * P], True
            if i < 17:
                return PC[:, i - 10, 4:S + 4], False
            return (Z1[:, i - 17, :] if i < 19 else Z2[:, i - 19, 32:S + 32]), False

        def counter():
            n = {}

            def nxt(name, by=1):
                n[name] = n.get(name, 0) + by
                return n[name]
            return nxt

        def last_chunk(ph):
            return ph["c0"] + (KT if ph["kind"] == "out" else 3 * ph["tiles"]) - 1

        def words(c_):
            return width.get(c_, 1024) if isinstance(c_, int) else 1024

        @block.tensor
        def _(pe):
            nxt = counter()
            mm = nc.tensor.matmul
            tr = nc.tensor.transpose

            def wslot(slot, k):
                return (WHI[:, slot, :].rearrange("p (k n) -> p k n", k=k),
                        WLO[:, slot, :].rearrange("p (k n) -> p k n", k=k))

            def narrow(slot, n):
                return (WHI[:, slot, 0:KT * n].rearrange("p (k n) -> p k n", k=KT),
                        WLO[:, slot, 0:KT * n].rearrange("p (k n) -> p k n", k=KT))

            def x_wait(first, kt):
                if first:
                    pe.wait_ge(s["x_ready"], nxt("x_ready"))

            def project(ph, dest):
                for i, n in enumerate(ph["cols"]):
                    c_, q = ph["c0"] + i, ph["q0"] + i
                    wait(pe, "lo_ready", c_ + 1)
                    wait(pe, "bank_free", q - 1)
                    wh, wl = narrow(c_ % RING, n)
                    bank = BANK[q % 2]
                    row = dest(i)[1]
                    for t in range(TT if row else 1):
                        for kt in range(KT):
                            if t == 0:
                                x_wait(i == 0, kt)
                            for a, (w, x) in enumerate(((wh, XHI), (wh, XLO), (wl, XHI))):
                                st, sp_ = (kt == 0 and a == 0), (kt == KT - 1 and a == 2)
                                if row:
                                    last = mm(bank[:, t * n:(t + 1) * n], x[:, kt, t * P:(t + 1) * P], w[:, kt, :],
                                              start=st, stop=sp_)
                                else:
                                    last = mm(bank[:, 0:S], w[:, kt, :], x[:, kt, :], start=st, stop=sp_)
                    last.then_inc(s["chunk_used"], 1)

            def output(ph):
                for kt in range(KT):
                    c_ = ph["c0"] + kt
                    wait(pe, "lo_ready", c_ + 1)
                    if kt == 0:
                        pe.wait_ge(s["x_ready"], nxt("x_ready", KT))
                    wh, wl = WHI[:, c_ % RING, :], WLO[:, c_ % RING, :]
                    for t in range(TT):
                        for a, (x, w) in enumerate(((XHI, wh), (XHI, wl), (XLO, wh))):
                            for h in range(2):
                                last = mm(YB[t][h][:, :], x[:, kt, t * P:(t + 1) * P], w[:, h * 512:(h + 1) * 512],
                                          start=(kt == 0 and a == 0), stop=(kt == KT - 1 and a == 2))
                    last.then_inc(s["chunk_used"], 1)

            def up(c_, slot, q, qb, first=False):
                wait(pe, "bank_free", q - 1)
                for half in range(2):
                    wait(pe, "lo_ready", c_ + half + 1)
                    wh, wl = wslot((slot + half) % RING, KT)
                    for kt in range(KT):
                        x_wait(first and half == 0, kt)
                        for a, (w, x) in enumerate(((wh, XHI), (wh, XLO), (wl, XHI))):
                            last = mm(BANK[qb][:, half * S:(half + 1) * S], w[:, kt, :], x[:, kt, :],
                                      start=(kt == 0 and a == 0), stop=(kt == KT - 1 and a == 2))
                    last.then_inc(s["chunk_used"], 1)

            def down(c_, slot, t_, b, start=False, stop=False):
                wait(pe, "lo_ready", c_ + 1)
                wait(pe, "hid_ready", t_ + 1)
                wh, wl = WHI[:, slot % RING, :], WLO[:, slot % RING, :]
                for t in range(TT):
                    for a, (x, w) in enumerate(((HIDHI, wh), (HIDHI, wl), (HIDLO, wh))):
                        for h in range(2):
                            last = mm(YB[t][h][:, :], x[:, b, t * P:(t + 1) * P], w[:, h * 512:(h + 1) * 512],
                                      start=(start and a == 0), stop=(stop and a == 2), skip_group_check=True)
                last.then_inc(s["chunk_used"], 1)

            def ffn(ph):
                c0, q0, t0, T = ph["c0"], ph["q0"], ph["t0"], ph["tiles"]
                up(c0, c0, q0, q0 % 2, True)
                up(c0 + 2, c0 + 2, q0 + 1, (q0 + 1) % 2)
                down(c0 + 4, c0 + 4, t0, t0 % 2, start=True)
                with pe.Fori(0, T // 2 - 1) as i:
                    up(c0 + 5 + 6 * i, c0 + 5, q0 + 2 + 2 * i, q0 % 2)
                    down(c0 + 7 + 6 * i, c0 + 7, t0 + 1 + 2 * i, (t0 + 1) % 2)
                    up(c0 + 8 + 6 * i, c0 + 8, q0 + 3 + 2 * i, (q0 + 1) % 2)
                    down(c0 + 10 + 6 * i, c0 + 10, t0 + 2 + 2 * i, t0 % 2)
                down(c0 + 3 * T - 1, c0 + 3 * T - 1, t0 + T - 1, (t0 + T - 1) % 2, stop=True)

            def turn(src, src_ready, row=False):
                pe.wait_ge(s[src_ready], nxt(src_ready))
                for b in range(4):
                    for j in range(2):
                        for t in range(TT):
                            kt = 2 * b + j
                            last = tr(BANK[4 + b][:, (2 * j + t) * P:(2 * j + t + 1) * P],
                                      src[:, t, kt * P:(kt + 1) * P], IDENT[:, :])
                    last.then_inc(s["tp_ready"], 1)

            def even_mixer():
                pe.wait_ge(s["conv_ready"], 1)
                for w, b in ((GA, 4), (GX, 6)):
                    for i in range(4):
                        last = mm(BANK[b + i // 2][:, (i % 2) * S:(i % 2 + 1) * S], w[:, i, :], XC[:, i, :],
                                  start=True, stop=True)
                last.then_inc(s["gates_mm"], 1)
                pe.wait_ge(s["small_ready"], 1)
                lf = SP[:, 4:20].rearrange("p (t h) -> p t h", t=TT)
                mm(BANK[0][0:8, 0:P], lf[:, 0, :], UPPER[:, :], start=True, stop=True)
                mm(BANK[0][0:8, P:S], lf[:, 0, :], ONES[:, :], start=True, stop=False)
                mm(BANK[0][0:8, P:S], lf[:, 1, :], UPPER[:, :], start=False, stop=True)
                mm(BANK[1][:, 0:8], UPPER[:, :], lf[:, 0, :], start=True, stop=True)
                mm(BANK[1][:, 8:16], ONES[:, :], lf[:, 0, :], start=True, stop=False)
                mm(BANK[1][:, 8:16], UPPER[:, :], lf[:, 1, :], start=False, stop=True).then_inc(s["cum_ready"], 1)
                pe.wait_ge(s["cumev_ready"], 1)

                def scores(u):
                    h, t = u // 2, u % 2
                    o, n = 64 * (h % 2), (t + 1) * P
                    wait(pe, "logit_ready", u - 1)
                    mm(BANK[2 + u % 2][:, 0:n], Q[o:o + 64, h // 2, t * P:(t + 1) * P], K[o:o + 64, h // 2, 0:n],
                       start=True, stop=False)
                    mm(BANK[2 + u % 2][:, 0:n], SEL[:, h, :], NCT[:, 0:n], start=False, stop=True)\
                        .then_inc(s["score_ready"], 1)
                scores(0)
                scores(1)
                pe.wait_ge(s["sig_ready"], 8)
                for u in range(16):
                    h, t = u // 2, u % 2
                    o = 64 * (h % 2)
                    pe.wait_ge(s["probn_ready"], u + 1)
                    wait(pe, "probt_copied", u - 1)
                    for b in range(t + 1):
                        last = tr(BANK[u % 2][:, b * P:(b + 1) * P], PR[:, u % 2, b * P:(b + 1) * P], IDENT[:, :])
                    last.then_inc(s["probt_ready"], 1)
                    if u + 2 < 16:
                        scores(u + 2)
                    pe.wait_ge(s["probt_copied"], u + 1)
                    for b in range(t + 1):
                        last = mm(BANK[4 + h // 2][o:o + 64, t * P:(t + 1) * P], V[:, b, h * 64:(h + 1) * 64],
                                  PT[:, u % 2, b, :], start=(b == 0), stop=(b == t))
                    last.then_inc(s["pv_ready"], 1)

            def odd_mixer():
                pe.wait_ge(s["lrk_ready"], 1)
                for t in range(TT):
                    last = tr(BANK[2][0:16, t * P:(t + 1) * P], OLR[:, t, :], IDENT[:, :])
                last.then_inc(s["lr_tp"], 1)
                pe.wait_ge(s["lrt_ready"], 1)
                pe.wait_ge(s["router_ready"], 32)
                for i in range(4):
                    last = mm(BANK[4 + i // 2][:, (i % 2) * S:(i % 2 + 1) * S], GW2[:, i * P:(i + 1) * P], LRT[:, :],
                              start=True, stop=True)
                last.then_inc(s["gate_mm"], 1)
                pe.wait_ge(s["kdec_ready"], 1)
                for t in range(TT):
                    for h in range(4):
                        last = tr(BANK[6 + t][:, h * P:(h + 1) * P], GXX[:, h, t * P:(t + 1) * P], IDENT[:, :])
                last.then_inc(s["kstp_ready"], 1)
                for t in range(TT):
                    for h in range(4):
                        last = mm(BANK[2 + t][:, h * P:(h + 1) * P], ENB[:, h, t * P:(t + 1) * P],
                                  EB[:, h, t * P:(t + 1) * P], start=True, stop=True)
                    last.then_inc(s["sct_mm"], 1)
                OB = [[BANK[4], BANK[5]], [BANK[0], BANK[1]]]
                pe.wait_ge(s["ksr_ready"], 1)
                for n in range(4):
                    t, o = n // 2, 64 * (n % 2)
                    if n % 2 == 0:
                        pe.wait_ge(s["sct_ready"], t + 1)
                        for h in range(4):
                            mm(OB[t][h // 2][:, (h % 2) * 256:(h % 2 + 1) * 256], SCT[:, t, h * P:(h + 1) * P],
                               OV[:, t, h * 256:(h + 1) * 256], start=(h % 2 == 0), stop=True, skip_group_check=True)
                    if n:
                        pe.wait_ge(s["state_ready"], n)
                    for h in range(4):
                        if n:
                            last = mm(OB[t][h // 2][o:o + 64, (h % 2) * 256:(h % 2 + 1) * 256],
                                      EB[:, h, n * 64:(n + 1) * 64], ST[:, h, :], start=False, stop=True,
                                      skip_group_check=True)
                        if n < 3:
                            upd = mm(BANK[6 + h // 2][:, (h % 2) * 256:(h % 2 + 1) * 256],
                                     KSR[o:o + 64, t, h * P:(h + 1) * P], OV[o:o + 64, t, h * 256:(h + 1) * 256],
                                     start=True, stop=True)
                    if n < 3:
                        upd.then_inc(s["upd_ready"], 1)
                    else:
                        last.then_inc(s["o_ready"], 1)

            def router():
                pe.wait_ge(s["x_ready"], KT * 6)
                for t in range(TT):
                    for kt in range(KT):
                        for a, x in enumerate((XHI, XLO)):
                            last = mm(BANK[2][:, t * NE:(t + 1) * NE], x[:, kt, t * P:(t + 1) * P].bitcast(F32),
                                      RT[:, kt, :], start=(kt == 0 and a == 0), stop=(kt == KT - 1 and a == 1))
                last.then_inc(s["score_ready"], 1)
                for e in range(NE):
                    for t in range(TT):
                        i = 2 * e + t
                        pe.wait_ge(s["gates_ready"], i + 1)
                        mm(BANK[2 + i % 2][:, 0:P], ONES[:, :],
                           SIL[:, i % 2, 0:P], start=True, stop=True).then_inc(s["gate_mm"], 1)

            def hybrid(l):
                R = range
                pe.wait_ge(s["vn_ready"], 2 * l + 1)
                for h in R(4):
                    last = tr(BANK[2][:, h * P:(h + 1) * P], SGW[:, h, :], IDENT[:, :])
                last.then_inc(s["wt_tp"], 1)
                pe.wait_ge(s["wt_ready"], l + 1)
                pe.wait_ge(s["vn_ready"], 2 * l + 2)
                for t in R(TT):
                    for h in R(4):
                        o = 64 * (h % 2)
                        dst = BANK[3][o:o + 64, (2 * (h // 2) + t) * P:(2 * (h // 2) + t + 1) * P]
                        mm(dst, VR[:, t, h * 64:(h + 1) * 64], WT[:, h, :], start=True, stop=False)
                        last = mm(dst, SEL[0:4, h, 0:64], SGB[:, :], start=False, stop=True)
                last.then_inc(s["sp_mm"], 1)
                pe.wait_ge(s["zln_in"], l + 1)
                for i in R(2):
                    last = mm(BANK[4][:, 0:S], ONES[:, :], Z1[:, i, :], start=(i == 0), stop=(i == 1))
                last.then_inc(s["zln_mm"], 1)
                pe.wait_ge(s["zc_in"], l + 1)
                for i in R(2):
                    last = mm(BANK[5][:, 0:S], ONES[:, :], Z2[:, i, 0:S], start=(i == 0), stop=(i == 1))
                last.then_inc(s["zv_mm"], 1)
                pe.wait_ge(s["lrk_act"], 3 * (l + 1))
                for j, (a, b) in enumerate(((0, 32), (32, 64), (64, 128))):
                    for i in R(2):
                        last = mm(BANK[6 if j == 0 else 7 if j == 1 else 2][:, i * S:(i + 1) * S],
                                  UPW[a:b, i * P:(i + 1) * P], LRK[a:b, :], start=True, stop=True)
                last.then_inc(s["up_mm"], 1)
                pe.wait_ge(s["kk_in"], l + 1)
                mm(BANK[3][:, :], BLOCK64[:, :], KN.rearrange("p a b -> p (a b)"), start=True, stop=True)\
                    .then_inc(s["nrm_mm"], 1)
                pe.wait_ge(s["bonus_in"], l + 1)
                mm(BANK[4][:, :], BLOCK64[:, :], RB.rearrange("p a b -> p (a b)"),
                   start=True, stop=True).then_inc(s["bonus_mm"], 1)
                pe.wait_ge(s["abkr_ready"], l + 1)
                for j, src in enumerate((BH, KH, CM[:, 4:6, :])):
                    for t in R(TT):
                        for i in R(2):
                            last = tr(BANK[5 + j][:, (2 * t + i) * P:(2 * t + i + 1) * P], src[:, i, t * P:(t + 1) * P],
                                      IDENT[:, :])
                last.then_inc(s["rows_tp"], 1)

                n = 0
                for lh, rh in ((BH, AH), (KH, AH), (BH, RH), (KH, RH)):
                    for par in R(2):
                        if n >= 2:
                            pe.wait_ge(s["pair_ready"], 8 * l + n - 1)
                        o = 64 * par
                        for t in R(TT):
                            for hp in R(2):
                                last = mm(BANK[n % 2][:, (2 * t + hp) * P:(2 * t + hp + 1) * P],
                                          lh[o:o + 64, hp, t * P:(t + 1) * P], rh[o:o + 64, hp, t * P:(t + 1) * P],
                                          start=True, stop=True)
                        last.then_inc(s["pair_mm"], 1)
                        n += 1
                pe.wait_ge(s["pair_ready"], 8 * l + 8)
                pe.wait_ge(s["rows_ready"], l + 1)
                for lv in R(6):
                    for t in R(TT):
                        m = 12 * l + 2 * lv + t
                        pe.wait_ge(s["lvl_in"], m + 1)
                        for h in R(4):
                            hs = slice(h * P, (h + 1) * P)
                            last = mm(BANK[2 + 3 * t][:, hs], LM[:, t, hs], XX[:, t, hs], start=True, stop=True)
                        last.then_inc(s["t1_mm"], 1)
                        pe.wait_ge(s["t1_ready"], m + 1)
                        for h in R(4):
                            hs = slice(h * P, (h + 1) * P)
                            if lv < 5:
                                mm(BANK[3 + 3 * t][:, hs], XT[:, t, hs], T1[:, hs], start=True, stop=True)
                            last = mm(BANK[4 + 3 * t][:, hs], T1[:, hs], XT[:, t, hs], start=True, stop=True)
                        last.then_inc(s["xx_mm"], 1)
                pe.wait_ge(s["xx_ready"], 12 * l + 12)
                AK, BR, KR = PAIR
                for n in R(4):
                    t, o = n // 2, 64 * (n % 2)
                    cs = slice(n * 64, (n + 1) * 64)
                    if n:
                        pe.wait_ge(s["sn_ready"], 3 * l + n)
                    new = 4 * (n % 2)
                    for h in R(4):
                        hc = slice(h * P + o, h * P + o + 64)
                        dst = BANK[0][o:o + 64, h * 64:(h + 1) * 64]
                        if n:
                            mm(dst, AH[:, h // 2, cs], ST2[:, new + h, :], start=True, stop=False)
                        last = mm(dst, AK[:, t, hc], RV[:, t, h * 64:(h + 1) * 64], start=(n == 0), stop=True)
                    last.then_inc(s["rhs_mm"], 1)
                    pe.wait_ge(s["rhs_ready"], 4 * l + n + 1)
                    for h in R(4):
                        hc = slice(h * P + o, h * P + o + 64)
                        last = mm(BANK[1][o:o + 64, h * 64:(h + 1) * 64], XT[:, t, hc], RHS[:, h, :],
                                  start=True, stop=True)
                    last.then_inc(s["sa_mm"], 1)
                    pe.wait_ge(s["sa_ready"], 4 * l + n + 1)
                    for h in R(4 if n < 3 else 0):
                        js, dst = slice((h // 2) * P, (h // 2 + 1) * P), BANK[2][:, h * 64:(h + 1) * 64]
                        mm(dst, RB[o:o + 64, t, js], SA[o:o + 64, h, :], start=True, stop=False)
                        last = mm(dst, RK[o:o + 64, t, js], RV[o:o + 64, t, h * 64:(h + 1) * 64],
                                  start=False, stop=True)
                    if n < 3:
                        last.then_inc(s["sn_mm"], 1)
                    for h in R(4):
                        ho, hc = 64 * (h % 2), slice(h * P + o, h * P + o + 64)
                        dst = BANK[3][ho:ho + 64, (h // 2) * S + n * 64:(h // 2) * S + (n + 1) * 64]
                        mm(dst, SA[:, h, :], BR[:, t, hc], start=True, stop=False)
                        if n:
                            mm(dst, ST2[:, new + h, :], RH[:, h // 2, cs], start=False, stop=False)
                        last = mm(dst, RV[:, t, h * 64:(h + 1) * 64], KR[:, t, hc], start=False, stop=True)
                    last.then_inc(s["yc_mm"], 1)
                pe.wait_ge(s["mean_in"], l + 1)
                mm(BANK[5][:, :], BLOCK64[:, :], AH.rearrange("p a b -> p (a b)"), start=True, stop=True)\
                    .then_inc(s["mean_mm"], 1)
                pe.wait_ge(s["var_in"], l + 1)
                mm(BANK[6][:, :], BLOCK64[:, :], BH.rearrange("p a b -> p (a b)"), start=True, stop=True)\
                    .then_inc(s["var_mm"], 1)

            pe.wait_ge(s["consts_ready"], 1)
            pe.wait_ge(s["loads_done"], 16 * N_LOADS)
            pe.wait_ge(s["rows_zero"], 1)
            for t in range(3):
                last = tr(BANK[t][:, 0:P], ROWS[:, t, :], IDENT[:, :])
            last.then_inc(s["cols_tp"], 1)
            pe.wait_ge(s["cols_ready"], 1)
            turn(HN, "hn_ready")
            project(EV_PROJ, ev_dest)
            even_mixer()
            output(EV_OUT)
            turn(HN, "hn_ready")
            ffn(EV_FFN)
            turn(HN, "hn_ready")
            project(OD_PROJ, od_dest)
            odd_mixer()
            turn(OG, "og_ready")
            output(OD_OUT)
            turn(HN, "hn_ready")
            router()
            ffn(MOE)
            for l in range(2):
                f1, pr, ou, f2 = HY[l]
                turn(HN, "hn_ready")
                ffn(f1)
                turn(HN, "hn_ready")
                project(pr, hy_dest)
                hybrid(l)
                output(ou)
                turn(HN, "hn_ready")
                ffn(f2)

        @block.scalar
        def _(act):
            nxt = counter()
            link = order(act, "act_order")
            af = nc.scalar.activation
            top = [0]

            def split_hi(c_, slot, n=1024):
                if isinstance(c_, int):
                    act.wait_ge(raw_full[slot], 16 * (c_ // RING + 1))
                    wait(act, "chunk_used", c_ - RING + 1)
                nc.scalar.copy(WHI[:, slot, 0:n], RAW[:, slot, 0:n]).then_inc(s["hi_ready"], 1)

            def ahead(c_):
                while top[0] < min(c_ + LEAD + 1, N_CHUNKS):
                    split_hi(top[0], top[0] % RING, words(top[0]))
                    top[0] += 1

            def norm():
                for t in range(TT):
                    act.wait_ge(s["h_ready"], nxt("h_ready"))
                    af(HN[:, t, :], H[:, t, :], ACT.Square, scale=D ** -0.5, accum_out=STAT[:, t:t + 1])\
                        .then_inc(s["ssq_ready"], 1)

            def gain(name):
                for b in range(4):
                    act.wait_ge(s["tp_ready"], nxt("tp_ready"))
                    for j in range(2):
                        kt = 2 * b + j
                        af(XHI[:, kt, :], BANK[4 + b][:, j * S:(j + 1) * S], ACT.Copy, scale=col(name, kt))\
                            .then_inc(s["xhi_ready"], 1)

            def project(ph):
                for i in range(len(ph["cols"])):
                    ahead(ph["c0"] + i)

            def output(ph):
                for i in range(KT):
                    ahead(ph["c0"] + i)

            def silu(q, b, c_):
                act.wait_ge(s["chunk_used"], c_ + 1)
                wait(act, "bank_free", q - 1)
                af(SIL[:, b, :], BANK[b][:, 0:S], ACT.Silu).then_inc(s["silu_ready"], 1)

            def ffn(ph):
                c0, q0, T = ph["c0"], ph["q0"], ph["tiles"]
                ahead(c0 + 1)
                silu(q0, q0 % 2, c0 + 1)
                ahead(c0 + 4)
                silu(q0 + 1, (q0 + 1) % 2, c0 + 3)
                base = top[0]
                assert base == c0 + 8
                with act.Fori(0, T // 2 - 2) as i:
                    for j in range(2):
                        for m in range(3):
                            k = base + 3 * j + m
                            act.wait_ge(raw_full[k % RING], 16 * (k // RING + 1) + 16 * i)
                            act.wait_ge(s["chunk_used"], k - RING + 1 + 6 * i)
                            split_hi(None, k % RING)
                        q = q0 + 2 + j
                        act.wait_ge(s["chunk_used"], c0 + 3 * (2 + j) + 1 + 6 * i)
                        act.wait_ge(s["bank_free"], q - 1 + 2 * i)
                        af(SIL[:, q % 2, :], BANK[q % 2][:, 0:S], ACT.Silu).then_inc(s["silu_ready"], 1)
                top[0] = base + 6 * (T // 2 - 2)
                for n in (T - 2, T - 1):
                    ahead(c0 + 3 * n + 1)
                    silu(q0 + n, (q0 + n) % 2, c0 + 3 * n)
                ahead(c0 + 3 * T - 1)

            def post(c_):
                act.wait_ge(s["chunk_used"], c_ + 1)
                for t in range(TT):
                    for h in range(2):
                        af(HN[:, t, h * 512:(h + 1) * 512], YB[t][h][:, :], ACT.Square, scale=D ** -0.5,
                           accum_out=STAT[:, 4 + 2 * t + h:5 + 2 * t + h]).then_inc(s["ssq_ready"], 1)

            def even_mixer():
                act.wait_ge(s["spx_ready"], 1)
                af(SPE[:, :], SPN[:, :], ACT.Exp).then_inc(s["spe_ready"], 1)
                act.wait_ge(s["gates_mm"], 1)
                for g, name, b in ((RG, "ga_b", 4), (IG, "gx_b", 6)):
                    for i in range(4):
                        af(g[:, i, :], BANK[b + i // 2][:, (i % 2) * S:(i % 2 + 1) * S], ACT.Sigmoid,
                           bias=col(name, i)).then_inc(s["sig_ready"], 1)
                act.wait_ge(s["sig_ready"], 8)
                act.wait_ge(s["small_ready"], 1)
                for i in range(4):
                    af(AE[:, i, :], RG[:, i, :], ACT.Exp, scale=SPR[:, i:i + 1]).then_inc(s["aexp_ready"], 1)
                    af(TH[:, i, :], RG[:, i, :], ACT.Tanh, scale=SPS[:, i:i + 1]).then_inc(s["aexp_ready"], 1)
                act.wait_ge(s["root_in"], 1)
                af(TH[:, :, :], TH[:, :, :], ACT.Sqrt).then_inc(s["root_ready"], 1)
                for i in range(4):
                    af(YR[:, i, :], YR[:, i, :], ACT.Gelu_apprx_tanh).then_inc(s["gelu_ready"], 1)

                def copy(u):
                    act.wait_ge(s["probt_ready"], u + 1)
                    wait(act, "pv_ready", u - 1)
                    n = u % 2 + 1
                    nc.scalar.copy(PT[:, u % 2, 0:n, :], BANK[u % 2][:, 0:n * P].rearrange("p (b q) -> p b q", b=n))\
                        .then_inc(s["probt_copied"], 1)
                for u in range(17):
                    if u < 16:
                        n = (u % 2 + 1) * P
                        act.wait_ge(s["logit_ready"], u + 1)
                        wait(act, "probt_ready", u - 1)
                        af(PR[:, u % 2, 0:n], LG[:, u % 2, 0:n], ACT.Exp, bias=AMX[:, u:u + 1],
                           accum_out=ASUM[:, u:u + 1]).then_inc(s["prob_ready"], 1)
                    if u:
                        copy(u - 1)

            def odd_mixer():
                act.wait_ge(s["nab_ready"], 1)
                af(GE[:, :, :], GE[:, :, :], ACT.Exp).then_inc(s["gexp_ready"], 1)
                act.wait_ge(s["gexp1_ready"], 1)
                af(GE[:, :, :], GE[:, :, :], ACT.Ln).then_inc(s["gln_ready"], 1)
                act.wait_ge(s["bcum_ready"], 1)
                af(EB[:, :, :], BC_[:, :, :], ACT.Exp, scale=1.0 / 16).then_inc(s["bexp_ready"], 1)
                af(ENB[:, :, :], BC_[:, :, :], ACT.Exp, scale=-1.0 / 16).then_inc(s["bexp_ready"], 1)
                af(GXX[:, :, :], GXX[:, :, :], ACT.Exp, scale=1.0 / 16).then_inc(s["bexp_ready"], 1)
                act.wait_ge(s["kstp_ready"], 1)
                for t in range(TT):
                    last = nc.scalar.copy(KSR[:, t, :], BANK[6 + t][:, :])
                last.then_inc(s["ksr_ready"], 1)
                af(OG[:, :, :], OG[:, :, :], ACT.Silu).then_inc(s["silug_ready"], 1)
                for t in range(TT):
                    if t == 0:
                        act.wait_ge(s["upd_ready"], 2)
                    else:
                        act.wait_ge(s["o_ready"], 1)
                    for h in range(4):
                        b = ((4, 5), (0, 1))[t][h // 2]
                        af(HN[:, t, h * 256:(h + 1) * 256], BANK[b][:, (h % 2) * 256:(h % 2 + 1) * 256], ACT.Square,
                           scale=256 ** -0.5, accum_out=STAT[:, 8 + 4 * t + h:9 + 4 * t + h]).then_inc(s["o_ssq"], 1)

            def router():
                act.wait_ge(s["spx_ready"], 2)
                af(GSM[:, :, 2], GSM[:, :, 1], ACT.Exp).then_inc(s["spe_ready"], 1)

            def hybrid(l):
                act.wait_ge(s["z_sig"], 2 * l + 1)
                af(Z2[:, :, 32:S + 32], Z2[:, :, 32:S + 32], ACT.Sigmoid).then_inc(s["zs_ready"], 1)
                act.wait_ge(s["zn_ready"], l + 1)
                for i in range(2):
                    af(Z1[:, i, :], Z1[:, i, :], ACT.Silu, scale=col(f"cm_ln_w{l}", i),
                       bias=col(f"cm_ln_b{l}", i)).then_inc(s["zs_ready"], 1)
                act.wait_ge(s["pexp_in"], 3 * l + 1)
                af(LRK[0:32, :], CM[0:32, 6, :], ACT.Tanh).then_inc(s["lrk_act"], 1)
                af(LRK[32:64, :], CM[32:64, 6, :], ACT.Copy).then_inc(s["lrk_act"], 1)
                af(LRK[64:128, :], CM[64:128, 6, :], ACT.Sigmoid).then_inc(s["lrk_act"], 1)
                act.wait_ge(s["up_mm"], l + 1)
                for i in range(2):
                    af(SGW_[:, i, :], BANK[6][:, i * S:(i + 1) * S], ACT.Sigmoid, bias=col(f"rk_w0{l}", i))\
                        .then_inc(s["upsig_ready"], 1)
                    af(AV[:, i, :], BANK[7][:, i * S:(i + 1) * S], ACT.Sigmoid, bias=col(f"rk_a0{l}", i))\
                        .then_inc(s["upsig_ready"], 1)
                nc.scalar.copy(GG.rearrange("p a b -> p (a b)"), BANK[2][:, :]).then_inc(s["upsig_ready"], 1)
                act.wait_ge(s["pexp_in"], 3 * l + 2)
                af(PP, CB, ACT.Exp, scale=-DECAY_C).then_inc(s["pexp_ready"], 1)
                af(PPV, PPV, ACT.Exp, scale=-DECAY_C).then_inc(s["pexp_ready"], 1)
                af(PIN, CB, ACT.Exp, scale=DECAY_C).then_inc(s["pexp_ready"], 1)
                act.wait_ge(s["rows_tp"], l + 1)
                for j, dst in enumerate((RB, RK, RV)):
                    last = nc.scalar.copy(dst.rearrange("p a b -> p (a b)"), BANK[5 + j][:, :])
                last.then_inc(s["rows_ready"], 1)
                for m in range(12):
                    t = m % 2
                    act.wait_ge(s["t1_mm"], 12 * l + m + 1)
                    if m:
                        act.wait_ge(s["xx_mm"], 12 * l + m)
                    nc.scalar.copy(T1[:, :], BANK[2 + 3 * t][:, :]).then_inc(s["t1_ready"], 1)
                for n in range(4):
                    o = 64 * (n % 2)
                    act.wait_ge(s["rhs_mm"], 4 * l + n + 1)
                    nc.scalar.copy(RHS[o:o + 64, :, :], BANK[0][o:o + 64, 0:256].rearrange("p (h i) -> p h i", h=4))\
                        .then_inc(s["rhs_ready"], 1)
                    act.wait_ge(s["sa_mm"], 4 * l + n + 1)
                    nc.scalar.copy(SA[o:o + 64, :, :], BANK[1][o:o + 64, 0:256].rearrange("p (h i) -> p h i", h=4))\
                        .then_inc(s["sa_ready"], 1)

            act.wait_ge(s["x_loaded"], 16)
            for t in range(TT):
                af(HN[:, t, :], H[:, t, :], ACT.Square, scale=D ** -0.5, accum_out=STAT[:, t:t + 1])\
                    .then_inc(s["ssq_ready"], 1)
            ahead(-1)
            act.wait_ge(s["cols_ready"], 1)
            gain("norm_mix0")
            project(EV_PROJ)
            even_mixer()
            output(EV_OUT)
            norm()
            gain("norm_ffn0")
            ffn(EV_FFN)
            norm()
            gain("norm_mix1")
            project(OD_PROJ)
            odd_mixer()
            gain("head_norm")
            output(OD_OUT)
            norm()
            gain("norm_ffn1")
            router()
            ffn(MOE)
            norm()
            for l in range(2):
                f1, pr, ou, f2 = HY[l]
                norm()
                gain(f"ffn1_pre{l}")
                ffn(f1)
                post(last_chunk(f1))
                norm()
                gain(f"mix_pre{l}")
                project(pr)
                hybrid(l)
                output(ou)
                post(last_chunk(ou))
                norm()
                gain(f"ffn2_pre{l}")
                ffn(f2)
                post(last_chunk(f2))

        @block.vector
        def _(dve):
            nxt = counter()
            link = order(dve, "dve_order")
            V_ = nc.vector
            marks = [0]

            def mark(name):
                marks[0] += 1
                V_.memset(STAT[:, 63 + marks[0]:64 + marks[0]], 0.0).then_inc(s[name], 1)
            top = [0]

            def split_lo(slot, n=1024):
                V_.tensor_tensor(WLO[:, slot, 0:n], RAW[:, slot, 0:n], WHI[:, slot, 0:n].bitcast(F32), ALU.subtract)\
                    .then_inc(s["lo_ready"], 1)

            def ahead(c_):
                while top[0] < min(c_ + LEAD + 1, N_CHUNKS):
                    dve.wait_ge(s["hi_ready"], top[0] + 1)
                    split_lo(top[0] % RING, words(top[0]))
                    top[0] += 1

            def split_x(src, a, b, inc=0):
                link(V_.tensor_copy(XHI[:, a:b, :], src))
                ins = V_.tensor_tensor(XLO[:, a:b, :], src, XHI[:, a:b, :].bitcast(F32), ALU.subtract)
                if inc:
                    ins.then_inc(s["x_ready"], inc)

            def rsqrt(y, x, tmp, mul=1.0, eps=EPS, floor=False):
                if floor:
                    link(V_.tensor_scalar(x, x, eps, None, ALU.max))
                else:
                    link(V_.tensor_scalar(x, x, mul, eps, ALU.mult, ALU.add))
                link(V_.tensor_scalar(y.bitcast(mybir.dt.int32), x.bitcast(mybir.dt.int32), -0.5, float(0x5F3759DF),
                                      ALU.mult, ALU.add))
                for _ in range(3):
                    link(V_.tensor_tensor(tmp, y, y, ALU.mult))
                    link(V_.tensor_tensor(tmp, tmp, x, ALU.mult))
                    link(V_.tensor_scalar(tmp, tmp, -0.5, 1.5, ALU.mult, ALU.add))
                    link(V_.tensor_tensor(y, y, tmp, ALU.mult))

            def norm():
                dve.wait_ge(s["ssq_ready"], nxt("ssq_ready", TT))
                rsqrt(STAT[:, 2:4], STAT[:, 0:2], STAT[:, 54:56])
                for t in range(TT):
                    last = V_.tensor_scalar(HN[:, t, :], H[:, t, :], STAT[:, 2 + t:3 + t], None, ALU.mult)
                last.then_inc(s["hn_ready"], 1)

            def gain(name):
                for b in range(4):
                    dve.wait_ge(s["xhi_ready"], nxt("xhi_ready", 2))
                    for j in range(2):
                        kt = 2 * b + j
                        V_.scalar_tensor_tensor(XLO[:, kt, :], BANK[4 + b][:, j * S:(j + 1) * S], col(name, kt),
                                                XHI[:, kt, :].bitcast(F32), ALU.mult, ALU.subtract)\
                            .then_inc(s["x_ready"], 1)

            def project(ph, dest):
                for i, n in enumerate(ph["cols"]):
                    ahead(ph["c0"] + i)
                    q = ph["q0"] + i
                    dst, row = dest(i)
                    dve.wait_ge(s["chunk_used"], ph["c0"] + i + 1)
                    src = BANK[q % 2][:, 0:2 * n].rearrange("p (t n) -> p t n", t=TT) if row else BANK[q % 2][:, 0:S]
                    V_.tensor_copy(dst, src).then_inc(s["bank_free"], 1)
                dve.wait_ge(s["bank_free"], ph["q0"] + len(ph["cols"]))

            def output(ph):
                for i in range(KT):
                    ahead(ph["c0"] + i)

            def hidden(q, t_, qb, b, gate=None):
                dve.wait_ge(s["silu_ready"], t_ + 1)
                V_.tensor_tensor(HID[:, b, :], SIL[:, qb, :], BANK[qb][:, S:2 * S], ALU.mult)\
                    .then_inc(s["bank_free"], 1)
                dve.wait_ge(s["bank_free"], q + 1)
                if gate is not None:
                    V_.tensor_tensor(HID[:, b, :], HID[:, b, :], gate, ALU.mult).then_inc(s["hid_gated"], 1)
                    dve.wait_ge(s["hid_gated"], t_ - MOE["t0"] + 1)
                V_.tensor_copy(HIDHI[:, b, :], HID[:, b, :]).then_inc(s["hidhi_made"], 1)
                dve.wait_ge(s["hidhi_made"], t_ + 1)
                V_.tensor_tensor(HIDLO[:, b, :], HID[:, b, :], HIDHI[:, b, :].bitcast(F32), ALU.subtract)\
                    .then_inc(s["hid_ready"], 1)

            def ffn(ph):
                c0, q0, t0, T, E = ph["c0"], ph["q0"], ph["t0"], ph["tiles"], ph["experts"]
                F = T // E
                g = (lambda e: GATE_BC[:, e, :]) if E > 1 else (lambda e: None)

                def one(n, e):
                    ahead(c0 + 3 * n + 1)
                    hidden(q0 + n, t0 + n, (q0 + n) % 2, (t0 + n) % 2, g(e))
                one(0, 0)
                one(1, 0)
                base = top[0]

                def pair(i, gate):
                    for j in range(2):
                        for m in range(3):
                            k = base + 3 * j + m
                            dve.wait_ge(s["hi_ready"], k + 1 + 6 * i)
                            split_lo(k % RING)
                        n = 2 + j
                        hidden(q0 + n + 2 * i, t0 + n + 2 * i, (q0 + n) % 2, (t0 + n) % 2, gate)
                if E == 1:
                    with dve.Fori(0, T // 2 - 2) as i:
                        pair(i, None)
                else:
                    with dve.Fori(0, F // 2 - 1) as i:
                        pair(i, g(0))
                    with dve.Fori(1, E - 1) as e:
                        with dve.Fori(0, F // 2) as i:
                            pair(F // 2 * e - 1 + i, GATE_BC[:, bass.ds(e, 1), :].rearrange("p a b -> p (a b)"))
                    with dve.Fori(0, F // 2 - 1) as i:
                        pair(F // 2 * (E - 1) - 1 + i, g(E - 1))
                top[0] = base + 6 * (T // 2 - 2)
                one(T - 2, E - 1)
                one(T - 1, E - 1)
                ahead(c0 + 3 * T - 1)

            def residual(ph):
                dve.wait_ge(s["chunk_used"], last_chunk(ph) + 1)
                for t in range(TT):
                    for h in range(2):
                        hs = slice(h * 512, (h + 1) * 512)
                        last = V_.tensor_tensor(H[:, t, hs], H[:, t, hs], YB[t][h][:, :], ALU.add)
                    last.then_inc(s["h_ready"], 1)

            ngbc = [0]

            def gains_wait():
                i = ngbc[0]
                dve.wait_ge(gbc_full[i % 2], 16 * (i // 2 + 1))
                ngbc[0] += 1
                return i % 2

            def post(resid):
                dve.wait_ge(s["ssq_ready"], nxt("ssq_ready", 4))
                gi = gains_wait()
                link(V_.tensor_tensor(STAT[:, 10:12], STAT[:, 4:8:2], STAT[:, 5:8:2], ALU.add))
                rsqrt(STAT[:, 12:14], STAT[:, 10:12], STAT[:, 54:56])
                link(V_.tensor_scalar(STAT[:, 12:14], STAT[:, 12:14], resid, None, ALU.mult))
                for t in range(TT):
                    for h in range(2):
                        hs = slice(h * 512, (h + 1) * 512)
                        last = V_.scalar_tensor_tensor(HN[:, t, hs], YB[t][h][:, :], STAT[:, 12 + t:13 + t],
                                                       GBC[:, gi, hs], ALU.mult, ALU.mult)
                    if t == TT - 1:
                        last.then_inc(s["gbc_used"], 1)
                dve.wait_ge(s["gbc_used"], ngbc[0])
                for t in range(TT):
                    V_.tensor_tensor(H[:, t, :], H[:, t, :], HN[:, t, :], ALU.add).then_inc(s["h_ready"], 1)

            def log1p(dst, e, t1, t2, t3):
                link(V_.tensor_scalar(t1, e, 2.0, None, ALU.add))
                link(V_.reciprocal(t2, t1))
                link(V_.tensor_tensor(t1, e, t2, ALU.mult))
                link(V_.tensor_tensor(t2, t1, t1, ALU.mult))
                link(V_.tensor_scalar(t3, t2, 1.0 / 15, None, ALU.mult))
                for k in (13, 11, 9, 7, 5, 3):
                    link(V_.scalar_tensor_tensor(t3, t3, 1.0 / k, t2, ALU.add, ALU.mult))
                link(V_.scalar_tensor_tensor(t3, t3, 1.0, t1, ALU.add, ALU.mult))
                link(V_.tensor_scalar(dst, t3, 2.0, None, ALU.mult))

            def flat_(ap):
                return ap.rearrange("p a b -> p (a b)")

            def even_mixer():
                link(V_.memset(XR[:, :, 0:4], 0.0))
                link(V_.tensor_scalar(flat_(Q), flat_(Q), 64 ** -0.5, None, ALU.mult))
                link(V_.tensor_copy(SPX[:, 0:4], colr("lam", 4)))
                for t in range(TT):
                    last = V_.tensor_tensor(SPX[:, 4 + 8 * t:12 + 8 * t], FL[:, t, :], FB[:, :], ALU.add)
                link(last)
                V_.scalar_tensor_tensor(SPN[:, :], SPX[:, :], -1.0, SPX[:, :], ALU.mult, ALU.min).then_inc(s["spx_ready"], 1)
                dve.wait_ge(s["spe_ready"], 1)
                log1p(SP[:, :], SPE[:, :], SPP[:, :], SPR[:, :], SPS[:, :])
                link(V_.tensor_scalar(SPX[:, :], SPX[:, :], -1.0, 0.0, ALU.mult, ALU.max))
                link(V_.tensor_tensor(SP[:, :], SP[:, :], SPX[:, :], ALU.add))
                link(V_.tensor_scalar(SPR[:, 0:4], SP[:, 0:4], -8.0, None, ALU.mult))
                link(V_.tensor_scalar(SPS[:, 0:4], SP[:, 0:4], 8.0, None, ALU.mult))
                V_.tensor_scalar(SP[:, 4:20], SP[:, 4:20], -1.0, None, ALU.mult).then_inc(s["small_ready"], 1)
                for j in range(4):
                    for i in range(4):
                        x = XR[:, i, 1 + j:1 + j + S]
                        w = col("conv_w", 4 * j + i)
                        if j == 0:
                            last = V_.tensor_scalar(XC[:, i, :], x, w, col("conv_b", i), ALU.mult, ALU.add)
                        else:
                            last = V_.scalar_tensor_tensor(XC[:, i, :], x, w, XC[:, i, :], ALU.mult, ALU.add)
                    if j < 3:
                        link(last)
                last.then_inc(s["conv_ready"], 1)
                dve.wait_ge(s["conv_ready"], 1)
                dve.wait_ge(s["cum_ready"], 1)
                V_.tensor_scalar(NCT[:, :], BANK[0][0:8, 0:S], -1.0, None, ALU.mult)
                V_.tensor_copy(CC[:, :, :], BANK[1][:, 0:16].rearrange("p (t h) -> p t h", t=TT))\
                    .then_inc(s["cumev_ready"], 1)
                dve.wait_ge(s["cumev_ready"], 1)

                dve.wait_ge(s["sig_ready"], 8)
                link(V_.tensor_tensor(flat_(IG), flat_(IG), flat_(XC), ALU.mult))
                dve.wait_ge(s["aexp_ready"], 8)
                link(V_.tensor_tensor(flat_(RG), flat_(AE), flat_(AE), ALU.mult))
                V_.scalar_tensor_tensor(flat_(TH), flat_(RG), 1.0, flat_(TH), ALU.add, ALU.mult)\
                    .then_inc(s["root_in"], 1)
                dve.wait_ge(s["root_ready"], 1)
                link(V_.tensor_tensor(flat_(IG), flat_(IG), flat_(TH), ALU.mult))
                for i in range(4):
                    last = V_.tensor_tensor_scan(XC[:, i, :], AE[:, i, :], IG[:, i, :], 0.0, ALU.mult, ALU.add)
                link(last)
                dve.wait_ge(s["gelu_ready"], 4)
                link(V_.tensor_tensor(flat_(YR), flat_(YR), flat_(XC), ALU.mult))
                split_x(YR[:, :, :], 0, 4, 4)

                def logits(u):
                    h, t = u // 2, u % 2
                    n = (t + 1) * P
                    dve.wait_ge(s["score_ready"], u + 1)
                    wait(dve, "prob_ready", u - 1)
                    link(V_.scalar_tensor_tensor(LG[:, u % 2, 0:n], BANK[2 + u % 2][:, 0:n], CC[:, t, h:h + 1],
                                                 CAUSAL[:, S - n:S], ALU.add, ALU.add))
                    V_.tensor_reduce(AMX[:, u:u + 1], LG[:, u % 2, 0:n], AX.X, ALU.max, negate=True)\
                        .then_inc(s["logit_ready"], 1)
                for u in range(17):
                    if u < 16:
                        logits(u)
                    if u:
                        v = u - 1
                        n = (v % 2 + 1) * P
                        dve.wait_ge(s["prob_ready"], v + 1)
                        link(V_.reciprocal(AREC[:, v:v + 1], ASUM[:, v:v + 1]))
                        V_.tensor_scalar(PR[:, v % 2, 0:n], PR[:, v % 2, 0:n], AREC[:, v:v + 1], None, ALU.mult)\
                            .then_inc(s["probn_ready"], 1)
                for p in range(4):
                    dve.wait_ge(s["pv_ready"], 4 * p + 4)
                    split_x(BANK[4 + p][:, 0:S], 4 + p, 5 + p, 1)
                dve.wait_ge(s["x_ready"], 16)
                mark("mixer_done")

            def odd_mixer():
                mark("lrk_ready")
                dve.wait_ge(s["lr_tp"], 1)
                V_.tensor_copy(LRT[:, :], BANK[2][0:16, 0:S]).then_inc(s["lrt_ready"], 1)
                dve.wait_ge(s["gate_mm"], 1)
                for i in range(4):
                    last = V_.tensor_scalar(GXX[:, i, :], BANK[4 + i // 2][:, (i % 2) * S:(i % 2 + 1) * S],
                                            col("gate_b", i), None, ALU.add)
                link(last)
                V_.scalar_tensor_tensor(flat_(GE), flat_(GXX), -1.0, flat_(GXX), ALU.mult, ALU.min).then_inc(s["nab_ready"], 1)
                dve.wait_ge(s["gexp_ready"], 1)
                V_.tensor_scalar(flat_(GE), flat_(GE), 1.0, None, ALU.add).then_inc(s["gexp1_ready"], 1)
                dve.wait_ge(s["gln_ready"], 1)
                link(V_.scalar_tensor_tensor(flat_(GE), flat_(GXX), 0.0, flat_(GE), ALU.min, ALU.subtract))
                link(V_.tensor_tensor_scan(flat_(BC_), RESET[:, :], flat_(GE), 0.0, ALU.mult, ALU.add))
                b16 = flat_(BC_).rearrange("p (c j) -> p c j", j=64)
                V_.tensor_tensor(flat_(GXX).rearrange("p (c j) -> p c j", j=64),
                                 b16[:, :, 63:64].broadcast_to([P, 16, 64]), b16, ALU.subtract)\
                    .then_inc(s["bcum_ready"], 1)
                dve.wait_ge(s["bexp_ready"], 3)
                link(V_.tensor_copy(SDEC[:, :, :], EB[:, :, 63:S:64]))
                V_.scalar_tensor_tensor(flat_(EB), flat_(OQ), P ** -0.5, flat_(EB), ALU.mult, ALU.mult)
                V_.tensor_tensor(flat_(ENB), flat_(OK), flat_(ENB), ALU.mult)
                V_.tensor_tensor(flat_(GXX), flat_(OK), flat_(GXX), ALU.mult).then_inc(s["kdec_ready"], 1)
                for t in range(TT):
                    dve.wait_ge(s["sct_mm"], t + 1)
                    V_.tensor_tensor(SCT[:, t, :].rearrange("p (h i) -> p h i", h=4),
                                     BANK[2 + t][:, :].rearrange("p (h i) -> p h i", h=4),
                                     bcast(UPPER64, 4),
                                     ALU.mult).then_inc(s["sct_ready"], 1)
                for n in range(3):
                    dve.wait_ge(s["upd_ready"], n + 1)
                    wait(dve, "state_ready", n)
                    for h in range(4):
                        ps = BANK[6 + h // 2][:, (h % 2) * 256:(h % 2 + 1) * 256]
                        if n == 0:
                            last = V_.tensor_copy(ST[:, h, :], ps)
                        else:
                            last = V_.scalar_tensor_tensor(ST[:, h, :], ST[:, h, :], SDEC[:, h, n:n + 1], ps,
                                                           ALU.mult, ALU.add)
                    last.then_inc(s["state_ready"], 1)
                dve.wait_ge(s["silug_ready"], 1)
                for t in range(TT):
                    dve.wait_ge(s["o_ssq"], 4 * (t + 1))
                    rsqrt(STAT[:, 24 + 4 * t:28 + 4 * t], STAT[:, 8 + 4 * t:12 + 4 * t], STAT[:, 54:58])
                    for h in range(4):
                        b = ((4, 5), (0, 1))[t][h // 2]
                        hs = slice(h * 256, (h + 1) * 256)
                        last = V_.scalar_tensor_tensor(OG[:, t, hs], BANK[b][:, (h % 2) * 256:(h % 2 + 1) * 256],
                                                       STAT[:, 24 + 4 * t + h:25 + 4 * t + h], OG[:, t, hs],
                                                       ALU.mult, ALU.mult)
                last.then_inc(s["og_ready"], 1)

            def router():
                dve.wait_ge(s["score_ready"], 17)
                link(V_.tensor_copy(flat_(LOGITS), BANK[2][:, 0:16]))
                for t in range(TT):
                    link(V_.max(GMAX[:, t, :], LOGITS[:, t, :]))
                    link(V_.max_index(GIDX[:, t, :], GMAX[:, t, :], LOGITS[:, t, :]))
                    link(V_.tensor_copy(GIF[:, t, :], GIDX[:, t, :]))
                    link(V_.tensor_scalar(EQ1[:, t, :], IOTA8[:, :], GIF[:, t, 0:1], None, ALU.is_equal))
                    link(V_.tensor_copy(GSM[:, t, 0:1], GMAX[:, t, 0:1]))
                    link(V_.scalar_tensor_tensor(LOGITS[:, t, :], EQ1[:, t, :], NEG, LOGITS[:, t, :],
                                                 ALU.mult, ALU.add))
                    link(V_.max(GMAX[:, t, :], LOGITS[:, t, :]))
                    link(V_.max_index(GIDX[:, t, :], GMAX[:, t, :], LOGITS[:, t, :]))
                    link(V_.tensor_copy(GIF[:, t, :], GIDX[:, t, :]))
                    link(V_.tensor_scalar(EQ2[:, t, :], IOTA8[:, :], GIF[:, t, 0:1], None, ALU.is_equal))
                    last = V_.tensor_tensor(GSM[:, t, 1:2], GMAX[:, t, 0:1], GSM[:, t, 0:1], ALU.subtract)
                last.then_inc(s["spx_ready"], 1)
                dve.wait_ge(s["spe_ready"], 2)
                link(V_.tensor_scalar(GSM[:, :, 3], GSM[:, :, 2], 1.0, None, ALU.add))
                link(V_.reciprocal(GSM[:, :, 4], GSM[:, :, 3]))
                link(V_.tensor_tensor(GSM[:, :, 5], GSM[:, :, 2], GSM[:, :, 4], ALU.mult))
                for t in range(TT):
                    link(V_.tensor_scalar(GATES[:, t, :], EQ1[:, t, :], GSM[:, t, 4:5], None, ALU.mult))
                    link(V_.scalar_tensor_tensor(GATES[:, t, :], EQ2[:, t, :], GSM[:, t, 5:6], GATES[:, t, :],
                                                 ALU.mult, ALU.add))
                for i in range(2 * NE + 1):
                    if i < 2 * NE:
                        wait(dve, "gate_mm", i) if i >= 2 else None
                        V_.tensor_scalar(SIL[:, i % 2, 0:P], IDENT[:, :], GATES[:, i % 2, i // 2:i // 2 + 1], None,
                                         ALU.mult).then_inc(s["gates_ready"], 1)
                    if i:
                        j = i - 1
                        dve.wait_ge(s["gate_mm"], 1 + i)
                        link(V_.tensor_copy(GATE_BC[:, j // 2, (j % 2) * P:(j % 2 + 1) * P], BANK[2 + j % 2][:, 0:P]))

            def bcast(t_, n):
                return t_[:, :].rearrange("p (a b) -> p a b", a=1).broadcast_to([P, n, P])

            def hybrid(l):
                R = range
                link(V_.memset(XA[:, :, 0:4], 0.0))
                link(V_.memset(PC[:, :, 0:4], 0.0))
                link(V_.memset(Z2[:, :, 0:32], 0.0))
                dve.wait_ge(s["up_in_ready"], 16 * 7 * (l + 1))
                mark("z_sig")
                mark("z_sig")
                mark("vn_ready")
                for t in R(TT):
                    link(V_.bn_stats(STAT[:, 44:50], VR[:, t, :]))
                    link(V_.bn_aggr(STAT[:, 50:52], STAT[:, 44:50]))
                    rsqrt(STAT[:, 52:53], STAT[:, 51:52], STAT[:, 54:55], eps=LN_EPS)
                    link(V_.tensor_scalar(VR[:, t, :], VR[:, t, :], STAT[:, 50:51], STAT[:, 52:53],
                                          ALU.subtract, ALU.mult))
                    link(V_.tensor_tensor(VR[:, t, :], VR[:, t, :], SGG[:, :], ALU.mult))
                    last = V_.tensor_tensor(VR[:, t, :], VR[:, t, :], SGBB[:, :], ALU.add)
                last.then_inc(s["vn_ready"], 1)
                dve.wait_ge(s["vn_ready"], 2 * l + 2)
                V_.memset(RHS[:, :, :], 0.0)
                V_.memset(SA[:, :, :], 0.0)
                dve.wait_ge(s["wt_tp"], l + 1)
                V_.tensor_tensor(WT[:, :, :], BANK[2][:, :].rearrange("p (h t) -> p h t", h=4), bcast(UPPER, 4),
                                 ALU.mult).then_inc(s["wt_ready"], 1)
                link(V_.tensor_tensor(XA[:, :, 4:S + 4], XA[:, :, 4:S + 4], GC[:, :, :], ALU.mult))
                for j in R(3):
                    for i in R(2):
                        x, w = XA[:, i, 2 + j:2 + j + S], col(f"sc_conv_w{l}", 2 * j + i)
                        if j == 0:
                            last = V_.tensor_scalar(GC[:, i, :], x, w, None, ALU.mult)
                        else:
                            last = V_.scalar_tensor_tensor(GC[:, i, :], x, w, GC[:, i, :], ALU.mult, ALU.add)
                    link(last)
                link(V_.tensor_tensor(flat_(GB), flat_(GB), flat_(GC), ALU.mult))
                split_x(GB[:, :, :], 0, 2)
                dve.wait_ge(s["sp_mm"], l + 1)
                link(V_.tensor_tensor(flat_(UU), flat_(UU), BANK[3][:, :], ALU.mult))
                split_x(UU[:, :, :], 2, 4)
                dve.wait_ge(s["zs_ready"], 3 * l + 1)
                link(V_.tensor_tensor(Z2[:, :, 32:S + 32], Z2[:, :, 32:S + 32], Z1[:, :, :], ALU.mult))
                for j in R(31):
                    for i in R(2):
                        x, w = Z2[:, i, 2 + j:2 + j + S], col(f"cm_conv_w{l}", 2 * j + i)
                        if j == 0:
                            last = V_.tensor_scalar(Z1[:, i, :], x, w, col(f"cm_conv_b{l}", i), ALU.mult, ALU.add)
                        else:
                            last = V_.scalar_tensor_tensor(Z1[:, i, :], x, w, Z1[:, i, :], ALU.mult, ALU.add)
                    if j < 30:
                        link(last)
                last.then_inc(s["zln_in"], 1)
                link(V_.tensor_tensor(CM[:, :, :], PC[:, :, 3:S + 3], PC[:, :, 4:S + 4], ALU.subtract))
                for i in (6, 0, 1, 2, 3, 4, 5):
                    ins = V_.scalar_tensor_tensor(CM[:, i, :], CM[:, i, :], col(f"rk_mu{l}", i), PC[:, i, 4:S + 4],
                                                  ALU.mult, ALU.add)
                    if i == 6:
                        ins.then_inc(s["pexp_in"], 1)
                link(ins)
                dve.wait_ge(s["zln_mm"], l + 1)
                for i in R(2):
                    last = V_.scalar_tensor_tensor(Z1[:, i, :], BANK[4][:, 0:S], -1.0 / 256, Z1[:, i, :],
                                                   ALU.mult, ALU.add)
                link(last)
                V_.tensor_tensor(Z2[:, :, 0:S], Z1[:, :, :], Z1[:, :, :], ALU.mult).then_inc(s["zc_in"], 1)
                dve.wait_ge(s["zv_mm"], l + 1)
                link(V_.tensor_copy(XA[:, 1, 0:S], BANK[5][:, 0:S]))
                rsqrt(XA[:, 0, 0:S], XA[:, 1, 0:S], GC[:, 0, :], mul=1.0 / 256, eps=LN_EPS)
                for i in R(2):
                    last = V_.tensor_tensor(Z1[:, i, :], Z1[:, i, :], XA[:, 0, 0:S], ALU.mult)
                last.then_inc(s["zn_ready"], 1)
                for i in R(2):
                    last = V_.tensor_scalar(KK[:, i, :], CM[:, 2 + i, :], col(f"rk_k_k{l}", i), None, ALU.mult)
                link(last)
                V_.tensor_tensor(flat_(KN), flat_(KK), flat_(KK), ALU.mult).then_inc(s["kk_in"], 1)
                dve.wait_ge(s["zs_ready"], 3 * l + 3)
                split_x(Z1[:, :, :], 6, 8)
                dve.wait_ge(s["nrm_mm"], l + 1)
                link(V_.tensor_copy(flat_(AH), BANK[3][:, :]))
                rsqrt(flat_(KN), flat_(AH), flat_(BH), eps=1e-24, floor=True)
                link(V_.tensor_tensor(flat_(KK), flat_(KK), flat_(KN), ALU.mult))
                dve.wait_ge(s["upsig_ready"], 5 * (l + 1))
                link(V_.tensor_tensor_scan(flat_(CB), RESET[:, 0:2 * S], flat_(SGW_), 0.0, ALU.mult, ALU.add))
                V_.tensor_tensor(flat_(PPV), flat_(CB), flat_(SGW_), ALU.subtract).then_inc(s["pexp_in"], 2)
                for i in R(2):
                    last = V_.tensor_scalar(KN[:, i, :], AV[:, i, :], 1.0, col(f"rk_k_a{l}", i), ALU.subtract, ALU.mult)
                link(last)
                link(V_.scalar_tensor_tensor(CM[:, 2:4, :], KN[:, :, :], 1.0, CM[:, 2:4, :], ALU.add, ALU.mult))
                for i in R(2):
                    last = V_.scalar_tensor_tensor(RB[:, i, :], CM[:, i, :], col(f"rk_r_k{l}", i), CM[:, 2 + i, :],
                                                   ALU.mult, ALU.mult)
                last.then_inc(s["bonus_in"], 1)
                dve.wait_ge(s["pexp_ready"], 3 * (l + 1))
                V_.scalar_tensor_tensor(flat_(AH), flat_(KK), -1.0, flat_(PPV), ALU.mult, ALU.mult)
                link(V_.tensor_tensor(flat_(BH), flat_(KK), flat_(AV), ALU.mult))
                V_.tensor_tensor(flat_(BH), flat_(BH), flat_(PIN), ALU.mult)
                V_.tensor_tensor(KH[:, :, :], CM[:, 2:4, :], PIN[:, :, :], ALU.mult)
                V_.tensor_tensor(RH[:, :, :], CM[:, 0:2, :], PP[:, :, :], ALU.mult)
                dve.wait_ge(s["bonus_mm"], l + 1)
                V_.tensor_tensor(KN[:, :, :], CM[:, 4:6, :], BANK[4][:, :].rearrange("p (a b) -> p a b", a=2),
                                 ALU.mult).then_inc(s["abkr_ready"], 1)
                dve.wait_ge(s["abkr_ready"], l + 1)
                for n in R(3):
                    for h in R(4):
                        V_.tensor_tensor(PPM[:, n, h, :], PP[:, h // 2, 64 * n + 63:64 * n + 64],
                                         BLOCK64[:, 64 * (h % 2):64 * (h % 2) + 1], ALU.mult)
                for t in R(TT):
                    last = V_.tensor_copy(XX[:, t, :].rearrange("p (h i) -> p h i", h=4), bcast(IDENT, 4))
                    last = V_.tensor_copy(XT[:, t, :].rearrange("p (h i) -> p h i", h=4), bcast(IDENT, 4))
                link(last)
                n = 0
                for dst, mask in ((LT, STRICT64), (PAIR[0], STRICT64), (PAIR[1], UPPER64), (PAIR[2], UPPER64)):
                    for par in R(2):
                        dve.wait_ge(s["pair_mm"], 8 * l + n + 1)
                        heads = dst.rearrange("p t (a b i) -> p (t a) b i", a=2, b=2)[:, :, par, :]
                        V_.tensor_tensor(heads, BANK[n % 2][:, :].rearrange("p (h i) -> p h i", h=4), bcast(mask, 4),
                                         ALU.mult).then_inc(s["pair_ready"], 1)
                        n += 1
                dve.wait_ge(s["pair_ready"], 8 * l + 8)
                for lv in R(7):
                    for t in R(TT):
                        if lv:
                            dve.wait_ge(s["xx_mm"], 12 * l + 2 * (lv - 1) + t + 1)
                            if lv < 6:
                                V_.tensor_tensor(XX[:, t, :], XX[:, t, :], BANK[3 + 3 * t][:, :], ALU.add)
                            V_.tensor_tensor(XT[:, t, :], XT[:, t, :], BANK[4 + 3 * t][:, :], ALU.add)\
                                .then_inc(s["xx_ready"], 1)
                        if lv < 6:
                            V_.tensor_tensor(LM[:, t, :].rearrange("p (h i) -> p h i", h=4),
                                             LT[:, t, :].rearrange("p (h i) -> p h i", h=4),
                                             LEVEL[:, lv:lv + 1, :].broadcast_to([P, 4, P]), ALU.mult)\
                                .then_inc(s["lvl_in"], 1)
                for n in R(3):
                    dve.wait_ge(s["sn_mm"], 3 * l + n + 1)
                    new, old = 4 * ((n + 1) % 2), 4 * (n % 2)
                    src = BANK[2][:, 0:256].rearrange("p (h i) -> p h i", h=4)
                    dst = ST2[:, new:new + 4, :]
                    if n:
                        link(V_.tensor_tensor(dst, ST2[:, old:old + 4, :], src, ALU.add))
                        src = dst
                    V_.tensor_tensor(dst, src, PPM[:, n, :, :].broadcast_to([P, 4, 64]), ALU.mult)\
                        .then_inc(s["sn_ready"], 1)
                    dve.wait_ge(s["sn_ready"], 3 * l + n + 1)
                dve.wait_ge(s["yc_mm"], 4 * (l + 1))
                V_.tensor_copy(flat_(AH), BANK[3][:, :]).then_inc(s["mean_in"], 1)
                dve.wait_ge(s["mean_mm"], l + 1)
                link(V_.scalar_tensor_tensor(flat_(AH), BANK[5][:, :], -1.0 / 64, flat_(AH), ALU.mult, ALU.add))
                V_.tensor_tensor(flat_(BH), flat_(AH), flat_(AH), ALU.mult).then_inc(s["var_in"], 1)
                dve.wait_ge(s["var_mm"], l + 1)
                link(V_.tensor_copy(flat_(KH), BANK[6][:, :]))
                rsqrt(flat_(RH), flat_(KH), flat_(BH), mul=1.0 / 64, eps=GN_EPS)
                link(V_.tensor_tensor(flat_(AH), flat_(AH), flat_(RH), ALU.mult))
                for i in R(2):
                    last = V_.tensor_scalar(AH[:, i, :], AH[:, i, :], col(f"rk_ln_w{l}", i), col(f"rk_ln_b{l}", i),
                                            ALU.mult, ALU.add)
                link(last)
                link(V_.tensor_tensor(flat_(AH), flat_(AH), flat_(KN), ALU.add))
                link(V_.tensor_tensor(flat_(AH), flat_(AH), flat_(GG), ALU.mult))
                split_x(AH[:, :, :], 4, 6, KT)
                dve.wait_ge(s["x_ready"], KT * (9 + 4 * l))
                mark("mixer_done")

            dve.wait_ge(s["x_loaded"], 16)
            norm()
            dve.wait_ge(s["loads_done"], 16 * N_LOADS)
            mark("rows_zero")
            dve.wait_ge(s["cols_tp"], 1)
            for t in range(3):
                last = V_.tensor_copy(COLS[:, t, :], BANK[t][:, 0:P])
            last.then_inc(s["cols_ready"], 1)
            dve.wait_ge(s["cols_ready"], 1)
            ahead(-1)
            gain("norm_mix0")
            project(EV_PROJ, ev_dest)
            even_mixer()
            output(EV_OUT)
            residual(EV_OUT)
            norm()
            gain("norm_ffn0")
            ffn(EV_FFN)
            residual(EV_FFN)
            norm()
            gain("norm_mix1")
            project(OD_PROJ, od_dest)
            odd_mixer()
            gain("head_norm")
            output(OD_OUT)
            residual(OD_OUT)
            norm()
            gain("norm_ffn1")
            router()
            ffn(MOE)
            residual(MOE)
            dve.wait_ge(s["ssq_ready"], nxt("ssq_ready", TT))
            gi = gains_wait()
            rsqrt(STAT[:, 2:4], STAT[:, 0:2], STAT[:, 54:56])
            for t in range(TT):
                V_.scalar_tensor_tensor(H[:, t, :], H[:, t, :], STAT[:, 2 + t:3 + t], GBC[:, gi, :], ALU.mult,
                                        ALU.mult).then_inc(s["h_ready"], 1)
            mark("gbc_used")
            mark("mixer_done")
            for l in range(2):
                f1, pr, ou, f2 = HY[l]
                norm()
                gain(f"ffn1_pre{l}")
                ffn(f1)
                post(0.5)
                norm()
                gain(f"mix_pre{l}")
                project(pr, hy_dest)
                hybrid(l)
                output(ou)
                post(1.0)
                norm()
                gain(f"ffn2_pre{l}")
                ffn(f2)
                post(0.5)


_INS = ['x', 'norm_mix', 'norm_ffn', 'norm_final', 'ev_w_in', 'ev_conv_w', 'ev_conv_b', 'ev_ga_w', 'ev_ga_b',
        'ev_gx_w', 'ev_gx_b', 'ev_lambda', 'ev_f_b', 'ev_w_out', 'ev_ffn_w1', 'ev_ffn_w3', 'ev_ffn_w2', 'od_w_in',
        'od_gate_w2', 'od_gate_b', 'od_head_norm', 'od_w_out', 'od_router', 'od_exp_w1', 'od_exp_w3', 'od_exp_w2',
        'ffn1_pre_g_2', 'ffn1_w_gate_2', 'ffn1_w_up_2', 'ffn1_w_down_2', 'ffn1_post_g_2', 'mix_pre_g_2', 'w_in_2',
        'sc_conv_w_2', 'sg_ln_w_2', 'sg_ln_b_2', 'sg_w_2', 'sg_b_2', 'rk_mu_2', 'rk_w0_2', 'rk_w_up_2', 'rk_a0_2',
        'rk_a_up_2', 'rk_g_up_2', 'rk_k_k_2', 'rk_k_a_2', 'rk_r_k_2', 'rk_ln_w_2', 'rk_ln_b_2', 'cm_conv_w_2',
        'cm_conv_b_2', 'cm_ln_w_2', 'cm_ln_b_2', 'w_out_2', 'mix_post_g_2', 'ffn2_pre_g_2', 'ffn2_w_gate_2',
        'ffn2_w_up_2', 'ffn2_w_down_2', 'ffn2_post_g_2']
_OUTS = [((1, S, D), 'float32')]


def kernel(**inputs):
    import numpy as _np
    import concourse.bacc as _bacc
    from concourse import mybir as _mybir
    from concourse.bass_utils import run_bass_kernel_spmd as _run

    nc = _bacc.Bacc("TRN2", target_bir_lowering=False, num_devices=1)
    arrays, args = {}, {}
    for name in _INS:
        a = _np.ascontiguousarray(inputs[name])
        arrays[f"in_{name}_dram"] = a
        args[name] = nc.dram_tensor(f"in_{name}_dram", a.shape, _mybir.dt.from_np(a.dtype), kind="ExternalInput").ap()
    outs = []
    for i, (shape, dtype) in enumerate(_OUTS):
        dt = _mybir.dt.from_np(_np.dtype(dtype))
        outs.append(nc.dram_tensor(f"out_{i}_dram", shape, dt, kind="ExternalOutput").ap())
    build(nc, args, outs[0])
    r = _run(nc, [arrays], core_ids=[0])
    got = tuple(r.results[0][f"out_{i}_dram"] for i in range(len(_OUTS)))
    return got[0]
```

```python
from contextlib import ExitStack

import concourse.bass as bass
from concourse import mybir

F32 = mybir.dt.float32
F32R = mybir.dt.float32r
ALU = mybir.AluOpType
ACT = mybir.ActivationFunctionType
AX = mybir.AxisListType

P = 128
S = 256
TT = S // P
D = 1024
KT = D // P
F_DENSE = 2816 // P
F_EXPERT = 3584 // P
NE = 8
RING = 6
LEAD = 3
EPS = 1e-6
LN_EPS = 1e-5
GN_EPS = 1e-5 * 64
DECAY_C = 0.6065306597126334
NEG = -1e30
ARENA_W = 19696

EV_COLS = [P] * 20 + [8]
OD_COLS = [P] * 24 + [16]
HY_COLS = [P] * 21


def build(nc, A, out):
    ctx = ExitStack()
    with ctx:
        ctx.enter_context(nc.allow_non_contiguous_dma(reason="small parameter rows"))

        def sb(name, shape, dt=F32):
            return ctx.enter_context(nc.sbuf_tensor(name, shape, dt))

        def sem(name):
            return ctx.enter_context(nc.semaphore(name))

        plan = []
        at = {"c": 0, "q": 0, "t": 0}

        def phase(kind, **kw):
            ph = dict(kind=kind, c0=at["c"], q0=at["q"], t0=at["t"], **kw)
            if kind == "proj":
                at["c"] += len(kw["cols"])
                at["q"] += len(kw["cols"])
            elif kind == "out":
                at["c"] += KT
            else:
                at["c"] += 3 * kw["tiles"]
                at["q"] += kw["tiles"]
                at["t"] += kw["tiles"]
            plan.append(ph)
            return ph

        EV_PROJ = phase("proj", w=A["ev_w_in"][0], cols=EV_COLS)
        EV_OUT = phase("out", w=A["ev_w_out"][0])
        EV_FFN = phase("ffn", tiles=F_DENSE, experts=1, w1=A["ev_ffn_w1"], w3=A["ev_ffn_w3"], w2=A["ev_ffn_w2"])
        OD_PROJ = phase("proj", w=A["od_w_in"][0], cols=OD_COLS)
        OD_OUT = phase("out", w=A["od_w_out"][0])
        MOE = phase("ffn", tiles=NE * F_EXPERT, experts=NE, w1=A["od_exp_w1"][0], w3=A["od_exp_w3"][0],
                    w2=A["od_exp_w2"][0])
        HY = []
        for l in range(2):
            f1 = phase("ffn", tiles=F_DENSE, experts=1, w1=A["ffn1_w_gate_2"][l:l + 1],
                       w3=A["ffn1_w_up_2"][l:l + 1], w2=A["ffn1_w_down_2"][l:l + 1])
            pr = phase("proj", w=A["w_in_2"][l], cols=HY_COLS)
            ou = phase("out", w=A["w_out_2"][l])
            f2 = phase("ffn", tiles=F_DENSE, experts=1, w1=A["ffn2_w_gate_2"][l:l + 1],
                       w3=A["ffn2_w_up_2"][l:l + 1], w2=A["ffn2_w_down_2"][l:l + 1])
            HY.append((f1, pr, ou, f2))
        N_CHUNKS = at["c"]
        width = {}
        for ph in plan:
            if ph["kind"] == "proj":
                for i, n in enumerate(ph["cols"]):
                    width[ph["c0"] + i] = KT * n

        RAW = sb("raw_ring", [P, RING, 1024])
        WHI = sb("whi_ring", [P, RING, 1024], F32R)
        WLO = sb("wlo_ring", [P, RING, 1024], F32R)
        XHI = sb("xhi", [P, KT, S], F32R)
        XLO = sb("xlo", [P, KT, S], F32R)
        H = sb("h", [P, TT, D])
        HID = sb("hid", [P, 2, S])
        HIDHI = sb("hidhi", [P, 2, S], F32R)
        HIDLO = sb("hidlo", [P, 2, S], F32R)
        SIL = sb("sil", [P, 2, S])
        IDENT = sb("ident", [P, P])
        ONES = sb("ones", [P, P])
        UPPER = sb("upper", [P, P])
        UPPER64 = sb("upper64", [P, P])
        STRICT64 = sb("strict64", [P, P])
        LEVEL = sb("level", [P, 6, P])
        BLOCK64 = sb("block64", [P, P])
        CAUSAL = sb("causal", [P, S])
        SEL = sb("sel", [8, 8, P])
        RESET = sb("reset", [P, 4 * S])
        IOTA = sb("iota", [P, P])
        ROWS = sb("rows", [P, 3, P])
        COLS = sb("cols", [P, 3, P])
        GBC = sb("gbc", [P, 2, D])
        STAT = sb("stat", [P, 84])
        ARENA = sb("arena", [P, ARENA_W])
        HN = ARENA[:, ARENA_W - 2 * D:].rearrange("p (t d) -> p t d", t=TT)

        class Carve:
            def __init__(self):
                self.at = 0

            def __call__(self, *dims, dt=F32, parts=P):
                n = 1
                for d_ in dims:
                    n *= d_
                ap = ARENA[0:parts, self.at:self.at + n]
                self.at += n
                assert self.at <= ARENA_W - 2 * D, self.at
                if len(dims) == 2:
                    ap = ap.rearrange("p (a b) -> p a b", a=dims[0])
                elif len(dims) == 3:
                    ap = ap.rearrange("p (a b c) -> p a b c", a=dims[0], b=dims[1])
                return ap

        BANK = [ctx.enter_context(nc.psum_tensor(f"bank{i}", [P, 512], F32)) for i in range(8)]
        OUTB = [BANK[2], BANK[3], BANK[6], BANK[7]]
        XGH = XHI[:, 0:4, :].rearrange("p a b -> p (a b)").rearrange("p (k n) -> p k n", k=KT)
        XGL = XLO[:, 0:4, :].rearrange("p a b -> p (a b)").rearrange("p (k n) -> p k n", k=KT)
        YB = [[BANK[4 + 2 * t + h] for h in range(2)] for t in range(TT)]

        names = """hi_ready lo_ready chunk_used bank_free silu_ready hid_made hid_gated hidhi_made
        hid_ready h_ready ssq_ready hn_ready tp_ready xhi_ready x_ready consts_ready cols_tp cols_ready
        loads_done gbc_used dve_order act_order pool_order x_loaded router_ready gates_ready rows_zero msk_ready pos_mm flag_ready hng_ready psel_ready pg_ready pgt_tp gath_mm xgh_ready xg_ready ye_act ye_ready outt_mm outt_ready outt_act outt_tp hidt_tp dense_order sparse_order out_tp zero_ready
        conv_ready gates_mm sig_ready aexp_ready gelu_ready root_in root_ready spx_ready spe_ready lrk_act small_ready cum_ready cumev_ready
        score_ready logit_ready prob_ready probn_ready probt_ready probt_copied pv_ready
        lr_tp lrt_ready gate_mm nab_ready gexp_ready gexp1_ready gln_ready bcum_ready bexp_ready kdec_ready kstp_ready
        ksr_ready sct_mm sct_ready upd_ready state_ready o_ready o_ssq og_ready silug_ready
        up_in_ready lrk_ready up_mm upsig_ready pexp_in pexp_ready kk_in nrm_mm abkr_ready rows_tp rows_ready
        pair_mm pair_ready lvl_in t1_mm t1_ready xx_mm xx_ready rhs_mm rhs_ready sa_mm sa_ready sn_mm sn_ready
        yc_mm mean_in mean_mm var_in var_mm bonus_in bonus_mm wt_tp wt_ready vn_ready sp_mm z_sig zln_in zln_mm
        zc_in zv_mm zn_ready zs_ready mixer_done fin_ready out_done""".split()
        s = {n: sem(n) for n in names}
        raw_full = [sem(f"raw_full{i}") for i in range(RING)]
        gbc_full = [sem(f"gbc_full{i}") for i in range(2)]

        row_at = {}
        row_loads = []
        fill = [0, 0, 0]

        def rows_of(name, src, tile):
            n = src.shape[0]
            row_at[name] = (tile, fill[tile])
            row_loads.append((ROWS[fill[tile]:fill[tile] + n, tile, :], src))
            fill[tile] += n
            assert fill[tile] <= P

        def vec(ap):
            return ap.rearrange("(k p) -> k p", p=P)

        for l in range(2):
            rows_of(f"norm_mix{l}", vec(A["norm_mix"][l]), 0)
            rows_of(f"norm_ffn{l}", vec(A["norm_ffn"][l]), 0)
            rows_of(f"ffn1_pre{l}", vec(A["ffn1_pre_g_2"][l]), 0)
            rows_of(f"mix_pre{l}", vec(A["mix_pre_g_2"][l]), 0)
            rows_of(f"ffn2_pre{l}", vec(A["ffn2_pre_g_2"][l]), 0)
        rows_of("head_norm", vec(A["od_head_norm"][0]), 0)
        rows_of("lam", vec(A["ev_lambda"][0]), 0)
        rows_of("conv_w", A["ev_conv_w"][0].rearrange("t (k p) -> (t k) p", p=P), 0)
        rows_of("conv_b", vec(A["ev_conv_b"][0]), 0)
        rows_of("ga_b", vec(A["ev_ga_b"][0]), 0)
        rows_of("gx_b", vec(A["ev_gx_b"][0]), 0)
        for l in range(2):
            for n, src in (("sc_conv_w", None), ("rk_mu", None), ("rk_w0", None), ("rk_a0", None), ("rk_k_k", None),
                           ("rk_k_a", None), ("rk_r_k", None), ("rk_ln_w", None), ("rk_ln_b", None),
                           ("cm_conv_w", None), ("cm_conv_b", None), ("cm_ln_w", None), ("cm_ln_b", None)):
                a = A[n + "_2"][l]
                if n in ("sc_conv_w", "cm_conv_w"):
                    a = a.rearrange("t (k p) -> (t k) p", p=P)
                elif n == "rk_r_k":
                    a = a.rearrange("(k x) d -> k (x d)", x=2)
                else:
                    a = vec(a)
                rows_of(f"{n}{l}", a, 1 + l)
        rows_of("gate_b", vec(A["od_gate_b"][0]), 1)

        def col(name, i=0):
            tile, r = row_at[name]
            return COLS[:, tile, r + i:r + i + 1]

        def colr(name, n):
            tile, r = row_at[name]
            return COLS[:, tile, r:r + n]

        c = Carve()
        GA, GX = c(4, P), c(4, P)
        FB = c(8)
        EV_KEEP = c.at
        XR = c(4, S + 4)
        YR, Q, K = c(4, S), c(4, S), c(4, S)
        V = c(2, 512)
        XC, RG, IG, AE, TH = c(4, S), c(4, S), c(4, S), c(4, S), c(4, S)
        FL = c(2, 8)
        SPX, SPE, SPN, SPR, SPS, SPP, SP = (c(20) for _ in range(7))
        NCT = c(S, parts=8)
        CC = c(2, 8)
        LG, PR = c(2, S), c(2, S)
        PT = c(2, 2, P)
        AMX, ASUM, AREC = c(16), c(16), c(16)
        c = Carve()
        GW2 = c(512, parts=16)
        RT = c(KT, NE)
        MOE_OVER = c.at
        OQ, OK, OV, OG = c(4, S), c(4, S), c(2, D), c(2, D)
        OLR = c(2, 16)
        LRT = c(S, parts=16)
        GXX, GE, BC_, EB, ENB = c(4, S), c(4, S), c(4, S), c(4, S), c(4, S)
        KSR = c(2, 512)
        SCT = c(2, 512)
        ST = c(4, 256)
        assert MOE_OVER + NE * S + 512 + TT * NE * P + 1024 + NE * S + D + KT * S <= c.at
        GATES = c(TT, NE)
        LOGITS, GMAX, EQ1, EQ2 = c(TT, NE), c(TT, NE), c(TT, NE), c(TT, NE)
        GIDX = c(TT, NE).bitcast(mybir.dt.uint32)
        GIF = c(TT, NE)
        GSM = c(TT, 8)
        SDEC = c(4, 4)
        MSK, POS = c(TT, NE), c(TT, NE)
        FLAG = c(8)
        FLAG_I = FLAG[0:1, 0:1].bitcast(mybir.dt.int32)
        c.at = MOE_OVER
        GATE_BC = c(NE, S)
        ZERO = c(512)
        PSEL = c(TT * NE, P)
        PG = c(2, 512)
        PGT = c(NE, S)
        YE = c(D)
        OUTT = c(KT, S)
        c = Carve()
        UPW = c(256)
        SGW = c(4, P)
        SGB = c(P, parts=4)
        SGG, SGBB = c(256), c(256)
        HY_EARLY = c.at
        GB, GC, XA = c(2, S), c(2, S), c(2, S + 4)
        UU, VR = c(2, S), c(2, S)
        PC = c(7, S + 4)
        Z1, Z2 = c(2, S), c(2, S + 32)
        HY_EARLY_END = c.at
        CM = c(7, S)
        LRK = c(S)
        HY_DEC = c.at
        SGW_, CB, PPV, PIN, KK = c(2, S), c(2, S), c(2, S), c(2, S), c(2, S)
        AV, GG, PP = c(2, S), c(2, S), c(2, S)
        AH, BH, KH, RH, KN = c(2, S), c(2, S), c(2, S), c(2, S), c(2, S)
        RB, RK, RV = c(2, 256), c(2, 256), c(2, 256)
        RHS = SGG.rearrange("p (h i) -> p h i", h=4)
        SA = SGBB.rearrange("p (h i) -> p h i", h=4)
        ST2 = c(8, 64)
        PPM = c(12, 1).rearrange("p (n h) a -> p n h a", n=3)
        WT = KN.rearrange("p a b -> p (a b)").rearrange("p (h t) -> p h t", h=4)
        c.at = HY_EARLY
        PAIR = [c(2, 512) for _ in range(3)]
        LT, XX = c(2, 512), c(2, 512)
        assert c.at <= HY_EARLY_END
        c.at = HY_DEC
        XT, LM, T1 = c(2, 512), c(2, 512), c(512)

        block = ctx.enter_context(nc.Block())

        def order(eng, name):
            n = [0]

            def link(ins):
                n[0] += 1
                ins.then_inc(s[name], 1)
                eng.wait_ge(s[name], n[0])
            return link

        def wait(eng, name, n):
            if not isinstance(n, int) or n > 0:
                eng.wait_ge(s[name], n)

        @block.sync
        def _(sp):
            def load(c_, slot, src):
                if not isinstance(c_, int) or c_ >= RING:
                    sp.wait_ge(s["lo_ready"], c_ - RING + 1)
                sp.dma_start(RAW[:, slot, :].rearrange("p (k n) -> p k n", k=src.shape[1]) if src.shape[1] * src.shape[2] == 1024
                             else RAW[:, slot, 0:src.shape[1] * src.shape[2]].rearrange("p (k n) -> p k n", k=src.shape[1]),
                             src).then_inc(raw_full[slot], 16)

            def columns(w, at_, n):
                return w[:, bass.ds(at_, n)].rearrange("(k p) n -> p k n", p=P)

            def rows(w, at_):
                return w[bass.ds(at_, P), :].rearrange("p (k n) -> p k n", k=1)

            for ph in plan:
                c0 = ph["c0"]
                if ph["kind"] == "proj":
                    x = 0
                    for i, n in enumerate(ph["cols"]):
                        load(c0 + i, (c0 + i) % RING, columns(ph["w"], x, n))
                        x += n
                elif ph["kind"] == "out":
                    for i in range(KT):
                        load(c0 + i, (c0 + i) % RING, rows(ph["w"], i * P))
                else:
                    F = ph["tiles"] // ph["experts"]
                    w1, w3 = ph["w1"].rearrange("e k n -> e k n"), ph["w3"]
                    w2 = ph["w2"].rearrange("e f n -> (e f) n")

                    def w13(e, j, c_, slot):
                        for w in (w1, w3):
                            if isinstance(e, int):
                                src = columns(w[e], j * P, P)
                            else:
                                src = columns(w[bass.ds(e, 1)].rearrange("e k n -> (e k) n"), j * P, P)
                            load(c_, slot % RING, src)
                            c_, slot = c_ + 1, slot + 1

                    def expert(e, c_):
                        n = F * e
                        w13(e, 0, c_, c0)
                        w13(e, 1, c_ + 2, c0 + 2)
                        load(c_ + 4, (c0 + 4) % RING, rows(w2, n * P))
                        with sp.Fori(1, F // 2) as i:
                            b = c_ + 6 * i - 1
                            w13(e, 2 * i, b, c0 + 5)
                            load(b + 2, (c0 + 7) % RING, rows(w2, (n + 2 * i - 1) * P))
                            w13(e, 2 * i + 1, b + 3, c0 + 8)
                            load(b + 5, (c0 + 10) % RING, rows(w2, (n + 2 * i) * P))
                        load(c_ + 3 * F - 1, (c0 + 3 * F - 1) % RING, rows(w2, (n + F - 1) * P))
                    expert(0, c0)
                    if ph["experts"] > 1:
                        with sp.Fori(1, ph["experts"]) as e:
                            expert(e, c0 + 3 * F * e)
            sp.wait_ge(s["h_ready"], 2 * 11)
            sp.dma_start(out[0].rearrange("(t p) d -> p t d", p=P), H[:, :, :]).then_inc(s["out_done"], 16)
            sp.wait_ge(s["out_done"], 16)

        gbc_list = [A["norm_ffn"][1], A["norm_final"]]
        for l in range(2):
            gbc_list += [A["ffn1_post_g_2"][l], A["mix_post_g_2"][l], A["ffn2_post_g_2"][l]]
        N_LOADS = len(row_loads) + 16 + 1

        @block.gpsimd
        def _(pool):
            link = order(pool, "pool_order")
            pool.dma_start(H[:, :, :], A["x"][0].rearrange("(t p) d -> p t d", p=P)).then_inc(s["x_loaded"], 16)
            link(nc.gpsimd.memset(ROWS[:, :, :], 0.0))
            for dst, src in row_loads:
                pool.dma_start(dst, src).then_inc(s["loads_done"], 16)
            link(nc.gpsimd.memset(GA[:, :, :], 0.0))
            link(nc.gpsimd.memset(GX[:, :, :], 0.0))
            for dst, src in ((GA, A["ev_ga_w"]), (GX, A["ev_gx_w"])):
                for n in range(8):
                    o = 64 * (n % 2)
                    pool.dma_start(dst[o:o + 64, n // 2, o:o + 64], src[0, n]).then_inc(s["loads_done"], 16)
            pool.dma_start(FB[:, :], A["ev_f_b"].broadcast_to([P, 8])).then_inc(s["loads_done"], 16)

            def select(t, op, fill_, pattern, base, cm):
                link(nc.gpsimd.affine_select(out=t, in_=t, compare_op=op, fill=fill_, base=base, pattern=pattern,
                                             channel_multiplier=cm))
            link(nc.gpsimd.memset(IDENT[:, :], 0.0))
            link(nc.gpsimd.memset(ONES[:, :], 1.0))
            link(nc.gpsimd.memset(UPPER[:, :], 1.0))
            link(nc.gpsimd.memset(BLOCK64[:, :], 0.0))
            link(nc.gpsimd.memset(BLOCK64[0:64, 0:64], 1.0))
            link(nc.gpsimd.memset(BLOCK64[64:128, 64:128], 1.0))
            link(nc.gpsimd.memset(CAUSAL[:, :], 0.0))
            link(nc.gpsimd.memset(SEL[:, :, :], 1.0))
            link(nc.gpsimd.memset(RESET[:, :], 1.0))
            link(nc.gpsimd.memset(RESET[:, 0:4 * S:64], 0.0))
            link(nc.gpsimd.memset(LEVEL[:, :, :], 1.0))
            select(IDENT[:, :], ALU.not_equal, 1.0, [[-1, P]], 0, 1)
            select(UPPER[:, :], ALU.is_ge, 0.0, [[1, P]], 0, -1)
            link(nc.gpsimd.tensor_tensor(UPPER64[:, :], UPPER[:, :], BLOCK64[:, :], ALU.mult))
            link(nc.gpsimd.tensor_tensor(STRICT64[:, :], UPPER64[:, :], IDENT[:, :], ALU.subtract))
            select(CAUSAL[:, P:2 * P], ALU.is_ge, NEG, [[-1, P]], 0, 1)
            select(SEL[:, :, :], ALU.is_equal, 0.0, [[1, 8], [0, P]], 0, -1)
            for lv in range(6):
                half = 1 << lv
                nb = P // (2 * half)
                view = LEVEL[:, lv, :].rearrange("p (b o x) -> p b o x", b=nb, o=2)
                link(nc.gpsimd.memset(view[:, :, 0, :], 0.0))
                part = view[:, :, 1, :]
                select(part, ALU.is_ge, 0.0, [[-2 * half, nb], [0, half]], 0, 1)
                select(part, ALU.is_ge, 0.0, [[2 * half, nb], [0, half]], half - 1, -1)
            nc.gpsimd.iota(IOTA[:, :], [[1, P]], base=0, channel_multiplier=0,
                           allow_small_or_imprecise_dtypes=True).then_inc(s["consts_ready"], 1)
            for i, g in enumerate(gbc_list):
                if i >= 2:
                    pool.wait_ge(s["gbc_used"], i - 1)
                pool.dma_start(GBC[:, i % 2, :], g.rearrange("(a n) -> a n", a=1).broadcast_to([P, D]))\
                    .then_inc(gbc_full[i % 2], 16)
                if i == 0:
                    pool.wait_ge(s["mixer_done"], 1)
                    pool.dma_start(GW2[:, :], A["od_gate_w2"][0]).then_inc(s["router_ready"], 16)
                    pool.dma_start(RT[:, :, :], A["od_router"][0].rearrange("(k p) e -> p k e", p=P))\
                        .then_inc(s["router_ready"], 16)
                if i in (2, 5):
                    l = (i - 2) // 3
                    pool.wait_ge(s["mixer_done"], 2 + l)
                    for dst, src in ((UPW[0:32, :], A["rk_w_up_2"][l]), (UPW[32:64, :], A["rk_a_up_2"][l]),
                                     (UPW[64:128, :], A["rk_g_up_2"][l]),
                                     (SGW[:, :, :], A["sg_w_2"][l].rearrange("h t s -> t h s")),
                                     (SGB[:, :], A["sg_b_2"][l]),
                                     (SGG[:, :], A["sg_ln_w_2"][l:l + 1, :].broadcast_to([P, 256])),
                                     (SGBB[:, :], A["sg_ln_b_2"][l:l + 1, :].broadcast_to([P, 256]))):
                        pool.dma_start(dst, src).then_inc(s["up_in_ready"], 16)

        def ev_dest(i):
            t, o = i // 4, i % 4
            if t == 0:
                return XR[:, o, 4:S + 4], False
            if t < 4:
                return (None, YR, Q, K)[t][:, o, :], False
            return (V[:, :, o * P:(o + 1) * P] if t == 4 else FL[:, :, :]), True

        def od_dest(i):
            if i < 8:
                return (OQ, OK)[i // 4][:, i % 4, :], False
            if i < 24:
                o = (i - 8) % 8
                return (OV, OG)[(i - 8) // 8][:, :, o * P:(o + 1) * P], True
            return OLR[:, :, :], True

        def hy_dest(i):
            if i < 6:
                return (GB, GC, XA)[i // 2][:, i % 2, 0:S] if i < 4 else XA[:, i % 2, 4:S + 4], False
            if i < 8:
                return UU[:, i % 2, :], False
            if i < 10:
                return VR[:, :, (i - 8) * P:(i - 7) * P], True
            if i < 17:
                return PC[:, i - 10, 4:S + 4], False
            return (Z1[:, i - 17, :] if i < 19 else Z2[:, i - 19, 32:S + 32]), False

        def counter():
            n = {}

            def nxt(name, by=1):
                n[name] = n.get(name, 0) + by
                return n[name]
            return nxt

        def last_chunk(ph):
            return ph["c0"] + (KT if ph["kind"] == "out" else 3 * ph["tiles"]) - 1

        def words(c_):
            return width.get(c_, 1024) if isinstance(c_, int) else 1024

        @block.tensor
        def _(pe):
            nxt = counter()
            mm = nc.tensor.matmul
            tr = nc.tensor.transpose

            def wslot(slot, k):
                return (WHI[:, slot, :].rearrange("p (k n) -> p k n", k=k),
                        WLO[:, slot, :].rearrange("p (k n) -> p k n", k=k))

            def narrow(slot, n):
                return (WHI[:, slot, 0:KT * n].rearrange("p (k n) -> p k n", k=KT),
                        WLO[:, slot, 0:KT * n].rearrange("p (k n) -> p k n", k=KT))

            def x_wait(first, kt):
                if first:
                    pe.wait_ge(s["x_ready"], nxt("x_ready"))

            def project(ph, dest):
                for i, n in enumerate(ph["cols"]):
                    c_, q = ph["c0"] + i, ph["q0"] + i
                    wait(pe, "lo_ready", c_ + 1)
                    wait(pe, "bank_free", q - 1)
                    wh, wl = narrow(c_ % RING, n)
                    bank = BANK[q % 2]
                    row = dest(i)[1]
                    for t in range(TT if row else 1):
                        for kt in range(KT):
                            if t == 0:
                                x_wait(i == 0, kt)
                            for a, (w, x) in enumerate(((wh, XHI), (wh, XLO), (wl, XHI))):
                                st, sp_ = (kt == 0 and a == 0), (kt == KT - 1 and a == 2)
                                if row:
                                    last = mm(bank[:, t * n:(t + 1) * n], x[:, kt, t * P:(t + 1) * P], w[:, kt, :],
                                              start=st, stop=sp_)
                                else:
                                    last = mm(bank[:, 0:S], w[:, kt, :], x[:, kt, :], start=st, stop=sp_)
                    last.then_inc(s["chunk_used"], 1)

            def output(ph):
                for kt in range(KT):
                    c_ = ph["c0"] + kt
                    wait(pe, "lo_ready", c_ + 1)
                    if kt == 0:
                        pe.wait_ge(s["x_ready"], nxt("x_ready", KT))
                    wh, wl = WHI[:, c_ % RING, :], WLO[:, c_ % RING, :]
                    for t in range(TT):
                        for a, (x, w) in enumerate(((XHI, wh), (XHI, wl), (XLO, wh))):
                            for h in range(2):
                                last = mm(YB[t][h][:, :], x[:, kt, t * P:(t + 1) * P], w[:, h * 512:(h + 1) * 512],
                                          start=(kt == 0 and a == 0), stop=(kt == KT - 1 and a == 2))
                    last.then_inc(s["chunk_used"], 1)

            def up(c_, slot, q, qb, first, n):
                wait(pe, "bank_free", q - 1)
                for half in range(2):
                    wait(pe, "lo_ready", c_ + half + 1)
                    wh, wl = wslot((slot + half) % RING, KT)
                    for kt in range(KT):
                        if first and half == 0:
                            pe.wait_ge(s["x_ready"], nxt("x_ready"))
                        xh, xl = XHI[:, kt, :], XLO[:, kt, :]
                        for a, (w, x) in enumerate(((wh, xh), (wh, xl), (wl, xh))):
                            last = mm(BANK[qb][:, half * S:half * S + n], w[:, kt, :], x,
                                      start=(kt == 0 and a == 0), stop=(kt == KT - 1 and a == 2))
                    last.then_inc(s["chunk_used"], 1)

            def down(c_, slot, t_, b, banks, start=False, stop=False):
                wait(pe, "lo_ready", c_ + 1)
                wait(pe, "hid_ready", t_ + 1)
                wh, wl = WHI[:, slot % RING, :], WLO[:, slot % RING, :]
                for t, pair in enumerate(banks):
                    for a, (x, w) in enumerate(((HIDHI, wh), (HIDHI, wl), (HIDLO, wh))):
                        for h in range(2):
                            last = mm(pair[h][:, :], x[:, b, t * P:(t + 1) * P], w[:, h * 512:(h + 1) * 512],
                                      start=(start and a == 0), stop=(stop and a == 2), skip_group_check=True)
                last.then_inc(s["chunk_used"], 1)

            def ffn(ph, m=0, T=None, first=True, n=S, banks=YB, start=True):
                T = T or ph["tiles"]
                cs, qs, ts = ph["c0"], ph["q0"], ph["t0"]
                c_, q, t_ = cs + 6 * m, qs + 2 * m, ts + 2 * m
                up(c_, cs, q, qs % 2, first, n)
                up(c_ + 2, cs + 2, q + 1, (qs + 1) % 2, False, n)
                down(c_ + 4, cs + 4, t_, ts % 2, banks, start=start)
                with pe.Fori(0, T // 2 - 1) as i:
                    c_, q, t_ = cs + 6 * m + 6 * i, qs + 2 * m + 2 * i, ts + 2 * m + 2 * i
                    up(c_ + 5, cs + 5, q + 2, qs % 2, False, n)
                    down(c_ + 7, cs + 7, t_ + 1, (ts + 1) % 2, banks)
                    up(c_ + 8, cs + 8, q + 3, (qs + 1) % 2, False, n)
                    down(c_ + 10, cs + 10, t_ + 2, ts % 2, banks)
                c_, t_ = cs + 6 * m, ts + 2 * m
                down(c_ + 3 * T - 1, cs + 3 * T - 1, t_ + T - 1, (ts + T - 1) % 2, banks, stop=True)

            def moe_dense():
                for e in range(NE):
                    for t in range(TT):
                        i = 2 * e + t
                        pe.wait_ge(s["gates_ready"], i + 1)
                        mm(BANK[2 + i % 2][:, 0:P], ONES[:, :], SIL[:, i % 2, 0:P], start=True, stop=True)\
                            .then_inc(s["gate_mm"], 1)
                pe.wait_ge(s["zero_ready"], 1)
                for t in range(TT):
                    for h in range(2):
                        mm(YB[t][h][:, :], ONES[:, :], ZERO[:, :], start=True, stop=True, skip_group_check=True)
                with pe.Fori(0, NE) as e:
                    ffn(MOE, F_EXPERT // 2 * e, F_EXPERT, first=False, start=False)

            def gather(e, half):
                for j in range(4):
                    kt = 4 * half + j
                    for t in range(TT):
                        last = mm(BANK[half][:, j * P:(j + 1) * P], HN[:, t, kt * P:(kt + 1) * P],
                                  PSEL[:, bass.ds(NE * t + e, 1), :].rearrange("p a b -> p (a b)"),
                                  start=(t == 0), stop=(t == TT - 1))
                last.then_inc(s["gath_mm"], 1)

            def up_slots(c_, slot, t_, qb, half):
                if half == 0:
                    pe.wait_ge(s["hid_ready"], t_ - 1)
                    pe.wait_ge(s["lo_ready"], c_ + 2)
                slot = slot % RING
                for kt in range(4 * half, 4 * half + 4):
                    wh, wl = (w[:, slot:slot + 2, kt * P:(kt + 1) * P] for w in (WHI, WLO))
                    for a, (x, w) in enumerate(((XGH, wh), (XGH, wl), (XGL, wh))):
                        last = mm(BANK[qb][:, 0:2 * P], x[:, kt, :], w,
                                  start=(kt == 0 and a == 0), stop=(kt == KT - 1 and a == 2))
                if half:
                    last.then_inc(s["chunk_used"], 2)

            def turn_hidden(q, qb, b):
                pe.wait_ge(s["bank_free"], q + 1)
                tr(BANK[qb][:, 2 * P:3 * P], HID[:, b, 0:P], IDENT[:, :]).then_inc(s["hidt_tp"], 1)

            def combine(e):
                pe.wait_ge(s["ye_act"], e + 1)
                pe.wait_ge(s["ye_ready"], e + 1)
                for k in range(KT):
                    last = mm(OUTB[k // 2][:, (k % 2) * S:(k % 2 + 1) * S], YE[:, k * P:(k + 1) * P],
                              PGT[:, bass.ds(e, 1), :].rearrange("p a b -> p (a b)"), start=False, stop=True,
                              skip_group_check=True)
                return last

            def moe_sparse():
                pe.wait_ge(s["hng_ready"], 1)
                pe.wait_ge(s["psel_ready"], 1)
                gather(0, 0)
                for g in range(4):
                    pe.wait_ge(s["pg_ready"], g + 1)
                    for j in range(4):
                        last = tr(BANK[2 + g % 2][:, j * P:(j + 1) * P], PG[:, g % 2, j * P:(j + 1) * P], IDENT[:, :])
                    last.then_inc(s["pgt_tp"], 1)
                gather(0, 1)
                pe.wait_ge(s["zero_ready"], 1)
                for b in range(4):
                    mm(OUTB[b][:, :], ONES[:, :], ZERO[:, :], start=True, stop=True, skip_group_check=True)
                cs, qs, ts, F = MOE["c0"], MOE["q0"], MOE["t0"], F_EXPERT

                def step(m, j, up_next=True, start=False, stop=False):
                    c_, t_ = 3 * F * m[0] + 6 * m[1], F * m[0] + 2 * m[1]
                    q0, b0 = (qs + j) % 2, (ts + j) % 2
                    if up_next:
                        up_slots(cs + c_ + 3 * j + 2, cs + 3 * j + 2, ts + t_ + j + 1, (qs + j + 1) % 2, 0)
                    turn_hidden(qs + t_ + j, q0, b0)
                    if up_next:
                        up_slots(cs + c_ + 3 * j + 2, cs + 3 * j + 2, ts + t_ + j + 1, (qs + j + 1) % 2, 1)
                        down(cs + c_ + 3 * j + 4, cs + 3 * j + 4, ts + t_ + j, b0, [YB[0]], start=start)

                def expert(e, more):
                    pe.wait_ge(s["xg_ready"], 2 * e + 2)
                    for half in range(2):
                        up_slots(cs + 3 * F * e, cs, ts + F * e, qs % 2, half)
                    step((e, 0), 0, start=True)
                    with pe.Fori(0, F // 2 - 1) as i:
                        step((e, i), 1)
                        step((e, i), 2)
                    step((e, 0), F - 1, up_next=False)
                    if more:
                        pe.wait_ge(s["hid_ready"], ts + F + F * e)
                        gather(e + 1, 0)
                    down(cs + 3 * F * e + 3 * F - 1, cs + 3 * F - 1, ts + F * e + F - 1, (ts + F - 1) % 2, [YB[0]],
                         stop=True)
                    if more:
                        gather(e + 1, 1)
                    return combine(e)
                with pe.Fori(0, NE - 1) as e:
                    expert(e, True)
                expert(NE - 1, False).then_inc(s["outt_mm"], 1)
                pe.wait_ge(s["outt_ready"], 4)
                for b in range(4):
                    for j in range(4):
                        k, t = 2 * b + j // 2, j % 2
                        last = tr(YB[t][k // 4][:, (k % 4) * P:(k % 4 + 1) * P], OUTT[:, k, t * P:(t + 1) * P],
                                  IDENT[:, :])
                last.then_inc(s["outt_tp"], 1)

            def turn(src, src_ready, row=False):
                pe.wait_ge(s[src_ready], nxt(src_ready))
                for b in range(4):
                    for j in range(2):
                        for t in range(TT):
                            kt = 2 * b + j
                            last = tr(BANK[4 + b][:, (2 * j + t) * P:(2 * j + t + 1) * P],
                                      src[:, t, kt * P:(kt + 1) * P], IDENT[:, :])
                    last.then_inc(s["tp_ready"], 1)

            def even_mixer():
                pe.wait_ge(s["conv_ready"], 1)
                for w, b in ((GA, 4), (GX, 6)):
                    for i in range(4):
                        last = mm(BANK[b + i // 2][:, (i % 2) * S:(i % 2 + 1) * S], w[:, i, :], XC[:, i, :],
                                  start=True, stop=True)
                last.then_inc(s["gates_mm"], 1)
                pe.wait_ge(s["small_ready"], 1)
                lf = SP[:, 4:20].rearrange("p (t h) -> p t h", t=TT)
                mm(BANK[0][0:8, 0:P], lf[:, 0, :], UPPER[:, :], start=True, stop=True)
                mm(BANK[0][0:8, P:S], lf[:, 0, :], ONES[:, :], start=True, stop=False)
                mm(BANK[0][0:8, P:S], lf[:, 1, :], UPPER[:, :], start=False, stop=True)
                mm(BANK[1][:, 0:8], UPPER[:, :], lf[:, 0, :], start=True, stop=True)
                mm(BANK[1][:, 8:16], ONES[:, :], lf[:, 0, :], start=True, stop=False)
                mm(BANK[1][:, 8:16], UPPER[:, :], lf[:, 1, :], start=False, stop=True).then_inc(s["cum_ready"], 1)
                pe.wait_ge(s["cumev_ready"], 1)

                def scores(u):
                    h, t = u // 2, u % 2
                    o, n = 64 * (h % 2), (t + 1) * P
                    wait(pe, "logit_ready", u - 1)
                    mm(BANK[2 + u % 2][:, 0:n], Q[o:o + 64, h // 2, t * P:(t + 1) * P], K[o:o + 64, h // 2, 0:n],
                       start=True, stop=False)
                    mm(BANK[2 + u % 2][:, 0:n], SEL[:, h, :], NCT[:, 0:n], start=False, stop=True)\
                        .then_inc(s["score_ready"], 1)
                scores(0)
                scores(1)
                pe.wait_ge(s["sig_ready"], 8)
                for u in range(16):
                    h, t = u // 2, u % 2
                    o = 64 * (h % 2)
                    pe.wait_ge(s["probn_ready"], u + 1)
                    wait(pe, "probt_copied", u - 1)
                    for b in range(t + 1):
                        last = tr(BANK[u % 2][:, b * P:(b + 1) * P], PR[:, u % 2, b * P:(b + 1) * P], IDENT[:, :])
                    last.then_inc(s["probt_ready"], 1)
                    if u + 2 < 16:
                        scores(u + 2)
                    pe.wait_ge(s["probt_copied"], u + 1)
                    for b in range(t + 1):
                        last = mm(BANK[4 + h // 2][o:o + 64, t * P:(t + 1) * P], V[:, b, h * 64:(h + 1) * 64],
                                  PT[:, u % 2, b, :], start=(b == 0), stop=(b == t))
                    last.then_inc(s["pv_ready"], 1)

            def odd_mixer():
                pe.wait_ge(s["lrk_ready"], 1)
                for t in range(TT):
                    last = tr(BANK[2][0:16, t * P:(t + 1) * P], OLR[:, t, :], IDENT[:, :])
                last.then_inc(s["lr_tp"], 1)
                pe.wait_ge(s["lrt_ready"], 1)
                pe.wait_ge(s["router_ready"], 32)
                for i in range(4):
                    last = mm(BANK[4 + i // 2][:, (i % 2) * S:(i % 2 + 1) * S], GW2[:, i * P:(i + 1) * P], LRT[:, :],
                              start=True, stop=True)
                last.then_inc(s["gate_mm"], 1)
                pe.wait_ge(s["kdec_ready"], 1)
                for t in range(TT):
                    for h in range(4):
                        last = tr(BANK[6 + t][:, h * P:(h + 1) * P], GXX[:, h, t * P:(t + 1) * P], IDENT[:, :])
                last.then_inc(s["kstp_ready"], 1)
                for t in range(TT):
                    for h in range(4):
                        last = mm(BANK[2 + t][:, h * P:(h + 1) * P], ENB[:, h, t * P:(t + 1) * P],
                                  EB[:, h, t * P:(t + 1) * P], start=True, stop=True)
                    last.then_inc(s["sct_mm"], 1)
                OB = [[BANK[4], BANK[5]], [BANK[0], BANK[1]]]
                pe.wait_ge(s["ksr_ready"], 1)
                for n in range(4):
                    t, o = n // 2, 64 * (n % 2)
                    if n % 2 == 0:
                        pe.wait_ge(s["sct_ready"], t + 1)
                        for h in range(4):
                            mm(OB[t][h // 2][:, (h % 2) * 256:(h % 2 + 1) * 256], SCT[:, t, h * P:(h + 1) * P],
                               OV[:, t, h * 256:(h + 1) * 256], start=(h % 2 == 0), stop=True, skip_group_check=True)
                    if n:
                        pe.wait_ge(s["state_ready"], n)
                    for h in range(4):
                        if n:
                            last = mm(OB[t][h // 2][o:o + 64, (h % 2) * 256:(h % 2 + 1) * 256],
                                      EB[:, h, n * 64:(n + 1) * 64], ST[:, h, :], start=False, stop=True,
                                      skip_group_check=True)
                        if n < 3:
                            upd = mm(BANK[6 + h // 2][:, (h % 2) * 256:(h % 2 + 1) * 256],
                                     KSR[o:o + 64, t, h * P:(h + 1) * P], OV[o:o + 64, t, h * 256:(h + 1) * 256],
                                     start=True, stop=True)
                    if n < 3:
                        upd.then_inc(s["upd_ready"], 1)
                    else:
                        last.then_inc(s["o_ready"], 1)

            def router():
                pe.wait_ge(s["x_ready"], KT * 6)
                for t in range(TT):
                    for kt in range(KT):
                        for a, x in enumerate((XHI, XLO)):
                            last = mm(BANK[2][:, t * NE:(t + 1) * NE], x[:, kt, t * P:(t + 1) * P].bitcast(F32),
                                      RT[:, kt, :], start=(kt == 0 and a == 0), stop=(kt == KT - 1 and a == 1))
                last.then_inc(s["score_ready"], 1)
                pe.wait_ge(s["msk_ready"], 1)
                mm(BANK[3][:, 0:8], UPPER[:, :], MSK[:, 0, :], start=True, stop=True)
                mm(BANK[3][:, 8:16], ONES[:, :], MSK[:, 0, :], start=True, stop=False)
                mm(BANK[3][:, 8:16], UPPER[:, :], MSK[:, 1, :], start=False, stop=True)
                mm(BANK[3][:, 16:24], ONES[:, :], MSK[:, 0, :], start=True, stop=False)
                mm(BANK[3][:, 16:24], ONES[:, :], MSK[:, 1, :], start=False, stop=True).then_inc(s["pos_mm"], 1)

            def hybrid(l):
                R = range
                pe.wait_ge(s["vn_ready"], 2 * l + 1)
                for h in R(4):
                    last = tr(BANK[2][:, h * P:(h + 1) * P], SGW[:, h, :], IDENT[:, :])
                last.then_inc(s["wt_tp"], 1)
                pe.wait_ge(s["wt_ready"], l + 1)
                pe.wait_ge(s["vn_ready"], 2 * l + 2)
                for t in R(TT):
                    for h in R(4):
                        o = 64 * (h % 2)
                        dst = BANK[3][o:o + 64, (2 * (h // 2) + t) * P:(2 * (h // 2) + t + 1) * P]
                        mm(dst, VR[:, t, h * 64:(h + 1) * 64], WT[:, h, :], start=True, stop=False)
                        last = mm(dst, SEL[0:4, h, 0:64], SGB[:, :], start=False, stop=True)
                last.then_inc(s["sp_mm"], 1)
                pe.wait_ge(s["zln_in"], l + 1)
                for i in R(2):
                    last = mm(BANK[4][:, 0:S], ONES[:, :], Z1[:, i, :], start=(i == 0), stop=(i == 1))
                last.then_inc(s["zln_mm"], 1)
                pe.wait_ge(s["zc_in"], l + 1)
                for i in R(2):
                    last = mm(BANK[5][:, 0:S], ONES[:, :], Z2[:, i, 0:S], start=(i == 0), stop=(i == 1))
                last.then_inc(s["zv_mm"], 1)
                pe.wait_ge(s["lrk_act"], 3 * (l + 1))
                for j, (a, b) in enumerate(((0, 32), (32, 64), (64, 128))):
                    for i in R(2):
                        last = mm(BANK[6 if j == 0 else 7 if j == 1 else 2][:, i * S:(i + 1) * S],
                                  UPW[a:b, i * P:(i + 1) * P], LRK[a:b, :], start=True, stop=True)
                last.then_inc(s["up_mm"], 1)
                pe.wait_ge(s["kk_in"], l + 1)
                mm(BANK[3][:, :], BLOCK64[:, :], KN.rearrange("p a b -> p (a b)"), start=True, stop=True)\
                    .then_inc(s["nrm_mm"], 1)
                pe.wait_ge(s["bonus_in"], l + 1)
                mm(BANK[4][:, :], BLOCK64[:, :], RB.rearrange("p a b -> p (a b)"),
                   start=True, stop=True).then_inc(s["bonus_mm"], 1)
                pe.wait_ge(s["abkr_ready"], l + 1)
                for j, src in enumerate((BH, KH, CM[:, 4:6, :])):
                    for t in R(TT):
                        for i in R(2):
                            last = tr(BANK[5 + j][:, (2 * t + i) * P:(2 * t + i + 1) * P], src[:, i, t * P:(t + 1) * P],
                                      IDENT[:, :])
                last.then_inc(s["rows_tp"], 1)

                n = 0
                for lh, rh in ((BH, AH), (KH, AH), (BH, RH), (KH, RH)):
                    for par in R(2):
                        if n >= 2:
                            pe.wait_ge(s["pair_ready"], 8 * l + n - 1)
                        o = 64 * par
                        for t in R(TT):
                            for hp in R(2):
                                last = mm(BANK[n % 2][:, (2 * t + hp) * P:(2 * t + hp + 1) * P],
                                          lh[o:o + 64, hp, t * P:(t + 1) * P], rh[o:o + 64, hp, t * P:(t + 1) * P],
                                          start=True, stop=True)
                        last.then_inc(s["pair_mm"], 1)
                        n += 1
                pe.wait_ge(s["pair_ready"], 8 * l + 8)
                pe.wait_ge(s["rows_ready"], l + 1)
                for lv in R(6):
                    for t in R(TT):
                        m = 12 * l + 2 * lv + t
                        pe.wait_ge(s["lvl_in"], m + 1)
                        for h in R(4):
                            hs = slice(h * P, (h + 1) * P)
                            last = mm(BANK[2 + 3 * t][:, hs], LM[:, t, hs], XX[:, t, hs], start=True, stop=True)
                        last.then_inc(s["t1_mm"], 1)
                        pe.wait_ge(s["t1_ready"], m + 1)
                        for h in R(4):
                            hs = slice(h * P, (h + 1) * P)
                            if lv < 5:
                                mm(BANK[3 + 3 * t][:, hs], XT[:, t, hs], T1[:, hs], start=True, stop=True)
                            last = mm(BANK[4 + 3 * t][:, hs], T1[:, hs], XT[:, t, hs], start=True, stop=True)
                        last.then_inc(s["xx_mm"], 1)
                pe.wait_ge(s["xx_ready"], 12 * l + 12)
                AK, BR, KR = PAIR
                for n in R(4):
                    t, o = n // 2, 64 * (n % 2)
                    cs = slice(n * 64, (n + 1) * 64)
                    if n:
                        pe.wait_ge(s["sn_ready"], 3 * l + n)
                    new = 4 * (n % 2)
                    for h in R(4):
                        hc = slice(h * P + o, h * P + o + 64)
                        dst = BANK[0][o:o + 64, h * 64:(h + 1) * 64]
                        if n:
                            mm(dst, AH[:, h // 2, cs], ST2[:, new + h, :], start=True, stop=False)
                        last = mm(dst, AK[:, t, hc], RV[:, t, h * 64:(h + 1) * 64], start=(n == 0), stop=True)
                    last.then_inc(s["rhs_mm"], 1)
                    pe.wait_ge(s["rhs_ready"], 4 * l + n + 1)
                    for h in R(4):
                        hc = slice(h * P + o, h * P + o + 64)
                        last = mm(BANK[1][o:o + 64, h * 64:(h + 1) * 64], XT[:, t, hc], RHS[:, h, :],
                                  start=True, stop=True)
                    last.then_inc(s["sa_mm"], 1)
                    pe.wait_ge(s["sa_ready"], 4 * l + n + 1)
                    for h in R(4 if n < 3 else 0):
                        js, dst = slice((h // 2) * P, (h // 2 + 1) * P), BANK[2][:, h * 64:(h + 1) * 64]
                        mm(dst, RB[o:o + 64, t, js], SA[o:o + 64, h, :], start=True, stop=False)
                        last = mm(dst, RK[o:o + 64, t, js], RV[o:o + 64, t, h * 64:(h + 1) * 64],
                                  start=False, stop=True)
                    if n < 3:
                        last.then_inc(s["sn_mm"], 1)
                    for h in R(4):
                        ho, hc = 64 * (h % 2), slice(h * P + o, h * P + o + 64)
                        dst = BANK[3][ho:ho + 64, (h // 2) * S + n * 64:(h // 2) * S + (n + 1) * 64]
                        mm(dst, SA[:, h, :], BR[:, t, hc], start=True, stop=False)
                        if n:
                            mm(dst, ST2[:, new + h, :], RH[:, h // 2, cs], start=False, stop=False)
                        last = mm(dst, RV[:, t, h * 64:(h + 1) * 64], KR[:, t, hc], start=False, stop=True)
                    last.then_inc(s["yc_mm"], 1)
                pe.wait_ge(s["mean_in"], l + 1)
                mm(BANK[5][:, :], BLOCK64[:, :], AH.rearrange("p a b -> p (a b)"), start=True, stop=True)\
                    .then_inc(s["mean_mm"], 1)
                pe.wait_ge(s["var_in"], l + 1)
                mm(BANK[6][:, :], BLOCK64[:, :], BH.rearrange("p a b -> p (a b)"), start=True, stop=True)\
                    .then_inc(s["var_mm"], 1)

            pe.wait_ge(s["consts_ready"], 1)
            pe.wait_ge(s["loads_done"], 16 * N_LOADS)
            pe.wait_ge(s["rows_zero"], 1)
            for t in range(3):
                last = tr(BANK[t][:, 0:P], ROWS[:, t, :], IDENT[:, :])
            last.then_inc(s["cols_tp"], 1)
            pe.wait_ge(s["cols_ready"], 1)
            turn(HN, "hn_ready")
            project(EV_PROJ, ev_dest)
            even_mixer()
            output(EV_OUT)
            turn(HN, "hn_ready")
            ffn(EV_FFN)
            turn(HN, "hn_ready")
            project(OD_PROJ, od_dest)
            odd_mixer()
            turn(OG, "og_ready")
            output(OD_OUT)
            turn(HN, "hn_ready")
            router()
            nxt("x_ready", KT)
            pe.wait_ge(s["flag_ready"], 1)
            crowded = pe.value_load(FLAG_I, min_val=0, max_val=1)
            with pe.If(crowded):
                moe_dense()
            with pe.Else():
                moe_sparse()
            for l in range(2):
                f1, pr, ou, f2 = HY[l]
                turn(HN, "hn_ready")
                ffn(f1)
                turn(HN, "hn_ready")
                project(pr, hy_dest)
                hybrid(l)
                output(ou)
                turn(HN, "hn_ready")
                ffn(f2)

        @block.scalar
        def _(act):
            nxt = counter()
            link = order(act, "act_order")
            af = nc.scalar.activation
            top = [0]

            def split_hi(c_, slot, n=1024):
                if isinstance(c_, int):
                    act.wait_ge(raw_full[slot], 16 * (c_ // RING + 1))
                    wait(act, "chunk_used", c_ - RING + 1)
                nc.scalar.copy(WHI[:, slot, 0:n], RAW[:, slot, 0:n]).then_inc(s["hi_ready"], 1)

            def ahead(c_):
                while top[0] < min(c_ + LEAD + 1, N_CHUNKS):
                    split_hi(top[0], top[0] % RING, words(top[0]))
                    top[0] += 1

            def norm():
                for t in range(TT):
                    act.wait_ge(s["h_ready"], nxt("h_ready"))
                    af(HN[:, t, :], H[:, t, :], ACT.Square, scale=D ** -0.5, accum_out=STAT[:, t:t + 1])\
                        .then_inc(s["ssq_ready"], 1)

            def gain(name):
                for b in range(4):
                    act.wait_ge(s["tp_ready"], nxt("tp_ready"))
                    for j in range(2):
                        kt = 2 * b + j
                        af(XHI[:, kt, :], BANK[4 + b][:, j * S:(j + 1) * S], ACT.Copy, scale=col(name, kt))\
                            .then_inc(s["xhi_ready"], 1)

            def project(ph):
                for i in range(len(ph["cols"])):
                    ahead(ph["c0"] + i)

            def output(ph):
                for i in range(KT):
                    ahead(ph["c0"] + i)

            def ffn(ph, m=0, T=None, n=S):
                T = T or ph["tiles"]
                cs, qs = ph["c0"], ph["q0"]

                def split(k, m_):
                    if isinstance(m_, int) and cs + k + 6 * m_ >= N_CHUNKS:
                        return
                    act.wait_ge(raw_full[(cs + k) % RING], 16 * ((cs + k) // RING + 1) + 16 * m_)
                    act.wait_ge(s["chunk_used"], cs + k - RING + 1 + 6 * m_)
                    split_hi(None, (cs + k) % RING)

                def silu(t_, m_):
                    act.wait_ge(s["chunk_used"], cs + (3 * t_ + 1 if t_ else 2) + 6 * m_)
                    act.wait_ge(s["bank_free"], qs + t_ - 1 + 2 * m_)
                    b = (qs + t_) % 2
                    af(SIL[:, b, 0:n], BANK[b][:, 0:n], ACT.Silu).then_inc(s["silu_ready"], 1)
                for k in (3, 4):
                    split(k, m)
                silu(0, m)
                for k in (5, 6, 7):
                    split(k, m)
                silu(1, m)
                with act.Fori(0, T // 2 - 2) as i:
                    for j in (2, 3):
                        for k in (2, 3, 4):
                            split(3 * j + k, m + i)
                        silu(j, m + i)
                for j in (T - 2, T - 1):
                    for k in (2, 3, 4):
                        split(3 * j + k, m)
                    silu(j, m)
                split(3 * T + 2, m)
                top[0] = min(cs + 3 * ph["tiles"] + LEAD, N_CHUNKS)

            def moe_dense():
                with act.Fori(0, NE) as e:
                    ffn(MOE, F_EXPERT // 2 * e, F_EXPERT)

            def moe_sparse():
                cs, qs, ts, F = MOE["c0"], MOE["q0"], MOE["t0"], F_EXPERT

                def gathered(e):
                    for half in range(2):
                        act.wait_ge(s["gath_mm"], 2 * e + half + 1)
                        nc.scalar.copy(XGH[:, 4 * half:4 * half + 4, :],
                                       BANK[half][:, :].rearrange("p (k n) -> p k n", k=4)).then_inc(s["xgh_ready"], 1)

                def split(m, k):
                    act.wait_ge(raw_full[(cs + k) % RING], 16 * ((cs + k) // RING + 1) + 8 * F * m[0] + 16 * m[1])
                    act.wait_ge(s["chunk_used"], cs + k - RING + 1 + 3 * F * m[0] + 6 * m[1])
                    split_hi(None, (cs + k) % RING)

                def tile(m, j, end=False):
                    q_, b, hb = 2 * m[1] + F * m[0] + j, (qs + j) % 2, (ts + j) % 2
                    act.wait_ge(s["chunk_used"], cs + (3 * j + 1 if j else 2) + 3 * F * m[0] + 6 * m[1])
                    act.wait_ge(s["bank_free"], qs + q_ - 1)
                    af(SIL[:, b, 0:P], BANK[b][:, 0:P], ACT.Silu).then_inc(s["silu_ready"], 1)
                    split(m, 3 * j + 5)
                    if not end:
                        split(m, 3 * j + 6)
                    act.wait_ge(s["hidt_tp"], q_ + 1)
                    nc.scalar.copy(HIDHI[:, hb, 0:P], BANK[b][:, 2 * P:3 * P]).then_inc(s["hidhi_made"], 1)
                    if not end:
                        split(m, 3 * j + 7)

                def expert(e, more):
                    tile((e, 0), 0)
                    tile((e, 0), 1)
                    with act.Fori(0, F // 2 - 2) as i:
                        tile((e, i), 2)
                        tile((e, i), 3)
                    tile((e, 0), F - 2)
                    tile((e, 0), F - 1, end=not more)
                    if more:
                        gathered(e + 1)
                    act.wait_ge(s["chunk_used"], cs + 3 * F + 3 * F * e)
                    nc.scalar.copy(YE[:, 0:512], YB[0][0][:, :]).then_inc(s["ye_act"], 1)
                gathered(0)
                split((0, 0), 3)
                split((0, 0), 4)
                with act.Fori(0, NE - 1) as e:
                    expert(e, True)
                expert(NE - 1, False)

            def post(c_):
                act.wait_ge(s["chunk_used"], c_ + 1)
                for t in range(TT):
                    for h in range(2):
                        af(HN[:, t, h * 512:(h + 1) * 512], YB[t][h][:, :], ACT.Square, scale=D ** -0.5,
                           accum_out=STAT[:, 4 + 2 * t + h:5 + 2 * t + h]).then_inc(s["ssq_ready"], 1)

            def even_mixer():
                act.wait_ge(s["spx_ready"], 1)
                af(SPE[:, :], SPN[:, :], ACT.Exp).then_inc(s["spe_ready"], 1)
                act.wait_ge(s["gates_mm"], 1)
                for g, name, b in ((RG, "ga_b", 4), (IG, "gx_b", 6)):
                    for i in range(4):
                        af(g[:, i, :], BANK[b + i // 2][:, (i % 2) * S:(i % 2 + 1) * S], ACT.Sigmoid,
                           bias=col(name, i)).then_inc(s["sig_ready"], 1)
                act.wait_ge(s["sig_ready"], 8)
                act.wait_ge(s["small_ready"], 1)
                for i in range(4):
                    af(AE[:, i, :], RG[:, i, :], ACT.Exp, scale=SPR[:, i:i + 1]).then_inc(s["aexp_ready"], 1)
                    af(TH[:, i, :], RG[:, i, :], ACT.Tanh, scale=SPS[:, i:i + 1]).then_inc(s["aexp_ready"], 1)
                act.wait_ge(s["root_in"], 1)
                af(TH[:, :, :], TH[:, :, :], ACT.Sqrt).then_inc(s["root_ready"], 1)
                for i in range(4):
                    af(YR[:, i, :], YR[:, i, :], ACT.Gelu_apprx_tanh).then_inc(s["gelu_ready"], 1)

                def copy(u):
                    act.wait_ge(s["probt_ready"], u + 1)
                    wait(act, "pv_ready", u - 1)
                    n = u % 2 + 1
                    nc.scalar.copy(PT[:, u % 2, 0:n, :], BANK[u % 2][:, 0:n * P].rearrange("p (b q) -> p b q", b=n))\
                        .then_inc(s["probt_copied"], 1)
                for u in range(17):
                    if u < 16:
                        n = (u % 2 + 1) * P
                        act.wait_ge(s["logit_ready"], u + 1)
                        wait(act, "probt_ready", u - 1)
                        af(PR[:, u % 2, 0:n], LG[:, u % 2, 0:n], ACT.Exp, bias=AMX[:, u:u + 1],
                           accum_out=ASUM[:, u:u + 1]).then_inc(s["prob_ready"], 1)
                    if u:
                        copy(u - 1)

            def odd_mixer():
                act.wait_ge(s["nab_ready"], 1)
                af(GE[:, :, :], GE[:, :, :], ACT.Exp).then_inc(s["gexp_ready"], 1)
                act.wait_ge(s["gexp1_ready"], 1)
                af(GE[:, :, :], GE[:, :, :], ACT.Ln).then_inc(s["gln_ready"], 1)
                act.wait_ge(s["bcum_ready"], 1)
                af(EB[:, :, :], BC_[:, :, :], ACT.Exp, scale=1.0 / 16).then_inc(s["bexp_ready"], 1)
                af(ENB[:, :, :], BC_[:, :, :], ACT.Exp, scale=-1.0 / 16).then_inc(s["bexp_ready"], 1)
                af(GXX[:, :, :], GXX[:, :, :], ACT.Exp, scale=1.0 / 16).then_inc(s["bexp_ready"], 1)
                act.wait_ge(s["kstp_ready"], 1)
                for t in range(TT):
                    last = nc.scalar.copy(KSR[:, t, :], BANK[6 + t][:, :])
                last.then_inc(s["ksr_ready"], 1)
                af(OG[:, :, :], OG[:, :, :], ACT.Silu).then_inc(s["silug_ready"], 1)
                for t in range(TT):
                    if t == 0:
                        act.wait_ge(s["upd_ready"], 2)
                    else:
                        act.wait_ge(s["o_ready"], 1)
                    for h in range(4):
                        b = ((4, 5), (0, 1))[t][h // 2]
                        af(HN[:, t, h * 256:(h + 1) * 256], BANK[b][:, (h % 2) * 256:(h % 2 + 1) * 256], ACT.Square,
                           scale=256 ** -0.5, accum_out=STAT[:, 8 + 4 * t + h:9 + 4 * t + h]).then_inc(s["o_ssq"], 1)

            def router():
                act.wait_ge(s["spx_ready"], 2)
                af(GSM[:, :, 2], GSM[:, :, 1], ACT.Exp).then_inc(s["spe_ready"], 1)

            def hybrid(l):
                act.wait_ge(s["z_sig"], 2 * l + 1)
                af(Z2[:, :, 32:S + 32], Z2[:, :, 32:S + 32], ACT.Sigmoid).then_inc(s["zs_ready"], 1)
                act.wait_ge(s["zn_ready"], l + 1)
                for i in range(2):
                    af(Z1[:, i, :], Z1[:, i, :], ACT.Silu, scale=col(f"cm_ln_w{l}", i),
                       bias=col(f"cm_ln_b{l}", i)).then_inc(s["zs_ready"], 1)
                act.wait_ge(s["pexp_in"], 3 * l + 1)
                af(LRK[0:32, :], CM[0:32, 6, :], ACT.Tanh).then_inc(s["lrk_act"], 1)
                af(LRK[32:64, :], CM[32:64, 6, :], ACT.Copy).then_inc(s["lrk_act"], 1)
                af(LRK[64:128, :], CM[64:128, 6, :], ACT.Sigmoid).then_inc(s["lrk_act"], 1)
                act.wait_ge(s["up_mm"], l + 1)
                for i in range(2):
                    af(SGW_[:, i, :], BANK[6][:, i * S:(i + 1) * S], ACT.Sigmoid, bias=col(f"rk_w0{l}", i))\
                        .then_inc(s["upsig_ready"], 1)
                    af(AV[:, i, :], BANK[7][:, i * S:(i + 1) * S], ACT.Sigmoid, bias=col(f"rk_a0{l}", i))\
                        .then_inc(s["upsig_ready"], 1)
                nc.scalar.copy(GG.rearrange("p a b -> p (a b)"), BANK[2][:, :]).then_inc(s["upsig_ready"], 1)
                act.wait_ge(s["pexp_in"], 3 * l + 2)
                af(PP, CB, ACT.Exp, scale=-DECAY_C).then_inc(s["pexp_ready"], 1)
                af(PPV, PPV, ACT.Exp, scale=-DECAY_C).then_inc(s["pexp_ready"], 1)
                af(PIN, CB, ACT.Exp, scale=DECAY_C).then_inc(s["pexp_ready"], 1)
                act.wait_ge(s["rows_tp"], l + 1)
                for j, dst in enumerate((RB, RK, RV)):
                    last = nc.scalar.copy(dst.rearrange("p a b -> p (a b)"), BANK[5 + j][:, :])
                last.then_inc(s["rows_ready"], 1)
                for m in range(12):
                    t = m % 2
                    act.wait_ge(s["t1_mm"], 12 * l + m + 1)
                    if m:
                        act.wait_ge(s["xx_mm"], 12 * l + m)
                    nc.scalar.copy(T1[:, :], BANK[2 + 3 * t][:, :]).then_inc(s["t1_ready"], 1)
                for n in range(4):
                    o = 64 * (n % 2)
                    act.wait_ge(s["rhs_mm"], 4 * l + n + 1)
                    nc.scalar.copy(RHS[o:o + 64, :, :], BANK[0][o:o + 64, 0:256].rearrange("p (h i) -> p h i", h=4))\
                        .then_inc(s["rhs_ready"], 1)
                    act.wait_ge(s["sa_mm"], 4 * l + n + 1)
                    nc.scalar.copy(SA[o:o + 64, :, :], BANK[1][o:o + 64, 0:256].rearrange("p (h i) -> p h i", h=4))\
                        .then_inc(s["sa_ready"], 1)

            act.wait_ge(s["x_loaded"], 16)
            for t in range(TT):
                af(HN[:, t, :], H[:, t, :], ACT.Square, scale=D ** -0.5, accum_out=STAT[:, t:t + 1])\
                    .then_inc(s["ssq_ready"], 1)
            ahead(-1)
            act.wait_ge(s["cols_ready"], 1)
            gain("norm_mix0")
            project(EV_PROJ)
            even_mixer()
            output(EV_OUT)
            norm()
            gain("norm_ffn0")
            ffn(EV_FFN)
            norm()
            gain("norm_mix1")
            project(OD_PROJ)
            odd_mixer()
            gain("head_norm")
            output(OD_OUT)
            norm()
            gain("norm_ffn1")
            router()
            act.wait_ge(s["flag_ready"], 1)
            crowded = act.value_load(FLAG_I, min_val=0, max_val=1)
            with act.If(crowded):
                moe_dense()
            with act.Else():
                moe_sparse()
            norm()
            for l in range(2):
                f1, pr, ou, f2 = HY[l]
                norm()
                gain(f"ffn1_pre{l}")
                ffn(f1)
                post(last_chunk(f1))
                norm()
                gain(f"mix_pre{l}")
                project(pr)
                hybrid(l)
                output(ou)
                post(last_chunk(ou))
                norm()
                gain(f"ffn2_pre{l}")
                ffn(f2)
                post(last_chunk(f2))

        @block.vector
        def _(dve):
            nxt = counter()
            link = order(dve, "dve_order")
            V_ = nc.vector
            marks = [0]

            def mark(name):
                marks[0] += 1
                V_.memset(STAT[:, 63 + marks[0]:64 + marks[0]], 0.0).then_inc(s[name], 1)
            top = [0]

            def split_lo(slot, n=1024):
                V_.tensor_tensor(WLO[:, slot, 0:n], RAW[:, slot, 0:n], WHI[:, slot, 0:n].bitcast(F32), ALU.subtract)\
                    .then_inc(s["lo_ready"], 1)

            def ahead(c_):
                while top[0] < min(c_ + LEAD + 1, N_CHUNKS):
                    dve.wait_ge(s["hi_ready"], top[0] + 1)
                    split_lo(top[0] % RING, words(top[0]))
                    top[0] += 1

            def split_x(src, a, b, inc=0):
                link(V_.tensor_copy(XHI[:, a:b, :], src))
                ins = V_.tensor_tensor(XLO[:, a:b, :], src, XHI[:, a:b, :].bitcast(F32), ALU.subtract)
                if inc:
                    ins.then_inc(s["x_ready"], inc)

            def rsqrt(y, x, tmp, mul=1.0, eps=EPS, floor=False):
                if floor:
                    link(V_.tensor_scalar(x, x, eps, None, ALU.max))
                else:
                    link(V_.tensor_scalar(x, x, mul, eps, ALU.mult, ALU.add))
                link(V_.tensor_scalar(y.bitcast(mybir.dt.int32), x.bitcast(mybir.dt.int32), -0.5, float(0x5F3759DF),
                                      ALU.mult, ALU.add))
                for _ in range(3):
                    link(V_.tensor_tensor(tmp, y, y, ALU.mult))
                    link(V_.tensor_tensor(tmp, tmp, x, ALU.mult))
                    link(V_.tensor_scalar(tmp, tmp, -0.5, 1.5, ALU.mult, ALU.add))
                    link(V_.tensor_tensor(y, y, tmp, ALU.mult))

            def norm():
                dve.wait_ge(s["ssq_ready"], nxt("ssq_ready", TT))
                rsqrt(STAT[:, 2:4], STAT[:, 0:2], STAT[:, 54:56])
                for t in range(TT):
                    last = V_.tensor_scalar(HN[:, t, :], H[:, t, :], STAT[:, 2 + t:3 + t], None, ALU.mult)
                last.then_inc(s["hn_ready"], 1)

            def gain(name):
                for b in range(4):
                    dve.wait_ge(s["xhi_ready"], nxt("xhi_ready", 2))
                    for j in range(2):
                        kt = 2 * b + j
                        V_.scalar_tensor_tensor(XLO[:, kt, :], BANK[4 + b][:, j * S:(j + 1) * S], col(name, kt),
                                                XHI[:, kt, :].bitcast(F32), ALU.mult, ALU.subtract)\
                            .then_inc(s["x_ready"], 1)

            def project(ph, dest):
                for i, n in enumerate(ph["cols"]):
                    ahead(ph["c0"] + i)
                    q = ph["q0"] + i
                    dst, row = dest(i)
                    dve.wait_ge(s["chunk_used"], ph["c0"] + i + 1)
                    src = BANK[q % 2][:, 0:2 * n].rearrange("p (t n) -> p t n", t=TT) if row else BANK[q % 2][:, 0:S]
                    V_.tensor_copy(dst, src).then_inc(s["bank_free"], 1)
                dve.wait_ge(s["bank_free"], ph["q0"] + len(ph["cols"]))

            def output(ph):
                for i in range(KT):
                    ahead(ph["c0"] + i)

            def ffn(ph, m=0, T=None, n=S, gate=None):
                T = T or ph["tiles"]
                cs, qs, ts = ph["c0"], ph["q0"], ph["t0"]

                def split(k, m_):
                    if isinstance(m_, int) and cs + k + 6 * m_ >= N_CHUNKS:
                        return
                    dve.wait_ge(s["hi_ready"], cs + k + 1 + 6 * m_)
                    split_lo((cs + k) % RING)

                def hidden(j, m_):
                    qb, b, t_ = (qs + j) % 2, (ts + j) % 2, ts + j + 2 * m_
                    dve.wait_ge(s["silu_ready"], t_ + 1)
                    V_.tensor_tensor(HID[:, b, 0:n], SIL[:, qb, 0:n], BANK[qb][:, S:S + n], ALU.mult)\
                        .then_inc(s["bank_free"], 1)
                    dve.wait_ge(s["bank_free"], qs + j + 1 + 2 * m_)
                    if gate is not None:
                        V_.tensor_tensor(HID[:, b, :], HID[:, b, :], gate, ALU.mult).then_inc(s["hid_gated"], 1)
                        dve.wait_ge(s["hid_gated"], j + 1 + 2 * m_)
                    V_.tensor_copy(HIDHI[:, b, 0:n], HID[:, b, 0:n]).then_inc(s["hidhi_made"], 1)
                    dve.wait_ge(s["hidhi_made"], t_ + 1)
                    V_.tensor_tensor(HIDLO[:, b, 0:n], HID[:, b, 0:n], HIDHI[:, b, 0:n].bitcast(F32), ALU.subtract)\
                        .then_inc(s["hid_ready"], 1)
                for k in (3, 4):
                    split(k, m)
                hidden(0, m)
                for k in (5, 6, 7):
                    split(k, m)
                hidden(1, m)
                with dve.Fori(0, T // 2 - 2) as i:
                    for j in (2, 3):
                        for k in (2, 3, 4):
                            split(3 * j + k, m + i)
                        hidden(j, m + i)
                for j in (T - 2, T - 1):
                    for k in (2, 3, 4):
                        split(3 * j + k, m)
                    hidden(j, m)
                split(3 * T + 2, m)
                top[0] = min(cs + 3 * ph["tiles"] + LEAD, N_CHUNKS)

            def moe_dense():
                link = order(dve, "dense_order")
                for i in range(2 * NE + 1):
                    if i < 2 * NE:
                        if i >= 2:
                            dve.wait_ge(s["gate_mm"], i)
                        V_.tensor_scalar(SIL[:, i % 2, 0:P], IDENT[:, :], GATES[:, i % 2, i // 2:i // 2 + 1], None,
                                         ALU.mult).then_inc(s["gates_ready"], 1)
                    if i:
                        j = i - 1
                        dve.wait_ge(s["gate_mm"], 1 + i)
                        link(V_.tensor_copy(GATE_BC[:, j // 2, (j % 2) * P:(j % 2 + 1) * P], BANK[2 + j % 2][:, 0:P]))
                V_.memset(ZERO[:, :], 0.0).then_inc(s["zero_ready"], 1)
                with dve.Fori(0, NE) as e:
                    ffn(MOE, F_EXPERT // 2 * e, F_EXPERT,
                        gate=GATE_BC[:, bass.ds(e, 1), :].rearrange("p a b -> p (a b)"))
                dve.wait_ge(s["chunk_used"], last_chunk(MOE) + 1)
                add_y()

            def moe_sparse():
                link = order(dve, "sparse_order")
                gi = 0
                dve.wait_ge(gbc_full[0], 16)
                for t in range(TT):
                    last = V_.tensor_tensor(HN[:, t, :], HN[:, t, :], GBC[:, gi, :], ALU.mult)
                last.then_inc(s["hng_ready"], 1)
                for t in range(TT):
                    for e in range(NE):
                        last = V_.tensor_scalar(PSEL[:, NE * t + e, :], IOTA[:, :], POS[:, t, e:e + 1], None,
                                                ALU.is_equal)
                last.then_inc(s["psel_ready"], 1)
                for g in range(5):
                    if g < 4:
                        if g >= 2:
                            dve.wait_ge(s["pgt_tp"], g - 1)
                        for j in range(4):
                            e, t = 2 * g + j // 2, j % 2
                            last = V_.tensor_scalar(PG[:, g % 2, j * P:(j + 1) * P], IOTA[:, :], POS[:, t, e:e + 1],
                                                    GATES[:, t, e:e + 1], ALU.is_equal, ALU.mult)
                        last.then_inc(s["pg_ready"], 1)
                    if g:
                        dve.wait_ge(s["pgt_tp"], g)
                        link(V_.tensor_copy(PGT[:, 2 * g - 2:2 * g, :], BANK[2 + (g - 1) % 2][:, :]
                                            .rearrange("p (e n) -> p e n", e=2)))
                V_.memset(ZERO[:, :], 0.0).then_inc(s["zero_ready"], 1)

                cs, qs, ts, F = MOE["c0"], MOE["q0"], MOE["t0"], F_EXPERT

                def gathered(e):
                    for half in range(2):
                        dve.wait_ge(s["xgh_ready"], 2 * e + half + 1)
                        V_.tensor_tensor(XGL[:, 4 * half:4 * half + 4, :],
                                         BANK[half][:, :].rearrange("p (k n) -> p k n", k=4),
                                         XGH[:, 4 * half:4 * half + 4, :].bitcast(F32), ALU.subtract)\
                            .then_inc(s["xg_ready"], 1)

                def split(m, k):
                    dve.wait_ge(s["hi_ready"], cs + k + 1 + 3 * F * m[0] + 6 * m[1])
                    split_lo((cs + k) % RING)

                def tile(m, j, end=False):
                    t_, b, hb = F * m[0] + 2 * m[1] + j, (qs + j) % 2, (ts + j) % 2
                    dve.wait_ge(s["silu_ready"], ts + t_ + 1)
                    V_.tensor_tensor(HID[:, hb, 0:P], SIL[:, b, 0:P], BANK[b][:, P:2 * P], ALU.mult)\
                        .then_inc(s["bank_free"], 1)
                    split(m, 3 * j + 5)
                    if not end:
                        split(m, 3 * j + 6)
                    dve.wait_ge(s["hidhi_made"], ts + t_ + 1)
                    V_.tensor_tensor(HIDLO[:, hb, 0:P], BANK[b][:, 2 * P:3 * P], HIDHI[:, hb, 0:P].bitcast(F32),
                                     ALU.subtract).then_inc(s["hid_ready"], 1)
                    if not end:
                        split(m, 3 * j + 7)

                def expert(e, more):
                    tile((e, 0), 0)
                    tile((e, 0), 1)
                    with dve.Fori(0, F // 2 - 2) as i:
                        tile((e, i), 2)
                        tile((e, i), 3)
                    tile((e, 0), F - 2)
                    tile((e, 0), F - 1, end=not more)
                    if more:
                        gathered(e + 1)
                    dve.wait_ge(s["chunk_used"], cs + 3 * F + 3 * F * e)
                    V_.tensor_copy(YE[:, 512:D], YB[0][1][:, :]).then_inc(s["ye_ready"], 1)
                gathered(0)
                split((0, 0), 3)
                split((0, 0), 4)
                with dve.Fori(0, NE - 1) as e:
                    expert(e, True)
                expert(NE - 1, False)
                dve.wait_ge(s["outt_mm"], 1)
                for b in range(4):
                    V_.tensor_copy(OUTT[:, 2 * b:2 * b + 2, :], OUTB[b][:, :].rearrange("p (k n) -> p k n", k=2))\
                        .then_inc(s["outt_ready"], 1)
                dve.wait_ge(s["outt_tp"], 1)
                add_y()

            def add_y():
                for t in range(TT):
                    for h in range(2):
                        hs = slice(h * 512, (h + 1) * 512)
                        last = V_.tensor_tensor(H[:, t, hs], H[:, t, hs], YB[t][h][:, :], ALU.add)
                    last.then_inc(s["h_ready"], 1)

            def residual(ph):
                dve.wait_ge(s["chunk_used"], last_chunk(ph) + 1)
                add_y()

            ngbc = [0]

            def gains_wait():
                i = ngbc[0]
                dve.wait_ge(gbc_full[i % 2], 16 * (i // 2 + 1))
                ngbc[0] += 1
                return i % 2

            def post(resid):
                dve.wait_ge(s["ssq_ready"], nxt("ssq_ready", 4))
                gi = gains_wait()
                link(V_.tensor_tensor(STAT[:, 10:12], STAT[:, 4:8:2], STAT[:, 5:8:2], ALU.add))
                rsqrt(STAT[:, 12:14], STAT[:, 10:12], STAT[:, 54:56])
                link(V_.tensor_scalar(STAT[:, 12:14], STAT[:, 12:14], resid, None, ALU.mult))
                for t in range(TT):
                    for h in range(2):
                        hs = slice(h * 512, (h + 1) * 512)
                        last = V_.scalar_tensor_tensor(HN[:, t, hs], YB[t][h][:, :], STAT[:, 12 + t:13 + t],
                                                       GBC[:, gi, hs], ALU.mult, ALU.mult)
                    if t == TT - 1:
                        last.then_inc(s["gbc_used"], 1)
                dve.wait_ge(s["gbc_used"], ngbc[0])
                for t in range(TT):
                    V_.tensor_tensor(H[:, t, :], H[:, t, :], HN[:, t, :], ALU.add).then_inc(s["h_ready"], 1)

            def log1p(dst, e, t1, t2, t3):
                link(V_.tensor_scalar(t1, e, 2.0, None, ALU.add))
                link(V_.reciprocal(t2, t1))
                link(V_.tensor_tensor(t1, e, t2, ALU.mult))
                link(V_.tensor_tensor(t2, t1, t1, ALU.mult))
                link(V_.tensor_scalar(t3, t2, 1.0 / 15, None, ALU.mult))
                for k in (13, 11, 9, 7, 5, 3):
                    link(V_.scalar_tensor_tensor(t3, t3, 1.0 / k, t2, ALU.add, ALU.mult))
                link(V_.scalar_tensor_tensor(t3, t3, 1.0, t1, ALU.add, ALU.mult))
                link(V_.tensor_scalar(dst, t3, 2.0, None, ALU.mult))

            def flat_(ap):
                return ap.rearrange("p a b -> p (a b)")

            def even_mixer():
                link(V_.memset(XR[:, :, 0:4], 0.0))
                link(V_.tensor_scalar(flat_(Q), flat_(Q), 64 ** -0.5, None, ALU.mult))
                link(V_.tensor_copy(SPX[:, 0:4], colr("lam", 4)))
                for t in range(TT):
                    last = V_.tensor_tensor(SPX[:, 4 + 8 * t:12 + 8 * t], FL[:, t, :], FB[:, :], ALU.add)
                link(last)
                V_.scalar_tensor_tensor(SPN[:, :], SPX[:, :], -1.0, SPX[:, :], ALU.mult, ALU.min).then_inc(s["spx_ready"], 1)
                dve.wait_ge(s["spe_ready"], 1)
                log1p(SP[:, :], SPE[:, :], SPP[:, :], SPR[:, :], SPS[:, :])
                link(V_.tensor_scalar(SPX[:, :], SPX[:, :], -1.0, 0.0, ALU.mult, ALU.max))
                link(V_.tensor_tensor(SP[:, :], SP[:, :], SPX[:, :], ALU.add))
                link(V_.tensor_scalar(SPR[:, 0:4], SP[:, 0:4], -8.0, None, ALU.mult))
                link(V_.tensor_scalar(SPS[:, 0:4], SP[:, 0:4], 8.0, None, ALU.mult))
                V_.tensor_scalar(SP[:, 4:20], SP[:, 4:20], -1.0, None, ALU.mult).then_inc(s["small_ready"], 1)
                for j in range(4):
                    for i in range(4):
                        x = XR[:, i, 1 + j:1 + j + S]
                        w = col("conv_w", 4 * j + i)
                        if j == 0:
                            last = V_.tensor_scalar(XC[:, i, :], x, w, col("conv_b", i), ALU.mult, ALU.add)
                        else:
                            last = V_.scalar_tensor_tensor(XC[:, i, :], x, w, XC[:, i, :], ALU.mult, ALU.add)
                    if j < 3:
                        link(last)
                last.then_inc(s["conv_ready"], 1)
                dve.wait_ge(s["conv_ready"], 1)
                dve.wait_ge(s["cum_ready"], 1)
                V_.tensor_scalar(NCT[:, :], BANK[0][0:8, 0:S], -1.0, None, ALU.mult)
                V_.tensor_copy(CC[:, :, :], BANK[1][:, 0:16].rearrange("p (t h) -> p t h", t=TT))\
                    .then_inc(s["cumev_ready"], 1)
                dve.wait_ge(s["cumev_ready"], 1)

                dve.wait_ge(s["sig_ready"], 8)
                link(V_.tensor_tensor(flat_(IG), flat_(IG), flat_(XC), ALU.mult))
                dve.wait_ge(s["aexp_ready"], 8)
                link(V_.tensor_tensor(flat_(RG), flat_(AE), flat_(AE), ALU.mult))
                V_.scalar_tensor_tensor(flat_(TH), flat_(RG), 1.0, flat_(TH), ALU.add, ALU.mult)\
                    .then_inc(s["root_in"], 1)
                dve.wait_ge(s["root_ready"], 1)
                link(V_.tensor_tensor(flat_(IG), flat_(IG), flat_(TH), ALU.mult))
                for i in range(4):
                    last = V_.tensor_tensor_scan(XC[:, i, :], AE[:, i, :], IG[:, i, :], 0.0, ALU.mult, ALU.add)
                link(last)
                dve.wait_ge(s["gelu_ready"], 4)
                link(V_.tensor_tensor(flat_(YR), flat_(YR), flat_(XC), ALU.mult))
                split_x(YR[:, :, :], 0, 4, 4)

                def logits(u):
                    h, t = u // 2, u % 2
                    n = (t + 1) * P
                    dve.wait_ge(s["score_ready"], u + 1)
                    wait(dve, "prob_ready", u - 1)
                    link(V_.scalar_tensor_tensor(LG[:, u % 2, 0:n], BANK[2 + u % 2][:, 0:n], CC[:, t, h:h + 1],
                                                 CAUSAL[:, S - n:S], ALU.add, ALU.add))
                    V_.tensor_reduce(AMX[:, u:u + 1], LG[:, u % 2, 0:n], AX.X, ALU.max, negate=True)\
                        .then_inc(s["logit_ready"], 1)
                for u in range(17):
                    if u < 16:
                        logits(u)
                    if u:
                        v = u - 1
                        n = (v % 2 + 1) * P
                        dve.wait_ge(s["prob_ready"], v + 1)
                        link(V_.reciprocal(AREC[:, v:v + 1], ASUM[:, v:v + 1]))
                        V_.tensor_scalar(PR[:, v % 2, 0:n], PR[:, v % 2, 0:n], AREC[:, v:v + 1], None, ALU.mult)\
                            .then_inc(s["probn_ready"], 1)
                for p in range(4):
                    dve.wait_ge(s["pv_ready"], 4 * p + 4)
                    split_x(BANK[4 + p][:, 0:S], 4 + p, 5 + p, 1)
                dve.wait_ge(s["x_ready"], 16)
                mark("mixer_done")

            def odd_mixer():
                mark("lrk_ready")
                dve.wait_ge(s["lr_tp"], 1)
                V_.tensor_copy(LRT[:, :], BANK[2][0:16, 0:S]).then_inc(s["lrt_ready"], 1)
                dve.wait_ge(s["gate_mm"], 1)
                for i in range(4):
                    last = V_.tensor_scalar(GXX[:, i, :], BANK[4 + i // 2][:, (i % 2) * S:(i % 2 + 1) * S],
                                            col("gate_b", i), None, ALU.add)
                link(last)
                V_.scalar_tensor_tensor(flat_(GE), flat_(GXX), -1.0, flat_(GXX), ALU.mult, ALU.min).then_inc(s["nab_ready"], 1)
                dve.wait_ge(s["gexp_ready"], 1)
                V_.tensor_scalar(flat_(GE), flat_(GE), 1.0, None, ALU.add).then_inc(s["gexp1_ready"], 1)
                dve.wait_ge(s["gln_ready"], 1)
                link(V_.scalar_tensor_tensor(flat_(GE), flat_(GXX), 0.0, flat_(GE), ALU.min, ALU.subtract))
                link(V_.tensor_tensor_scan(flat_(BC_), RESET[:, :], flat_(GE), 0.0, ALU.mult, ALU.add))
                b16 = flat_(BC_).rearrange("p (c j) -> p c j", j=64)
                V_.tensor_tensor(flat_(GXX).rearrange("p (c j) -> p c j", j=64),
                                 b16[:, :, 63:64].broadcast_to([P, 16, 64]), b16, ALU.subtract)\
                    .then_inc(s["bcum_ready"], 1)
                dve.wait_ge(s["bexp_ready"], 3)
                link(V_.tensor_copy(SDEC[:, :, :], EB[:, :, 63:S:64]))
                V_.scalar_tensor_tensor(flat_(EB), flat_(OQ), P ** -0.5, flat_(EB), ALU.mult, ALU.mult)
                V_.tensor_tensor(flat_(ENB), flat_(OK), flat_(ENB), ALU.mult)
                V_.tensor_tensor(flat_(GXX), flat_(OK), flat_(GXX), ALU.mult).then_inc(s["kdec_ready"], 1)
                for t in range(TT):
                    dve.wait_ge(s["sct_mm"], t + 1)
                    V_.tensor_tensor(SCT[:, t, :].rearrange("p (h i) -> p h i", h=4),
                                     BANK[2 + t][:, :].rearrange("p (h i) -> p h i", h=4),
                                     bcast(UPPER64, 4),
                                     ALU.mult).then_inc(s["sct_ready"], 1)
                for n in range(3):
                    dve.wait_ge(s["upd_ready"], n + 1)
                    wait(dve, "state_ready", n)
                    for h in range(4):
                        ps = BANK[6 + h // 2][:, (h % 2) * 256:(h % 2 + 1) * 256]
                        if n == 0:
                            last = V_.tensor_copy(ST[:, h, :], ps)
                        else:
                            last = V_.scalar_tensor_tensor(ST[:, h, :], ST[:, h, :], SDEC[:, h, n:n + 1], ps,
                                                           ALU.mult, ALU.add)
                    last.then_inc(s["state_ready"], 1)
                dve.wait_ge(s["silug_ready"], 1)
                for t in range(TT):
                    dve.wait_ge(s["o_ssq"], 4 * (t + 1))
                    rsqrt(STAT[:, 24 + 4 * t:28 + 4 * t], STAT[:, 8 + 4 * t:12 + 4 * t], STAT[:, 54:58])
                    for h in range(4):
                        b = ((4, 5), (0, 1))[t][h // 2]
                        hs = slice(h * 256, (h + 1) * 256)
                        last = V_.scalar_tensor_tensor(OG[:, t, hs], BANK[b][:, (h % 2) * 256:(h % 2 + 1) * 256],
                                                       STAT[:, 24 + 4 * t + h:25 + 4 * t + h], OG[:, t, hs],
                                                       ALU.mult, ALU.mult)
                last.then_inc(s["og_ready"], 1)

            def router():
                dve.wait_ge(s["score_ready"], 17)
                link(V_.tensor_copy(flat_(LOGITS), BANK[2][:, 0:16]))
                for t in range(TT):
                    link(V_.max(GMAX[:, t, :], LOGITS[:, t, :]))
                    link(V_.max_index(GIDX[:, t, :], GMAX[:, t, :], LOGITS[:, t, :]))
                    link(V_.tensor_copy(GIF[:, t, :], GIDX[:, t, :]))
                    link(V_.tensor_scalar(EQ1[:, t, :], IOTA[:, 0:NE], GIF[:, t, 0:1], None, ALU.is_equal))
                    link(V_.tensor_copy(GSM[:, t, 0:1], GMAX[:, t, 0:1]))
                    link(V_.scalar_tensor_tensor(LOGITS[:, t, :], EQ1[:, t, :], NEG, LOGITS[:, t, :],
                                                 ALU.mult, ALU.add))
                    link(V_.max(GMAX[:, t, :], LOGITS[:, t, :]))
                    link(V_.max_index(GIDX[:, t, :], GMAX[:, t, :], LOGITS[:, t, :]))
                    link(V_.tensor_copy(GIF[:, t, :], GIDX[:, t, :]))
                    link(V_.tensor_scalar(EQ2[:, t, :], IOTA[:, 0:NE], GIF[:, t, 0:1], None, ALU.is_equal))
                    last = V_.tensor_tensor(GSM[:, t, 1:2], GMAX[:, t, 0:1], GSM[:, t, 0:1], ALU.subtract)
                last.then_inc(s["spx_ready"], 1)
                dve.wait_ge(s["spe_ready"], 2)
                link(V_.tensor_tensor(flat_(MSK), flat_(EQ1), flat_(EQ2), ALU.add))
                mark("msk_ready")
                dve.wait_ge(s["pos_mm"], 1)
                link(V_.tensor_tensor(flat_(POS), BANK[3][:, 0:16], flat_(MSK), ALU.mult))
                link(V_.tensor_scalar(GSM[:, :, 3], GSM[:, :, 2], 1.0, None, ALU.add))
                link(V_.reciprocal(GSM[:, :, 4], GSM[:, :, 3]))
                link(V_.tensor_tensor(GSM[:, :, 5], GSM[:, :, 2], GSM[:, :, 4], ALU.mult))
                for t in range(TT):
                    link(V_.tensor_scalar(GATES[:, t, :], EQ1[:, t, :], GSM[:, t, 4:5], None, ALU.mult))
                    link(V_.scalar_tensor_tensor(GATES[:, t, :], EQ2[:, t, :], GSM[:, t, 5:6], GATES[:, t, :],
                                                 ALU.mult, ALU.add))
                link(V_.tensor_scalar(flat_(POS), flat_(POS), -1.0, None, ALU.add))
                link(V_.tensor_reduce(FLAG[:, 1:2], BANK[3][:, 16:24], AX.X, ALU.max))
                V_.tensor_scalar(FLAG[:, 0:1].bitcast(mybir.dt.int32), FLAG[:, 1:2], float(P) + 0.5, None, ALU.is_gt)\
                    .then_inc(s["flag_ready"], 1)
                dve.wait_ge(s["flag_ready"], 1)
                crowded = dve.value_load(FLAG_I, min_val=0, max_val=1)
                with dve.If(crowded):
                    moe_dense()
                with dve.Else():
                    moe_sparse()
                ngbc[0] += 1
                mark("gbc_used")

            def bcast(t_, n):
                return t_[:, :].rearrange("p (a b) -> p a b", a=1).broadcast_to([P, n, P])

            def hybrid(l):
                R = range
                link(V_.memset(XA[:, :, 0:4], 0.0))
                link(V_.memset(PC[:, :, 0:4], 0.0))
                link(V_.memset(Z2[:, :, 0:32], 0.0))
                dve.wait_ge(s["up_in_ready"], 16 * 7 * (l + 1))
                mark("z_sig")
                mark("z_sig")
                mark("vn_ready")
                for t in R(TT):
                    link(V_.bn_stats(STAT[:, 44:50], VR[:, t, :]))
                    link(V_.bn_aggr(STAT[:, 50:52], STAT[:, 44:50]))
                    rsqrt(STAT[:, 52:53], STAT[:, 51:52], STAT[:, 54:55], eps=LN_EPS)
                    link(V_.tensor_scalar(VR[:, t, :], VR[:, t, :], STAT[:, 50:51], STAT[:, 52:53],
                                          ALU.subtract, ALU.mult))
                    link(V_.tensor_tensor(VR[:, t, :], VR[:, t, :], SGG[:, :], ALU.mult))
                    last = V_.tensor_tensor(VR[:, t, :], VR[:, t, :], SGBB[:, :], ALU.add)
                last.then_inc(s["vn_ready"], 1)
                dve.wait_ge(s["vn_ready"], 2 * l + 2)
                V_.memset(RHS[:, :, :], 0.0)
                V_.memset(SA[:, :, :], 0.0)
                dve.wait_ge(s["wt_tp"], l + 1)
                V_.tensor_tensor(WT[:, :, :], BANK[2][:, :].rearrange("p (h t) -> p h t", h=4), bcast(UPPER, 4),
                                 ALU.mult).then_inc(s["wt_ready"], 1)
                link(V_.tensor_tensor(XA[:, :, 4:S + 4], XA[:, :, 4:S + 4], GC[:, :, :], ALU.mult))
                for j in R(3):
                    for i in R(2):
                        x, w = XA[:, i, 2 + j:2 + j + S], col(f"sc_conv_w{l}", 2 * j + i)
                        if j == 0:
                            last = V_.tensor_scalar(GC[:, i, :], x, w, None, ALU.mult)
                        else:
                            last = V_.scalar_tensor_tensor(GC[:, i, :], x, w, GC[:, i, :], ALU.mult, ALU.add)
                    link(last)
                link(V_.tensor_tensor(flat_(GB), flat_(GB), flat_(GC), ALU.mult))
                split_x(GB[:, :, :], 0, 2)
                dve.wait_ge(s["sp_mm"], l + 1)
                link(V_.tensor_tensor(flat_(UU), flat_(UU), BANK[3][:, :], ALU.mult))
                split_x(UU[:, :, :], 2, 4)
                dve.wait_ge(s["zs_ready"], 3 * l + 1)
                link(V_.tensor_tensor(Z2[:, :, 32:S + 32], Z2[:, :, 32:S + 32], Z1[:, :, :], ALU.mult))
                for j in R(31):
                    for i in R(2):
                        x, w = Z2[:, i, 2 + j:2 + j + S], col(f"cm_conv_w{l}", 2 * j + i)
                        if j == 0:
                            last = V_.tensor_scalar(Z1[:, i, :], x, w, col(f"cm_conv_b{l}", i), ALU.mult, ALU.add)
                        else:
                            last = V_.scalar_tensor_tensor(Z1[:, i, :], x, w, Z1[:, i, :], ALU.mult, ALU.add)
                    if j < 30:
                        link(last)
                last.then_inc(s["zln_in"], 1)
                link(V_.tensor_tensor(CM[:, :, :], PC[:, :, 3:S + 3], PC[:, :, 4:S + 4], ALU.subtract))
                for i in (6, 0, 1, 2, 3, 4, 5):
                    ins = V_.scalar_tensor_tensor(CM[:, i, :], CM[:, i, :], col(f"rk_mu{l}", i), PC[:, i, 4:S + 4],
                                                  ALU.mult, ALU.add)
                    if i == 6:
                        ins.then_inc(s["pexp_in"], 1)
                link(ins)
                dve.wait_ge(s["zln_mm"], l + 1)
                for i in R(2):
                    last = V_.scalar_tensor_tensor(Z1[:, i, :], BANK[4][:, 0:S], -1.0 / 256, Z1[:, i, :],
                                                   ALU.mult, ALU.add)
                link(last)
                V_.tensor_tensor(Z2[:, :, 0:S], Z1[:, :, :], Z1[:, :, :], ALU.mult).then_inc(s["zc_in"], 1)
                dve.wait_ge(s["zv_mm"], l + 1)
                link(V_.tensor_copy(XA[:, 1, 0:S], BANK[5][:, 0:S]))
                rsqrt(XA[:, 0, 0:S], XA[:, 1, 0:S], GC[:, 0, :], mul=1.0 / 256, eps=LN_EPS)
                for i in R(2):
                    last = V_.tensor_tensor(Z1[:, i, :], Z1[:, i, :], XA[:, 0, 0:S], ALU.mult)
                last.then_inc(s["zn_ready"], 1)
                for i in R(2):
                    last = V_.tensor_scalar(KK[:, i, :], CM[:, 2 + i, :], col(f"rk_k_k{l}", i), None, ALU.mult)
                link(last)
                V_.tensor_tensor(flat_(KN), flat_(KK), flat_(KK), ALU.mult).then_inc(s["kk_in"], 1)
                dve.wait_ge(s["zs_ready"], 3 * l + 3)
                split_x(Z1[:, :, :], 6, 8)
                dve.wait_ge(s["nrm_mm"], l + 1)
                link(V_.tensor_copy(flat_(AH), BANK[3][:, :]))
                rsqrt(flat_(KN), flat_(AH), flat_(BH), eps=1e-24, floor=True)
                link(V_.tensor_tensor(flat_(KK), flat_(KK), flat_(KN), ALU.mult))
                dve.wait_ge(s["upsig_ready"], 5 * (l + 1))
                link(V_.tensor_tensor_scan(flat_(CB), RESET[:, 0:2 * S], flat_(SGW_), 0.0, ALU.mult, ALU.add))
                V_.tensor_tensor(flat_(PPV), flat_(CB), flat_(SGW_), ALU.subtract).then_inc(s["pexp_in"], 2)
                for i in R(2):
                    last = V_.tensor_scalar(KN[:, i, :], AV[:, i, :], 1.0, col(f"rk_k_a{l}", i), ALU.subtract, ALU.mult)
                link(last)
                link(V_.scalar_tensor_tensor(CM[:, 2:4, :], KN[:, :, :], 1.0, CM[:, 2:4, :], ALU.add, ALU.mult))
                for i in R(2):
                    last = V_.scalar_tensor_tensor(RB[:, i, :], CM[:, i, :], col(f"rk_r_k{l}", i), CM[:, 2 + i, :],
                                                   ALU.mult, ALU.mult)
                last.then_inc(s["bonus_in"], 1)
                dve.wait_ge(s["pexp_ready"], 3 * (l + 1))
                V_.scalar_tensor_tensor(flat_(AH), flat_(KK), -1.0, flat_(PPV), ALU.mult, ALU.mult)
                link(V_.tensor_tensor(flat_(BH), flat_(KK), flat_(AV), ALU.mult))
                V_.tensor_tensor(flat_(BH), flat_(BH), flat_(PIN), ALU.mult)
                V_.tensor_tensor(KH[:, :, :], CM[:, 2:4, :], PIN[:, :, :], ALU.mult)
                V_.tensor_tensor(RH[:, :, :], CM[:, 0:2, :], PP[:, :, :], ALU.mult)
                dve.wait_ge(s["bonus_mm"], l + 1)
                V_.tensor_tensor(KN[:, :, :], CM[:, 4:6, :], BANK[4][:, :].rearrange("p (a b) -> p a b", a=2),
                                 ALU.mult).then_inc(s["abkr_ready"], 1)
                dve.wait_ge(s["abkr_ready"], l + 1)
                for n in R(3):
                    for h in R(4):
                        V_.tensor_tensor(PPM[:, n, h, :], PP[:, h // 2, 64 * n + 63:64 * n + 64],
                                         BLOCK64[:, 64 * (h % 2):64 * (h % 2) + 1], ALU.mult)
                for t in R(TT):
                    last = V_.tensor_copy(XX[:, t, :].rearrange("p (h i) -> p h i", h=4), bcast(IDENT, 4))
                    last = V_.tensor_copy(XT[:, t, :].rearrange("p (h i) -> p h i", h=4), bcast(IDENT, 4))
                link(last)
                n = 0
                for dst, mask in ((LT, STRICT64), (PAIR[0], STRICT64), (PAIR[1], UPPER64), (PAIR[2], UPPER64)):
                    for par in R(2):
                        dve.wait_ge(s["pair_mm"], 8 * l + n + 1)
                        heads = dst.rearrange("p t (a b i) -> p (t a) b i", a=2, b=2)[:, :, par, :]
                        V_.tensor_tensor(heads, BANK[n % 2][:, :].rearrange("p (h i) -> p h i", h=4), bcast(mask, 4),
                                         ALU.mult).then_inc(s["pair_ready"], 1)
                        n += 1
                dve.wait_ge(s["pair_ready"], 8 * l + 8)
                for lv in R(7):
                    for t in R(TT):
                        if lv:
                            dve.wait_ge(s["xx_mm"], 12 * l + 2 * (lv - 1) + t + 1)
                            if lv < 6:
                                V_.tensor_tensor(XX[:, t, :], XX[:, t, :], BANK[3 + 3 * t][:, :], ALU.add)
                            V_.tensor_tensor(XT[:, t, :], XT[:, t, :], BANK[4 + 3 * t][:, :], ALU.add)\
                                .then_inc(s["xx_ready"], 1)
                        if lv < 6:
                            V_.tensor_tensor(LM[:, t, :].rearrange("p (h i) -> p h i", h=4),
                                             LT[:, t, :].rearrange("p (h i) -> p h i", h=4),
                                             LEVEL[:, lv:lv + 1, :].broadcast_to([P, 4, P]), ALU.mult)\
                                .then_inc(s["lvl_in"], 1)
                for n in R(3):
                    dve.wait_ge(s["sn_mm"], 3 * l + n + 1)
                    new, old = 4 * ((n + 1) % 2), 4 * (n % 2)
                    src = BANK[2][:, 0:256].rearrange("p (h i) -> p h i", h=4)
                    dst = ST2[:, new:new + 4, :]
                    if n:
                        link(V_.tensor_tensor(dst, ST2[:, old:old + 4, :], src, ALU.add))
                        src = dst
                    V_.tensor_tensor(dst, src, PPM[:, n, :, :].broadcast_to([P, 4, 64]), ALU.mult)\
                        .then_inc(s["sn_ready"], 1)
                    dve.wait_ge(s["sn_ready"], 3 * l + n + 1)
                dve.wait_ge(s["yc_mm"], 4 * (l + 1))
                V_.tensor_copy(flat_(AH), BANK[3][:, :]).then_inc(s["mean_in"], 1)
                dve.wait_ge(s["mean_mm"], l + 1)
                link(V_.scalar_tensor_tensor(flat_(AH), BANK[5][:, :], -1.0 / 64, flat_(AH), ALU.mult, ALU.add))
                V_.tensor_tensor(flat_(BH), flat_(AH), flat_(AH), ALU.mult).then_inc(s["var_in"], 1)
                dve.wait_ge(s["var_mm"], l + 1)
                link(V_.tensor_copy(flat_(KH), BANK[6][:, :]))
                rsqrt(flat_(RH), flat_(KH), flat_(BH), mul=1.0 / 64, eps=GN_EPS)
                link(V_.tensor_tensor(flat_(AH), flat_(AH), flat_(RH), ALU.mult))
                for i in R(2):
                    last = V_.tensor_scalar(AH[:, i, :], AH[:, i, :], col(f"rk_ln_w{l}", i), col(f"rk_ln_b{l}", i),
                                            ALU.mult, ALU.add)
                link(last)
                link(V_.tensor_tensor(flat_(AH), flat_(AH), flat_(KN), ALU.add))
                link(V_.tensor_tensor(flat_(AH), flat_(AH), flat_(GG), ALU.mult))
                split_x(AH[:, :, :], 4, 6, KT)
                dve.wait_ge(s["x_ready"], KT * (9 + 4 * l))
                mark("mixer_done")

            dve.wait_ge(s["x_loaded"], 16)
            norm()
            dve.wait_ge(s["loads_done"], 16 * N_LOADS)
            mark("rows_zero")
            dve.wait_ge(s["cols_tp"], 1)
            for t in range(3):
                last = V_.tensor_copy(COLS[:, t, :], BANK[t][:, 0:P])
            last.then_inc(s["cols_ready"], 1)
            dve.wait_ge(s["cols_ready"], 1)
            ahead(-1)
            gain("norm_mix0")
            project(EV_PROJ, ev_dest)
            even_mixer()
            output(EV_OUT)
            residual(EV_OUT)
            norm()
            gain("norm_ffn0")
            ffn(EV_FFN)
            residual(EV_FFN)
            norm()
            gain("norm_mix1")
            project(OD_PROJ, od_dest)
            odd_mixer()
            gain("head_norm")
            output(OD_OUT)
            residual(OD_OUT)
            norm()
            gain("norm_ffn1")
            router()
            dve.wait_ge(s["ssq_ready"], nxt("ssq_ready", TT))
            gi = gains_wait()
            rsqrt(STAT[:, 2:4], STAT[:, 0:2], STAT[:, 54:56])
            for t in range(TT):
                V_.scalar_tensor_tensor(H[:, t, :], H[:, t, :], STAT[:, 2 + t:3 + t], GBC[:, gi, :], ALU.mult,
                                        ALU.mult).then_inc(s["h_ready"], 1)
            mark("gbc_used")
            mark("mixer_done")
            for l in range(2):
                f1, pr, ou, f2 = HY[l]
                norm()
                gain(f"ffn1_pre{l}")
                ffn(f1)
                post(0.5)
                norm()
                gain(f"mix_pre{l}")
                project(pr, hy_dest)
                hybrid(l)
                output(ou)
                post(1.0)
                norm()
                gain(f"ffn2_pre{l}")
                ffn(f2)
                post(0.5)


_INS = ['x', 'norm_mix', 'norm_ffn', 'norm_final', 'ev_w_in', 'ev_conv_w', 'ev_conv_b', 'ev_ga_w', 'ev_ga_b',
        'ev_gx_w', 'ev_gx_b', 'ev_lambda', 'ev_f_b', 'ev_w_out', 'ev_ffn_w1', 'ev_ffn_w3', 'ev_ffn_w2', 'od_w_in',
        'od_gate_w2', 'od_gate_b', 'od_head_norm', 'od_w_out', 'od_router', 'od_exp_w1', 'od_exp_w3', 'od_exp_w2',
        'ffn1_pre_g_2', 'ffn1_w_gate_2', 'ffn1_w_up_2', 'ffn1_w_down_2', 'ffn1_post_g_2', 'mix_pre_g_2', 'w_in_2',
        'sc_conv_w_2', 'sg_ln_w_2', 'sg_ln_b_2', 'sg_w_2', 'sg_b_2', 'rk_mu_2', 'rk_w0_2', 'rk_w_up_2', 'rk_a0_2',
        'rk_a_up_2', 'rk_g_up_2', 'rk_k_k_2', 'rk_k_a_2', 'rk_r_k_2', 'rk_ln_w_2', 'rk_ln_b_2', 'cm_conv_w_2',
        'cm_conv_b_2', 'cm_ln_w_2', 'cm_ln_b_2', 'w_out_2', 'mix_post_g_2', 'ffn2_pre_g_2', 'ffn2_w_gate_2',
        'ffn2_w_up_2', 'ffn2_w_down_2', 'ffn2_post_g_2']
_OUTS = [((1, S, D), 'float32')]


def kernel(**inputs):
    import numpy as _np
    import concourse.bacc as _bacc
    from concourse import mybir as _mybir
    from concourse.bass_utils import run_bass_kernel_spmd as _run

    nc = _bacc.Bacc("TRN2", target_bir_lowering=False, num_devices=1)
    arrays, args = {}, {}
    for name in _INS:
        a = _np.ascontiguousarray(inputs[name])
        arrays[f"in_{name}_dram"] = a
        args[name] = nc.dram_tensor(f"in_{name}_dram", a.shape, _mybir.dt.from_np(a.dtype), kind="ExternalInput").ap()
    outs = []
    for i, (shape, dtype) in enumerate(_OUTS):
        dt = _mybir.dt.from_np(_np.dtype(dtype))
        outs.append(nc.dram_tensor(f"out_{i}_dram", shape, dt, kind="ExternalOutput").ap())
    build(nc, args, outs[0])
    r = _run(nc, [arrays], core_ids=[0])
    got = tuple(r.results[0][f"out_{i}_dram"] for i in range(len(_OUTS)))
    return got[0]
```
